# Optimizing a Trainium2 kernel written in Bass

```python
import math
import jax, jax.numpy as jnp
from jax import lax
import numpy as np
import jax
import jax.numpy as jnp

D_MODEL = 1024
BATCH = 1
SEQ = 512
DEPTH = 2

N_MIXERS = 2
N_A_LAYERS = (DEPTH + 1) // 2
N_B_LAYERS = DEPTH // 2

GDN_HEADS = 8
GDN_DK = 128
GDN_DV = 128
GDN_CONV = 4
GDN_CHUNK = 64
GDN_HK = GDN_HEADS * GDN_DK
GDN_HV = GDN_HEADS * GDN_DV
GDN_IN = 2 * GDN_HK + 2 * GDN_HV + 2 * GDN_HEADS
GDN_CONV_CH = 2 * GDN_HK + GDN_HV

DSW_GROUPS = ((128, 1), (512, 4), (2048, 16))
DSW_N_GROUPS = len(DSW_GROUPS)
DSW_HEADS = 8
DSW_DH = 64
DSW_HG = DSW_HEADS * DSW_DH
DSW_IN = 3 * DSW_N_GROUPS * DSW_HG

REL_BUCKETS = 32
REL_MAX_DIST = 2048
REL_HEADS = DSW_N_GROUPS * DSW_HEADS

FFN_HIDDEN = -(-8 * D_MODEL // (3 * 256)) * 256

RMS_EPS = 1e-6


def rms_norm(x, gain):
    xf = x.astype(jnp.float32)
    y = xf * lax.rsqrt(jnp.mean(xf * xf, axis=-1, keepdims=True) + RMS_EPS)
    return y * gain.astype(jnp.float32)

def l2_norm(x):
    xf = x.astype(jnp.float32)
    return xf * lax.rsqrt(jnp.sum(xf * xf, axis=-1, keepdims=True) + RMS_EPS)

def causal_depthwise_conv(x, w):
    K, C = w.shape
    return lax.conv_general_dilated(
        x, w[:, None, :].astype(x.dtype), window_strides=(1,),
        padding=((K - 1, 0),), dimension_numbers=("NWC", "WIO", "NWC"),
        feature_group_count=C)

def chunk_gated_delta_rule(q, k, v, g, beta):
    Bsz, S, H, dk = q.shape
    dv = v.shape[-1]
    C = GDN_CHUNK
    N = S // C
    to_chunks = lambda t: jnp.transpose(t.reshape(Bsz, N, C, H, t.shape[-1]), (0, 3, 1, 2, 4))
    q = to_chunks(q * (dk ** -0.5))
    k = to_chunks(k)
    v = to_chunks(v.astype(jnp.float32))
    beta = jnp.transpose(beta.reshape(Bsz, N, C, H), (0, 3, 1, 2))
    g = jnp.cumsum(jnp.transpose(g.reshape(Bsz, N, C, H), (0, 3, 1, 2)), axis=-1)

    causal = jnp.tril(jnp.ones((C, C), dtype=bool))
    strict = jnp.tril(jnp.ones((C, C), dtype=bool), -1)
    decay = jnp.exp(jnp.where(causal, g[..., :, None] - g[..., None, :], -jnp.inf))
    kb = k * beta[..., None]
    vb = v * beta[..., None]
    Lmat = jnp.where(strict, jnp.einsum('bhncd,bhnmd->bhncm', kb, k) * decay, 0.0)
    rhs = jnp.concatenate([vb, kb * jnp.exp(g)[..., None]], axis=-1)
    sol = lax.linalg.triangular_solve(Lmat, rhs, left_side=True, lower=True, unit_diagonal=True)
    u = sol[..., :dv]
    w = sol[..., dv:]
    qk = jnp.where(causal, jnp.einsum('bhncd,bhnmd->bhncm', q, k) * decay, 0.0)

    g_last = g[..., -1]
    q_dec = q * jnp.exp(g)[..., None]
    k_dec = k * jnp.exp(g_last[..., None] - g)[..., None]

    def step(state, inp):
        qd, a, uu, ww, kd, gl = inp
        v_new = uu - jnp.einsum('bhck,bhkv->bhcv', ww, state)
        o = jnp.einsum('bhck,bhkv->bhcv', qd, state) + jnp.einsum('bhcm,bhmv->bhcv', a, v_new)
        state = state * jnp.exp(gl)[..., None, None] + jnp.einsum('bhck,bhcv->bhkv', kd, v_new)
        return state, o

    xs = tuple(jnp.moveaxis(t, 2, 0) for t in (q_dec, qk, u, w, k_dec, g_last))
    state0 = jnp.zeros((Bsz, H, dk, dv), jnp.float32)
    _, o = lax.scan(step, state0, xs)
    return jnp.transpose(o, (1, 0, 3, 2, 4)).reshape(Bsz, S, H, dv)

def gated_deltanet_mixer(h, w_in, conv_w, a_log, dt_bias, out_gain, w_out):
    Bsz, S, _ = h.shape
    proj = h @ w_in
    qkv, z, a, b = jnp.split(proj, [GDN_CONV_CH, GDN_CONV_CH + GDN_HV,
                                    GDN_CONV_CH + GDN_HV + GDN_HEADS], axis=-1)
    qkv = jax.nn.silu(causal_depthwise_conv(qkv, conv_w))
    q, k, v = jnp.split(qkv, [GDN_HK, 2 * GDN_HK], axis=-1)
    q = l2_norm(q.reshape(Bsz, S, GDN_HEADS, GDN_DK))
    k = l2_norm(k.reshape(Bsz, S, GDN_HEADS, GDN_DK))
    v = v.reshape(Bsz, S, GDN_HEADS, GDN_DV)
    beta = jax.nn.sigmoid(b.astype(jnp.float32))
    g = -jnp.exp(a_log.astype(jnp.float32)) * jax.nn.softplus(a.astype(jnp.float32) + dt_bias.astype(jnp.float32))
    o = chunk_gated_delta_rule(q, k, v, g, beta)
    zf = z.reshape(Bsz, S, GDN_HEADS, GDN_DV).astype(jnp.float32)
    o = rms_norm(o, out_gain) * jax.nn.silu(zf)
    return o.reshape(Bsz, S, GDN_HV).astype(h.dtype) @ w_out

def t5_causal_bucket(dist):
    max_exact = REL_BUCKETS // 2
    scaled = jnp.log(jnp.maximum(dist, 1).astype(jnp.float32) / max_exact) / math.log(REL_MAX_DIST / max_exact)
    large = max_exact + (scaled * (REL_BUCKETS - max_exact)).astype(jnp.int32)
    large = jnp.minimum(large, REL_BUCKETS - 1)
    return jnp.where(dist < max_exact, dist, large)

def dilated_window_group(q, k, v, bias_table, window, dilation):
    Bsz, S, H, dh = q.shape
    span = window // dilation
    blk = span
    unit = dilation * blk
    S_pad = -(-S // unit) * unit
    nb = S_pad // unit

    def sub(t):
        t = jnp.pad(t, ((0, 0), (0, S_pad - S), (0, 0), (0, 0)))
        return jnp.transpose(t.reshape(Bsz, nb, blk, dilation, H, dh), (0, 3, 1, 2, 4, 5))

    qs, ks, vs = sub(q), sub(k), sub(v)
    shift = lambda t: jnp.concatenate([jnp.zeros_like(t[:, :, :1]), t[:, :, :-1]], axis=2)
    kb = jnp.concatenate([shift(ks), ks], axis=3)
    vb = jnp.concatenate([shift(vs), vs], axis=3)

    qi = jnp.arange(blk)[:, None] + blk
    ki = jnp.arange(2 * blk)[None, :]
    dist = qi - ki
    band = (dist >= 0) & (dist <= span)
    valid = band[None] & ((jnp.arange(nb) > 0)[:, None, None] | (ki >= blk)[None])
    bias = jnp.transpose(bias_table.astype(jnp.float32)[t5_causal_bucket(jnp.maximum(dist, 0) * dilation)], (2, 0, 1))

    logits = jnp.einsum('brnqhd,brnkhd->brnhqk', qs, kb) + bias[None, None, None]
    logits = jnp.where(valid[None, None, :, None], logits, -jnp.inf)
    m = jnp.max(logits, axis=-1, keepdims=True)
    p = jnp.exp(logits - m)
    l = jnp.sum(p, axis=-1, keepdims=True)
    o = jnp.einsum('brnhqk,brnkhd->brnqhd', p / l, vb)
    lse = (m + jnp.log(l))[..., 0]
    o = jnp.transpose(o, (0, 2, 3, 1, 4, 5)).reshape(Bsz, S_pad, H, dh)[:, :S]
    lse = jnp.transpose(lse, (0, 2, 4, 1, 3)).reshape(Bsz, S_pad, H)[:, :S]
    return o, lse

def dilated_attention_mixer(h, w_in, q_gain, k_gain, rel_bias, w_out):
    Bsz, S, _ = h.shape
    proj = (h @ w_in).reshape(Bsz, S, 3, DSW_N_GROUPS, DSW_HEADS, DSW_DH)
    q = rms_norm(proj[:, :, 0], q_gain) * (DSW_DH ** -0.5)
    k = rms_norm(proj[:, :, 1], k_gain)
    v = proj[:, :, 2].astype(jnp.float32)
    outs, lses = [], []
    for gi, (window, dilation) in enumerate(DSW_GROUPS):
        o, lse = dilated_window_group(q[:, :, gi], k[:, :, gi], v[:, :, gi],
                                      rel_bias[:, gi * DSW_HEADS:(gi + 1) * DSW_HEADS], window, dilation)
        outs.append(o)
        lses.append(lse)
    wts = jax.nn.softmax(jnp.stack(lses), axis=0)
    o = jnp.sum(wts[..., None] * jnp.stack(outs), axis=0)
    return o.reshape(Bsz, S, DSW_HG).astype(h.dtype) @ w_out

def swiglu(h, w_in, w_out):
    gate, up = jnp.split(h @ w_in, 2, axis=-1)
    return (jax.nn.silu(gate) * up) @ w_out

def first_inputs(seed: int = 0) -> dict:
    key = jax.random.key(seed)
    ks = jax.random.split(key, 20)
    nrm = lambda k, shape, s: jax.random.normal(k, shape, jnp.float32) * s
    D = D_MODEL
    a_init = jax.random.uniform(ks[10], (N_A_LAYERS, GDN_HEADS), jnp.float32, 1.0, 16.0)
    dt = jnp.exp(jax.random.uniform(ks[11], (N_A_LAYERS, GDN_HEADS), jnp.float32,
                                    math.log(1e-3), math.log(1e-1)))
    return {
        "x": nrm(ks[0], (BATCH, SEQ, D), 1.0),
        "c": nrm(ks[1], (BATCH, D), 1.0),
        "w_ada": nrm(ks[2], (DEPTH, D, 6 * D), D ** -0.5),
        "b_ada": nrm(ks[3], (DEPTH, 6 * D), 0.02),
        "norm_mix": 1.0 + nrm(ks[4], (DEPTH, D), 0.02),
        "norm_ffn": 1.0 + nrm(ks[5], (DEPTH, D), 0.02),
        "w_ffn_in": nrm(ks[6], (DEPTH, D, 2 * FFN_HIDDEN), D ** -0.5),
        "w_ffn_out": nrm(ks[7], (DEPTH, FFN_HIDDEN, D), FFN_HIDDEN ** -0.5),
        "gdn_w_in": nrm(ks[8], (N_A_LAYERS, D, GDN_IN), D ** -0.5),
        "gdn_conv": nrm(ks[9], (N_A_LAYERS, GDN_CONV, GDN_CONV_CH), GDN_CONV ** -0.5),
        "gdn_a_log": jnp.log(a_init),
        "gdn_dt_bias": dt + jnp.log(-jnp.expm1(-dt)),
        "gdn_out_norm": 1.0 + nrm(ks[12], (N_A_LAYERS, GDN_DV), 0.02),
        "gdn_w_out": nrm(ks[13], (N_A_LAYERS, GDN_HV, D), GDN_HV ** -0.5),
        "dsw_w_in": nrm(ks[14], (N_B_LAYERS, D, DSW_IN), D ** -0.5),
        "dsw_q_norm": 1.0 + nrm(ks[15], (N_B_LAYERS, DSW_DH), 0.02),
        "dsw_k_norm": 1.0 + nrm(ks[16], (N_B_LAYERS, DSW_DH), 0.02),
        "dsw_w_out": nrm(ks[17], (N_B_LAYERS, DSW_HG, D), DSW_HG ** -0.5),
        "rel_bias": nrm(ks[18], (REL_BUCKETS, REL_HEADS), 0.5),
    }

def first_block(x, c, w_ada, b_ada, norm_mix, norm_ffn, w_ffn_in, w_ffn_out,
              gdn_w_in, gdn_conv, gdn_a_log, gdn_dt_bias, gdn_out_norm, gdn_w_out,
              dsw_w_in, dsw_q_norm, dsw_k_norm, dsw_w_out, rel_bias):
    cond = jax.nn.silu(c.astype(jnp.float32))
    for layer in range(DEPTH):
        mod = (cond @ w_ada[layer].astype(jnp.float32) + b_ada[layer].astype(jnp.float32)).astype(x.dtype)
        sh1, sc1, g1, sh2, sc2, g2 = jnp.split(mod[:, None, :], 6, axis=-1)

        h = (rms_norm(x, norm_mix[layer]) * (1.0 + sc1) + sh1).astype(x.dtype)
        j = layer // N_MIXERS
        if layer % N_MIXERS == 0:
            y = gated_deltanet_mixer(h, gdn_w_in[j], gdn_conv[j], gdn_a_log[j], gdn_dt_bias[j],
                                     gdn_out_norm[j], gdn_w_out[j])
        else:
            y = dilated_attention_mixer(h, dsw_w_in[j], dsw_q_norm[j], dsw_k_norm[j],
                                        rel_bias, dsw_w_out[j])
        x = x + g1 * y

        h = (rms_norm(x, norm_ffn[layer]) * (1.0 + sc2) + sh2).astype(x.dtype)
        x = x + g2 * swiglu(h, w_ffn_in[layer], w_ffn_out[layer])
    return x


HEAD_DIM = 64
ROPE_THETA = 10000.0
NORM_EPS = 1e-6
NEG = -1e30
BRANCH_W = D_MODEL // 2
N_BRANCH = 4
NSA_HEADS = BRANCH_W // HEAD_DIM
NSA_KV = 2
NSA_R = NSA_HEADS // NSA_KV
CMP_LEN = 32
CMP_STRIDE = 16
CMP_HIDDEN = 256
SEL_LEN = 64
SEL_TOPK = 16
NSA_WINDOW = 512
SEL_Q_CHUNK = 32
FORCE_BONUS = 1e3
SWA_HEADS = BRANCH_W // HEAD_DIM
SWA_KV = 2
SWA_R = SWA_HEADS // SWA_KV
SWA_WINDOW = 128
Q_BLOCK = 128
CONV_CH = BRANCH_W
CONV_WIDTH = 31
POOL_CH = BRANCH_W
POOL_WINDOWS = (2, 4, 8, 16)
POOL_GROUPS = 4
POOL_GROUP_CH = POOL_CH // POOL_GROUPS
D_FF = ((8 * D_MODEL // 3) + 127) // 128 * 128
FFN_CONV_WIDTH = 3
IN_SIZES = (
    NSA_HEADS * HEAD_DIM,
    3 * 2 * NSA_KV * HEAD_DIM,
    3 * NSA_HEADS,
    SWA_HEADS * HEAD_DIM,
    2 * SWA_KV * HEAD_DIM,
    2 * CONV_CH,
    POOL_CH,
)
IN_COLS = sum(IN_SIZES)


def rms_norm_2(x, g):
    xf = x.astype(jnp.float32)
    y = xf * lax.rsqrt(jnp.mean(xf * xf, axis=-1, keepdims=True) + NORM_EPS)
    return (y * g.astype(jnp.float32)).astype(x.dtype)

def layer_norm(x, g, b):
    xf = x.astype(jnp.float32)
    mu = jnp.mean(xf, axis=-1, keepdims=True)
    var = jnp.mean(jnp.square(xf - mu), axis=-1, keepdims=True)
    y = (xf - mu) * lax.rsqrt(var + NORM_EPS)
    return (y * g.astype(jnp.float32) + b.astype(jnp.float32)).astype(x.dtype)

def rope_tables(seq):
    inv = 1.0 / (ROPE_THETA ** (jnp.arange(0, HEAD_DIM, 2, dtype=jnp.float32) / HEAD_DIM))
    ang = jnp.arange(seq, dtype=jnp.float32)[:, None] * inv[None, :]
    return jnp.cos(ang), jnp.sin(ang)

def apply_rope(x, cos, sin):
    shp = (1, x.shape[1]) + (1,) * (x.ndim - 3) + (HEAD_DIM // 2,)
    c, s = cos.reshape(shp), sin.reshape(shp)
    xf = x.astype(jnp.float32)
    x1, x2 = xf[..., : HEAD_DIM // 2], xf[..., HEAD_DIM // 2:]
    return jnp.concatenate([x1 * c - x2 * s, x2 * c + x1 * s], axis=-1).astype(x.dtype)

def causal_depthwise_conv_2(x, w, b):
    k, c = w.shape
    y = lax.conv_general_dilated(
        x, w[:, None, :].astype(x.dtype), window_strides=(1,), padding=[(k - 1, 0)],
        dimension_numbers=("NWC", "WIO", "NWC"), feature_group_count=c)
    return y + b.astype(x.dtype)

def masked_softmax(s, mask):
    p = jax.nn.softmax(jnp.where(mask, s, NEG), axis=-1)
    return jnp.where(mask, p, 0.0)

def banded_attention(q, k, v, window, sinks):
    bsz, seq, g, r, dk = q.shape
    span = window + Q_BLOCK
    k_pad = jnp.pad(k, ((0, 0), (window, 0), (0, 0), (0, 0)))
    v_pad = jnp.pad(v, ((0, 0), (window, 0), (0, 0), (0, 0)))
    scale = dk ** -0.5

    def block(i):
        start = i * Q_BLOCK
        qb = lax.dynamic_slice_in_dim(q, start, Q_BLOCK, axis=1)
        kb = lax.dynamic_slice_in_dim(k_pad, start, span, axis=1)
        vb = lax.dynamic_slice_in_dim(v_pad, start, span, axis=1)
        t = start + jnp.arange(Q_BLOCK)
        j = start - window + jnp.arange(span)
        mask = (j[None, :] <= t[:, None]) & (j[None, :] > t[:, None] - window) & (j[None, :] >= 0)
        mask = mask[None, None, None]
        s = jnp.einsum("bqgrd,bkgd->bgrqk", qb, kb, preferred_element_type=jnp.float32) * scale
        if sinks is None:
            p = masked_softmax(s, mask)
        else:
            sink = sinks.astype(jnp.float32).reshape(g, r)[None, :, :, None, None]
            s = jnp.where(mask, s, NEG)
            m = jnp.maximum(jnp.max(s, axis=-1, keepdims=True), sink)
            e = jnp.exp(s - m)
            p = e / (jnp.sum(e, axis=-1, keepdims=True) + jnp.exp(sink - m))
        return jnp.einsum("bgrqk,bkgd->bqgrd", p.astype(v.dtype), vb)

    out = lax.map(block, jnp.arange(seq // Q_BLOCK))
    return jnp.moveaxis(out, 0, 1).reshape(bsz, seq, g, r, dk)

def nsa_compress(k, pos, w1, w2):
    bsz, seq, g, dk = k.shape
    n_cmp = (seq - CMP_LEN) // CMP_STRIDE + 1
    idx = np.arange(n_cmp)[:, None] * CMP_STRIDE + np.arange(CMP_LEN)[None, :]
    blk = jnp.swapaxes(k[:, idx], 2, 3) + pos.astype(k.dtype)
    flat = blk.reshape(bsz, n_cmp, g, CMP_LEN * dk)
    return jax.nn.gelu(flat @ w1, approximate=True) @ w2

def nsa_compressed_attention(q, kc, vc):
    seq, n_cmp = q.shape[1], kc.shape[1]
    t = jnp.arange(seq)
    blk_end = jnp.arange(n_cmp) * CMP_STRIDE + CMP_LEN - 1
    mask = (blk_end[None, :] <= t[:, None])[None, :, None, None, :]
    s = jnp.einsum("bsgrd,bngd->bsgrn", q, kc, preferred_element_type=jnp.float32) * HEAD_DIM ** -0.5
    p = masked_softmax(s, mask)
    o = jnp.einsum("bsgrn,bngd->bsgrd", p.astype(vc.dtype), vc)
    return o, p

def nsa_select_blocks(p_cmp, seq):
    n_cmp = p_cmp.shape[-1]
    n_slc = seq // SEL_LEN
    i = jnp.arange(n_cmp)
    j = jnp.arange(n_slc)
    overlap = ((i[:, None] * CMP_STRIDE < (j[None, :] + 1) * SEL_LEN)
               & (i[:, None] * CMP_STRIDE + CMP_LEN > j[None, :] * SEL_LEN)).astype(jnp.float32)
    imp = jnp.einsum("bsgrn,nj->bsgj", p_cmp, overlap)
    cur = jnp.arange(seq) // SEL_LEN
    valid = (j[None, :] <= cur[:, None])[None, :, None, :]
    forced = ((j[None, :] == 0) | (j[None, :] == cur[:, None]) | (j[None, :] == cur[:, None] - 1))[None, :, None, :]
    score = jnp.where(valid, imp + jnp.where(forced, FORCE_BONUS, 0.0), -1.0)
    _, sel = lax.top_k(score, min(SEL_TOPK, n_slc))
    return sel

def nsa_selected_attention(q, k, v, sel):
    bsz, seq, g, r, dk = q.shape
    n_slc = seq // SEL_LEN
    n_top = sel.shape[-1]
    kb = k.reshape(bsz, n_slc, SEL_LEN, g, dk).transpose(0, 3, 1, 2, 4)
    vb = v.reshape(bsz, n_slc, SEL_LEN, g, dk).transpose(0, 3, 1, 2, 4)
    nc = seq // SEL_Q_CHUNK
    qc = jnp.moveaxis(q.reshape(bsz, nc, SEL_Q_CHUNK, g, r, dk), 1, 0)
    sc = jnp.moveaxis(sel.reshape(bsz, nc, SEL_Q_CHUNK, g, n_top), 1, 0)
    b_idx = jnp.arange(bsz)[:, None, None, None]
    g_idx = jnp.arange(g)[None, None, :, None]
    scale = dk ** -0.5

    def chunk(args):
        q_c, sel_c, c = args
        t = c * SEL_Q_CHUNK + jnp.arange(SEL_Q_CHUNK)
        kg = kb[b_idx, g_idx, sel_c]
        vg = vb[b_idx, g_idx, sel_c]
        s = jnp.einsum("bcgrd,bcgkld->bcgrkl", q_c, kg, preferred_element_type=jnp.float32) * scale
        kpos = sel_c[..., None] * SEL_LEN + jnp.arange(SEL_LEN)
        mask = (kpos <= t[None, :, None, None, None])[:, :, :, None]
        flat = (bsz, SEL_Q_CHUNK, g, r, n_top * SEL_LEN)
        p = masked_softmax(s.reshape(flat), mask.reshape(bsz, SEL_Q_CHUNK, g, 1, n_top * SEL_LEN)).reshape(s.shape)
        return jnp.einsum("bcgrkl,bcgkld->bcgrd", p.astype(vg.dtype), vg)

    out = lax.map(chunk, (qc, sc, jnp.arange(nc)))
    return jnp.moveaxis(out, 0, 1).reshape(bsz, seq, g, r, dk)

def conformer_conv(u, conv_w, conv_b, ln_g, ln_b):
    a, gte = jnp.split(u, 2, axis=-1)
    c = a * jax.nn.sigmoid(gte)
    c = causal_depthwise_conv_2(c, conv_w, conv_b)
    return jax.nn.silu(layer_norm(c, ln_g, ln_b))

def pool_mixer(u, w, scale):
    bsz, seq, _ = u.shape
    uf = u.reshape(bsz, seq, POOL_GROUPS, POOL_GROUP_CH).astype(jnp.float32)
    cs = jnp.pad(jnp.cumsum(uf, axis=1), ((0, 0), (1, 0), (0, 0), (0, 0)))
    t = jnp.arange(seq)[:, None]
    win = jnp.array(POOL_WINDOWS, dtype=jnp.int32)[None, :]
    lo = jnp.maximum(t + 1 - win, 0)
    g_idx = jnp.arange(POOL_GROUPS)[None, :]
    mean = (cs[:, 1:] - cs[:, lo, g_idx]) / (t + 1 - lo).astype(jnp.float32)[None, :, :, None]
    pooled = (mean - uf).astype(u.dtype)
    mixed = jnp.einsum("bsgc,gcd->bsgd", pooled, w)
    return mixed.reshape(bsz, seq, POOL_CH) * scale

def second_inputs(seed: int = 0) -> dict:
    key = jax.random.key(seed)
    ks = jax.random.split(key, 24)
    f32 = jnp.float32
    L = DEPTH

    def nrm(k, shape, scale):
        return jax.random.normal(k, shape, f32) * scale

    return {
        "x": nrm(ks[0], (BATCH, SEQ, D_MODEL), 1.0),
        "norm_mix_pre": 1.0 + nrm(ks[1], (L, D_MODEL), 0.05),
        "norm_mix_post": 1.0 + nrm(ks[2], (L, D_MODEL), 0.05),
        "norm_ffn_pre": 1.0 + nrm(ks[3], (L, D_MODEL), 0.05),
        "norm_ffn_post": 1.0 + nrm(ks[4], (L, D_MODEL), 0.05),
        "w_in": nrm(ks[5], (L, D_MODEL, IN_COLS), D_MODEL ** -0.5),
        "nsa_cmp_pos": nrm(ks[6], (L, 2, CMP_LEN, HEAD_DIM), 0.1),
        "nsa_cmp_w1": nrm(ks[7], (L, 2, CMP_LEN * HEAD_DIM, CMP_HIDDEN), (CMP_LEN * HEAD_DIM) ** -0.5),
        "nsa_cmp_w2": nrm(ks[8], (L, 2, CMP_HIDDEN, HEAD_DIM), CMP_HIDDEN ** -0.5),
        "swa_sinks": nrm(ks[9], (L, SWA_HEADS), 0.5),
        "conv_w": nrm(ks[10], (L, CONV_WIDTH, CONV_CH), CONV_WIDTH ** -0.5),
        "conv_b": nrm(ks[11], (L, CONV_CH), 0.01),
        "conv_ln_g": 1.0 + nrm(ks[12], (L, CONV_CH), 0.05),
        "conv_ln_b": nrm(ks[13], (L, CONV_CH), 0.01),
        "pool_w": nrm(ks[14], (L, POOL_GROUPS, POOL_GROUP_CH, POOL_GROUP_CH), POOL_GROUP_CH ** -0.5),
        "pool_scale": 1.0 + nrm(ks[15], (L, POOL_CH), 0.1),
        "w_branch": nrm(ks[16], (L, N_BRANCH, BRANCH_W, D_MODEL), BRANCH_W ** -0.5),
        "w_gate": nrm(ks[17], (L, D_MODEL, N_BRANCH * D_MODEL), D_MODEL ** -0.5),
        "w_o": nrm(ks[18], (L, D_MODEL, D_MODEL), D_MODEL ** -0.5),
        "ffn_w_up": nrm(ks[19], (L, D_MODEL, 2 * D_FF), D_MODEL ** -0.5),
        "ffn_conv_w": nrm(ks[20], (L, FFN_CONV_WIDTH, 2 * D_FF), FFN_CONV_WIDTH ** -0.5),
        "ffn_conv_b": nrm(ks[21], (L, 2 * D_FF), 0.01),
        "ffn_w_down": nrm(ks[22], (L, D_FF, D_MODEL), D_FF ** -0.5),
    }

def second_block(x, norm_mix_pre, norm_mix_post, norm_ffn_pre, norm_ffn_post, w_in,
              nsa_cmp_pos, nsa_cmp_w1, nsa_cmp_w2, swa_sinks, conv_w, conv_b, conv_ln_g,
              conv_ln_b, pool_w, pool_scale, w_branch, w_gate, w_o, ffn_w_up, ffn_conv_w,
              ffn_conv_b, ffn_w_down):
    bsz, seq, _ = x.shape
    cos, sin = rope_tables(seq)
    splits = np.cumsum(IN_SIZES)[:-1].tolist()
    for l in range(DEPTH):
        h = rms_norm_2(x, norm_mix_pre[l])
        proj = h @ w_in[l]
        a_q, a_kv, a_gate, d_q, d_kv, b_in, c_in = jnp.split(proj, splits, axis=-1)

        qa = a_q.reshape(bsz, seq, NSA_KV, NSA_R, HEAD_DIM)
        kv = a_kv.reshape(bsz, seq, 3, 2, NSA_KV, HEAD_DIM)
        k_cmp = nsa_compress(kv[:, :, 0, 0], nsa_cmp_pos[l, 0], nsa_cmp_w1[l, 0], nsa_cmp_w2[l, 0])
        v_cmp = nsa_compress(kv[:, :, 0, 1], nsa_cmp_pos[l, 1], nsa_cmp_w1[l, 1], nsa_cmp_w2[l, 1])
        o_cmp, p_cmp = nsa_compressed_attention(qa, k_cmp, v_cmp)
        sel = nsa_select_blocks(p_cmp, seq)
        qa_rot = apply_rope(qa, cos, sin)
        o_slc = nsa_selected_attention(qa_rot, apply_rope(kv[:, :, 1, 0], cos, sin), kv[:, :, 1, 1], sel)
        o_win = banded_attention(qa_rot, apply_rope(kv[:, :, 2, 0], cos, sin), kv[:, :, 2, 1], NSA_WINDOW, None)
        ga = jax.nn.sigmoid(a_gate).reshape(bsz, seq, 3, NSA_KV, NSA_R, 1)
        o_a = (ga[:, :, 0] * o_cmp + ga[:, :, 1] * o_slc + ga[:, :, 2] * o_win).reshape(bsz, seq, BRANCH_W)

        o_b = conformer_conv(b_in, conv_w[l], conv_b[l], conv_ln_g[l], conv_ln_b[l])

        o_c = pool_mixer(c_in, pool_w[l], pool_scale[l])

        qd = apply_rope(d_q.reshape(bsz, seq, SWA_KV, SWA_R, HEAD_DIM), cos, sin)
        kvd = d_kv.reshape(bsz, seq, 2, SWA_KV, HEAD_DIM)
        o_d = banded_attention(qd, apply_rope(kvd[:, :, 0], cos, sin), kvd[:, :, 1], SWA_WINDOW,
                               swa_sinks[l]).reshape(bsz, seq, BRANCH_W)

        branches = jnp.stack([o_a, o_b, o_c, o_d], axis=2)
        up = jnp.einsum("bsnc,ncd->bsnd", branches, w_branch[l])
        gates = jax.nn.sigmoid((h @ w_gate[l]).reshape(bsz, seq, N_BRANCH, D_MODEL))
        mix = jnp.einsum("bsnd,bsnd->bsd", gates, up) @ w_o[l]
        x = x + rms_norm_2(mix, norm_mix_post[l])

        hf = rms_norm_2(x, norm_ffn_pre[l])
        u = causal_depthwise_conv_2(hf @ ffn_w_up[l], ffn_conv_w[l], ffn_conv_b[l])
        gate, val = jnp.split(u, 2, axis=-1)
        f = (jax.nn.gelu(gate, approximate=True) * val) @ ffn_w_down[l]
        x = x + rms_norm_2(f, norm_ffn_post[l])
    return x


def setup_inputs(seed=0):
    out = dict(first_inputs(seed))
    for name, value in second_inputs(seed + 1).items():
        if name != "x":
            out[name + "_2"] = value
    return out


def reference(
    x, c, w_ada, b_ada, norm_mix, norm_ffn, w_ffn_in, w_ffn_out, gdn_w_in, gdn_conv, gdn_a_log,
    gdn_dt_bias, gdn_out_norm, gdn_w_out, dsw_w_in, dsw_q_norm, dsw_k_norm, dsw_w_out, rel_bias,
    norm_mix_pre_2, norm_mix_post_2, norm_ffn_pre_2, norm_ffn_post_2, w_in_2, nsa_cmp_pos_2,
    nsa_cmp_w1_2, nsa_cmp_w2_2, swa_sinks_2, conv_w_2, conv_b_2, conv_ln_g_2, conv_ln_b_2,
    pool_w_2, pool_scale_2, w_branch_2, w_gate_2, w_o_2, ffn_w_up_2, ffn_conv_w_2, ffn_conv_b_2,
    ffn_w_down_2,
):
    x = first_block(
        x, c, w_ada, b_ada, norm_mix, norm_ffn, w_ffn_in, w_ffn_out, gdn_w_in, gdn_conv,
        gdn_a_log, gdn_dt_bias, gdn_out_norm, gdn_w_out, dsw_w_in, dsw_q_norm, dsw_k_norm,
        dsw_w_out, rel_bias,
    )
    return second_block(
        x, norm_mix_pre_2, norm_mix_post_2, norm_ffn_pre_2, norm_ffn_post_2, w_in_2,
        nsa_cmp_pos_2, nsa_cmp_w1_2, nsa_cmp_w2_2, swa_sinks_2, conv_w_2, conv_b_2, conv_ln_g_2,
        conv_ln_b_2, pool_w_2, pool_scale_2, w_branch_2, w_gate_2, w_o_2, ffn_w_up_2,
        ffn_conv_w_2, ffn_conv_b_2, ffn_w_down_2,
    )


_drawn_inputs = setup_inputs


def setup_inputs(seed=0):
    import zlib

    import numpy as np

    out = dict(_drawn_inputs(seed))
    spreads = {}
    factors = {'norm_mix': 2.973,
     'gdn_out_norm': 4.472,
     'dsw_q_norm': 27.738,
     'dsw_k_norm': 21.986,
     'swa_sinks_2': 200.0,
     'conv_b_2': 200.0,
     'conv_ln_b_2': 200.0,
     'ffn_conv_b_2': 69.671,
     'norm_ffn': 6.61,
     'rel_bias': 3.225,
     'norm_mix_pre_2': 4.893,
     'norm_mix_post_2': 28.946,
     'norm_ffn_pre_2': 13.969,
     'norm_ffn_post_2': 28.574,
     'nsa_cmp_pos_2': 60.165,
     'conv_ln_g_2': 64.0,
     'pool_scale_2': 11.294,
     'nsa_cmp_w1_2': 2.726}
    for name, (base, spread) in spreads.items():
        noise = np.random.default_rng([zlib.crc32(name.encode()), seed]).standard_normal(out[name].shape)
        drawn = base * np.exp(spread * noise) if base else spread * noise
        out[name] = jnp.asarray(drawn.astype(out[name].dtype))
    for name, factor in factors.items():
        out[name] = (out[name] * factor).astype(out[name].dtype)
    return out
```

```python
import math
from contextlib import ExitStack, contextmanager

import numpy as np
import concourse.bass as bass
from concourse import mybir
from concourse.alu_op_type import AluOpType as ALU

F32 = mybir.dt.float32
ACT = mybir.ActivationFunctionType
AX = mybir.AxisListType
ds = bass.ds

P = 128
S = 512
D = 1024
KT = D // P
TT = S // P
EPS = 1e-6
NEG = -1e30
DEPTH = 2

GH, GDK, GCONV, GC = 8, 128, 4, 64
GHK = GH * GDK
GCH = 3 * GHK
NCH = S // GC
LEVELS = 6
WG, WH, WD = 3, 8, 64
WHG = WH * WD
DILATIONS = (1, 4, 16)
BUCKETS = 32
F1 = 2816
F2 = 2816
FT = F1 // P
BW = 512
IN2 = 3608
CMP_LEN, CMP_STRIDE, CMP_HID = 32, 16, 256
NCMP = (S - CMP_LEN) // CMP_STRIDE + 1
CONVW = 31
POOLW = (2, 4, 8, 16)

SLOT = 4096
BANK = 40


def bucket_of(dist):
    exact = BUCKETS // 2
    d = np.maximum(dist, 1).astype(np.float32)
    scaled = np.log(d / np.float32(exact)) / np.float32(math.log(2048 / exact))
    large = exact + (scaled * np.float32(BUCKETS - exact)).astype(np.int32)
    return np.where(dist < exact, dist, np.minimum(large, BUCKETS - 1))


def constant_tables():
    p = np.arange(P)
    row, col = p[:, None], p[None, :]
    t = {}
    t["ident"] = np.eye(P)
    t["ones"] = np.ones((P, P))
    t["halves"] = (row // 64 == col // 64) * 1.0
    levels = []
    for lv in range(LEVELS):
        same = (row >> (lv + 1)) == (col >> (lv + 1))
        levels.append(same & ((col >> lv) & 1 == 1) & ((row >> lv) & 1 == 0))
    t["levels"] = np.concatenate(levels, 1) * 1.0
    t["chunkmask"] = ((row // GC == col // GC) & (row <= col)) * 1.0
    t["resets"] = np.broadcast_to((np.arange(S) % GC != 0) * 1.0, (GH, S))
    t["hot8"] = np.eye(GH)
    hot = []
    for dil, off in ((1, 0), (4, 0), (16, 0), (1, P)):
        limit = 31 if dil == 16 else P
        dist = 127 - np.arange(256) + off
        valid = (dist >= 0) & (dist <= limit) & (np.arange(256) < 255)
        b = np.where(valid, bucket_of(np.maximum(dist, 0) * dil), BUCKETS)
        hot.append((np.arange(BUCKETS + 1)[:, None] == b[None, :]) * 1.0)
    t["buckets"] = np.concatenate(hot, 1)
    t["classmask"] = np.where(row // 32 == col // 32, 0.0, NEG)
    t["flip"] = np.eye(P)[::-1]
    pairs = [(np.arange(WH)[:, None] == 2 * j + col // 64) * 1.0 for j in range(4)]
    t["pairsel"] = np.concatenate(pairs, 1)
    inv = (1.0 / (np.float32(10000.0) ** (np.arange(0, 64, 2, dtype=np.float32) / np.float32(64)))).astype(np.float32)
    ang = np.arange(S, dtype=np.float32)[None, :] * inv[p % 32][:, None]
    t["cos"] = np.cos(ang)
    t["sin"] = np.sin(ang) * np.where(p % 64 < 32, -1.0, 1.0)[:, None]
    t["swap"] = ((row // 64 == col // 64) & ((row - col) % 64 == 32)) * 1.0
    t["band"] = np.concatenate([np.where(col > row, 0.0, NEG), np.where(col <= row, 0.0, NEG)], 1)
    end = np.arange(NCMP) * CMP_STRIDE + CMP_LEN - 1
    seen = [end[None, :] <= (i * P + row) for i in range(TT)]
    t["cmpadd"] = np.concatenate([np.where(m, 0.0, NEG) for m in seen], 1)
    t["cmpmul"] = np.concatenate(seen, 1) * 1.0
    t["poolinv"] = np.broadcast_to(
        np.concatenate([1.0 / np.minimum(np.arange(16) + 1, w) for w in POOLW]), (P, 64))
    return {k: np.ascontiguousarray(v, dtype=np.float32) for k, v in t.items()}


TABLES = constant_tables()
PLACES, CW = {}, 0
for _name, _t in TABLES.items():
    PLACES[_name] = CW
    CW += _t.shape[1]


def packed_constants():
    out = np.zeros((P, CW), np.float32)
    for name, t in TABLES.items():
        out[:t.shape[0], PLACES[name]:PLACES[name] + t.shape[1]] = t
    return out


class Links:

    def __init__(self, engine, sem, base=0):
        self.engine, self.sem, self.base, self.n = engine, sem, base, 0

    def do(self, instruction):
        self.n += 1
        instruction.then_inc(self.sem, 1)
        self.engine.wait_ge(self.sem, self.base + self.n)


class Core:

    def __init__(self, nc, ctx, ins, out):
        self.nc, self.ins, self.out = nc, ins, out
        self.turn = 0
        sb = lambda name, shape: ctx.enter_context(nc.sbuf_tensor(name, shape, F32))
        self.banks = [[ctx.enter_context(nc.semaphore(f"bank{b}_{i}")) for i in range(BANK)] for b in range(2)]
        self.x = sb("x_residual", [P, KT, S])
        self.h = sb("h_normed", [P, KT, S])
        self.slots = [sb(f"weight_slot{i}", [P, SLOT]) for i in range(2)]
        self.vec = sb("vectors", [P, 8 * P])
        self.mod = sb("modulation", [P, DEPTH * 48])
        self.gains = sb("modulated_gains", [P, DEPTH * 2 * KT])
        self.ident = sb("ident", [P, P])
        self.ones = sb("ones", [P, P])
        self.halves = sb("halves", [P, P])
        self.eps = sb("eps", [P, 1])
        self.ps = ctx.enter_context(nc.psum_tensor("psum", [P, 8, 512], F32))
        self.places = {}

    def const(self, name, rows=P):
        w = TABLES[name].shape[1]
        return self.ins["constants"][0:rows, PLACES[name]:PLACES[name] + w]

    def column(self, name, n=0):
        return self.places[name] + n

    @contextmanager
    def stage(self, **buffers):
        self.turn ^= 1
        bank, used = self.banks[self.turn], self.banks[1 - self.turn]
        numbers = [s.num for s in used]
        assert numbers == list(range(numbers[0], numbers[0] + BANK))
        with ExitStack() as ctx:
            made = [ctx.enter_context(self.nc.sbuf_tensor(f"{k}_{self.nc.next_id()}", list(v), F32))
                    for k, v in buffers.items()]
            block = ctx.enter_context(self.nc.Block(no_gpsimd_drain=True))

            @block.gpsimd
            def _(pool):
                pool.sem_clear(range(numbers[0], numbers[-1] + 1))

            yield (block, list(bank), *made)


def stream_weights(sp, c, steps, loads, loaded, done):
    with sp.Fori(0, steps // 2) as i:
        for s in range(2):
            sp.wait_ge(done, i * 2 + s + 1)
            for dst, src in loads(i * 2 + s, c.slots[s]):
                sp.dma_start(dst, src).then_inc(loaded[s], 16)


def multiply_steps(pe, c, steps, dmas, loaded, done, freed, tiles, kt, weights, moving):
    pe.sem_inc(done, 2)
    with pe.Fori(0, steps // 2) as i:
        for s in range(2):
            pe.wait_ge(loaded[s], i * (16 * dmas) + 16 * dmas)
            pe.wait_ge(freed, i * 2 + s + 1)
            for t in range(tiles):
                for k in range(kt):
                    last = c.nc.tensor.matmul(c.ps[:, 4 * s + t, :], weights(c.slots[s], t, k),
                                              moving(k), start=(k == 0), stop=(k == kt - 1))
            last.then_inc(done, 1)


def columns(w, n0, n):
    return w.rearrange("(k p) n -> p k n", p=P)[:, :, ds(n0, n)]


def set_up(c):
    nc, ins = c.nc, c.ins
    rows = []

    def vectors(name, ap, half=None):
        rows.append((name, ap, half))

    def flat(name):
        a = ins[name]
        letters = " ".join("abcdef"[:len(a.shape)])
        f = a if len(a.shape) == 1 else a.rearrange(f"{letters} -> ({letters})")
        return f.rearrange("(n p) -> n p", p=P)

    for name in ("c", "b_ada", "norm_mix", "norm_ffn", "gdn_conv", "gdn_out_norm", "norm_mix_pre_2",
                 "norm_mix_post_2", "norm_ffn_pre_2", "norm_ffn_post_2", "conv_w_2", "conv_b_2",
                 "conv_ln_g_2", "conv_ln_b_2", "pool_scale_2", "ffn_conv_w_2", "ffn_conv_b_2"):
        vectors(name, flat(name))
    for name in ("dsw_q_norm", "dsw_k_norm"):
        vectors(name, (ins[name], ins[name]))
    for layer in range(DEPTH):
        pos = ins["nsa_cmp_pos_2"]
        vectors(f"cmp_pos{layer}", (pos[layer, 0, :, :], pos[layer, 1, :, :]))
    loads, at = [], 0
    for name, ap, _ in rows:
        c.places[name] = at
        parts = [(ap, 0, P)] if not isinstance(ap, tuple) else [(ap[0], 0, 64), (ap[1], 64, 64)]
        n = parts[0][0].shape[0]
        for part, c0, w in parts:
            done = 0
            while done < n:
                r = at + done
                k = min(n - done, P - r % P)
                loads.append((r // P, r % P, k, c0, w, part[done:done + k, :]))
                done += k
        at += n
    assert 7 * P < at <= 8 * P
    early = [x for x in loads if x[0] < 7]
    late = [x for x in loads if x[0] == 7]

    w_ada, ADA, STEPS = ins["w_ada"], 6, 6 * D // 512
    assert STEPS % ADA == 0
    with c.stage(x_rows=[P, TT, D], vec_rows=[P, 8, P], cond=[P, KT], tiles=[P, ADA, KT, 512],
                 scaled=[P, 2, 2, 512]) as (block, sems, x_rows, vec_rows, cond, tiles, scaled):
        x_loaded, consts_loaded, vecs_loaded, cleared, turned, copied, cond_ready, done, mod_ready, added, summed = sems[:11]
        loaded = sems[11:11 + ADA]

        @block.gpsimd
        def _(pool):
            nc.gpsimd.memset(vec_rows[:, 7, :], 0.0).then_inc(cleared, 1)
            nc.gpsimd.memset(c.eps[:, :], EPS).then_inc(cleared, 1)
            pool.wait_ge(cleared, 2)

        @block.sync
        def _(sp):
            sp.dma_start(c.ident[:, :], c.const("ident")).then_inc(consts_loaded, 16)
            sp.dma_start(c.ones[:, :], c.const("ones")).then_inc(consts_loaded, 16)
            sp.dma_start(c.halves[:, :], c.const("halves")).then_inc(consts_loaded, 16)
            sp.dma_start(x_rows[:, :, :], ins["x"][0, :, :].rearrange("(t p) d -> p t d", p=P)).then_inc(x_loaded, 16)
            for tile, r, k, c0, w, src in early:
                sp.dma_start(vec_rows[r:r + k, tile, c0:c0 + w], src).then_inc(vecs_loaded, 16)
            sp.wait_ge(cleared, 1)
            for tile, r, k, c0, w, src in late:
                sp.dma_start(vec_rows[r:r + k, tile, c0:c0 + w], src).then_inc(vecs_loaded, 16)

        @block.tensor
        def _(pe):
            pe.wait_ge(consts_loaded, 48)
            pe.wait_ge(x_loaded, 16)
            for k in range(KT):
                for t in range(TT):
                    last = nc.tensor.transpose(c.ps[:, k, t * P:(t + 1) * P],
                                               x_rows[:, t, k * P:(k + 1) * P], c.ident[:, :])
                last.then_inc(turned, 1)
            pe.wait_ge(vecs_loaded, 16 * len(loads))
            for b in range(2):
                pe.wait_ge(copied, b + 1)
                for t in range(4):
                    last = nc.tensor.transpose(c.ps[:, b, t * P:(t + 1) * P], vec_rows[:, 4 * b + t, :], c.ident[:, :])
                last.then_inc(turned, 1)
            pe.wait_ge(cond_ready, 1)
            with pe.Fori(0, DEPTH * STEPS // 2) as i:
                for s in range(2):
                    pe.wait_ge(done, i * 2 + (s + 1 + ADA))
                    for t in range(4):
                        for part in range(2):
                            last = nc.tensor.matmul(c.ps[:, 0, ds(i * 8 + (4 * s + t), 1)],
                                                    scaled[:, s, part, t * P:(t + 1) * P], c.ones[:, 0:1],
                                                    start=(part == 0), stop=(part == 1))
                    last.then_inc(summed, 1)

        @block.scalar
        def _(act):
            def load(layer, i):
                for s in range(ADA):
                    act.wait_ge(done, i * ADA + (layer * STEPS + s + 1))
                    act.dma_start(tiles[:, s, :, :], columns(w_ada[layer, :, :], i * (512 * ADA) + 512 * s, 512)).then_inc(loaded[s], 16)

            load(0, 0)
            act.wait_ge(copied, KT + 2)
            cc = c.column("c")
            nc.scalar.activation(cond[:, :], c.vec[:, cc:cc + KT], ACT.Silu).then_inc(cond_ready, 1)
            for i in range(1, STEPS // ADA):
                load(0, i)
            for layer in range(1, DEPTH):
                with act.Fori(0, STEPS // ADA) as i:
                    load(layer, i)

        @block.vector
        def _(dve):
            dve.sem_inc(done, ADA)
            dve.sem_inc(summed, 2)
            for k in range(KT):
                dve.wait_ge(turned, k + 1)
                nc.vector.tensor_copy(c.x[:, k, :], c.ps[:, k, :]).then_inc(copied, 1)
            for b in range(2):
                dve.wait_ge(turned, KT + b + 1)
                nc.vector.tensor_copy(c.vec[:, b * 512:(b + 1) * 512], c.ps[:, b, :]).then_inc(copied, 1)
            dve.wait_ge(copied, KT + 2)
            dve.wait_ge(cond_ready, 1)
            with dve.Fori(0, DEPTH * STEPS // ADA) as i:
                for s in range(ADA):
                    n = i * ADA + s
                    dve.wait_ge(loaded[s], i * 16 + 16)
                    dve.wait_ge(summed, n + 1)
                    for k in range(KT):
                        to = scaled[:, s % 2, k % 2, :]
                        if k < 2:
                            ins = nc.vector.tensor_scalar(to, tiles[:, s, k, :], cond[:, k:k + 1], None, ALU.mult)
                        else:
                            dve.wait_ge(added, n * (KT - 1) + (k - 1))
                            ins = nc.vector.scalar_tensor_tensor(to, tiles[:, s, k, :], cond[:, k:k + 1], to, ALU.mult, ALU.add)
                        ins.then_inc(added if k < KT - 1 else done, 1)
            dve.wait_ge(summed, DEPTH * STEPS + 2)
            at = c.column("b_ada")
            nc.vector.tensor_tensor(c.mod[:, :], c.ps[:, 0, 0:DEPTH * 48], c.vec[:, at:at + DEPTH * 48],
                                    ALU.add).then_inc(mod_ready, 1)
            dve.wait_ge(mod_ready, 1)
            for layer in range(DEPTH):
                for j, (name, part) in enumerate((("norm_mix", 1), ("norm_ffn", 4))):
                    g = c.column(name, layer * KT)
                    m = layer * 48 + part * KT
                    o = (layer * 2 + j) * KT
                    nc.vector.scalar_tensor_tensor(c.gains[:, o:o + KT], c.mod[:, m:m + KT], 1.0,
                                                   c.vec[:, g:g + KT], ALU.add, ALU.mult)


def modulation(c, layer, part):
    return layer * 48 + part * KT


def norm(c, gain, shift=None):
    nc = c.nc
    with c.stage(root=[P, S], rstd=[P, S]) as (block, sems, root, rstd):
        squared, summed, root_ready, rstd_ready, scaled = sems[:5]

        @block.scalar
        def _(act):
            for k in range(KT):
                nc.scalar.activation(c.h[:, k, :], c.x[:, k, :], ACT.Square).then_inc(squared, 1)
            act.wait_ge(summed, 1)
            nc.scalar.activation(root[:, :], c.ps[:, 0, :], ACT.Sqrt, bias=c.eps[:, :], scale=1.0 / D).then_inc(root_ready, 1)
            if shift is not None:
                for k in range(KT):
                    act.wait_ge(scaled, k + 1)
                    nc.scalar.activation(c.h[:, k, :], c.h[:, k, :], ACT.Identity, bias=shift(k))

        @block.tensor
        def _(pe):
            for k in range(KT):
                pe.wait_ge(squared, k + 1)
                last = nc.tensor.matmul(c.ps[:, 0, :], c.ones[:, :], c.h[:, k, :], start=(k == 0), stop=(k == KT - 1))
            last.then_inc(summed, 1)

        @block.vector
        def _(dve):
            dve.wait_ge(root_ready, 1)
            nc.vector.reciprocal(rstd[:, :], root[:, :]).then_inc(rstd_ready, 1)
            dve.wait_ge(rstd_ready, 1)
            for k in range(KT):
                nc.vector.scalar_tensor_tensor(c.h[:, k, :], c.x[:, k, :], gain(k), rstd[:, :],
                                               ALU.mult, ALU.mult).then_inc(scaled, 1)


def project_out(c, w, kt, moving, finish):
    nc = c.nc
    with c.stage() as (block, sems):
        loaded, done, freed = sems[0:2], sems[2], sems[3]

        @block.sync
        def _(sp):
            stream_weights(sp, c, KT, lambda n, slot: [
                (slot[:, 0:kt * P].rearrange("p (k n) -> p k n", k=kt), columns(w, n * P, P))], loaded, done)

        @block.tensor
        def _(pe):
            multiply_steps(pe, c, KT, 1, loaded, done, freed, 1, kt,
                           lambda slot, t, k: slot[:, k * P:(k + 1) * P], moving)

        @block.vector
        def _(dve):
            dve.sem_inc(freed, 2)
            with dve.Fori(0, KT // 2) as i:
                for s in range(2):
                    dve.wait_ge(done, i * 2 + s + 3)
                    finish(i * 2 + s, c.ps[:, 4 * s, :]).then_inc(freed, 1)


def add_gated(c, layer, part):
    g = modulation(c, layer, part)
    return lambda n, psum: c.nc.vector.scalar_tensor_tensor(
        c.x[:, ds(n, 1), :], psum, c.mod[:, ds(n + g, 1)], c.x[:, ds(n, 1), :], ALU.mult, ALU.add)


def swiglu(c, layer):
    nc = c.nc
    w_in, w_out = c.ins["w_ffn_in"][layer, :, :], c.ins["w_ffn_out"][layer, :, :]
    norm(c, lambda k: c.gains[:, (layer * 2 + 1) * KT + k:(layer * 2 + 1) * KT + k + 1],
         lambda k: c.mod[:, modulation(c, layer, 3) + k:modulation(c, layer, 3) + k + 1])
    with c.nc.sbuf_tensor(f"ffn_hidden{layer}", [P, FT, S], F32) as hidden:
        with c.stage(gate=[P, 2, S]) as (block, sems, gate):
            loaded, done, freed, gated = sems[0:2], sems[2], sems[3], sems[4]

            @block.sync
            def _(sp):
                def loads(n, slot):
                    v = slot[:, 0:2 * KT * P].rearrange("p (g k n) -> p g k n", g=2, k=KT)
                    return [(v[:, g, :, :], columns(w_in, n * P + g * F1, P)) for g in range(2)]
                stream_weights(sp, c, FT, loads, loaded, done)

            @block.tensor
            def _(pe):
                multiply_steps(pe, c, FT, 2, loaded, done, freed, 2, KT,
                               lambda slot, t, k: slot[:, (t * KT + k) * P:(t * KT + k + 1) * P],
                               lambda k: c.h[:, k, :])

            @block.scalar
            def _(act):
                with act.Fori(0, FT // 2) as i:
                    for s in range(2):
                        act.wait_ge(done, i * 2 + s + 3)
                        act.wait_ge(freed, i * 2 + s + 1)
                        nc.scalar.activation(gate[:, s, :], c.ps[:, 4 * s, :], ACT.Silu).then_inc(gated, 1)

            @block.vector
            def _(dve):
                dve.sem_inc(freed, 2)
                with dve.Fori(0, FT // 2) as i:
                    for s in range(2):
                        dve.wait_ge(gated, i * 2 + s + 1)
                        nc.vector.tensor_tensor(hidden[:, ds(i * 2 + s, 1), :], c.ps[:, 4 * s + 1, :],
                                                gate[:, s, :], ALU.mult).then_inc(freed, 1)

        project_out(c, w_out, FT, lambda k: hidden[:, k, :], add_gated(c, layer, 5))


def write_out(c):
    nc = c.nc
    with c.stage(x_rows=[P, TT, D]) as (block, sems, x_rows):
        turned, copied, stored = sems[:3]

        @block.tensor
        def _(pe):
            for b in range(8):
                t, half = b // 2, b % 2
                for j in range(4):
                    last = nc.tensor.transpose(c.ps[:, b, j * P:(j + 1) * P],
                                               c.x[:, half * 4 + j, t * P:(t + 1) * P], c.ident[:, :])
                last.then_inc(turned, 1)

        @block.vector
        def _(dve):
            for b in range(8):
                dve.wait_ge(turned, b + 1)
                nc.vector.tensor_copy(x_rows[:, b // 2, (b % 2) * 512:(b % 2 + 1) * 512], c.ps[:, b, :]).then_inc(copied, 1)

        @block.sync
        def _(sp):
            for t in range(TT):
                sp.wait_ge(copied, 2 * t + 2)
                sp.dma_start(c.out[0, t * P:(t + 1) * P, :], x_rows[:, t, :]).then_inc(stored, 16)
            sp.wait_ge(stored, 16 * TT)


def gdn_rows(c, decay_rows, decay_cols):
    nc, w = c.nc, c.ins["gdn_w_in"][0, :, :]
    G, E, B = range(3)
    with c.stage(w_ab=[P, KT, 2 * GH], stacked=[P, S], work=[GH, 4, S], resets=[GH, S],
                 scalars=[GH, 4]) as (block, sems, w_ab, stacked, work, resets, scalars):
        (loaded, projected, cleared, rows_stacked, turned, act_link, dve_link, rate_ready, exp_ready,
         log_ready, scanned, e_ready, sum_ready, beta_ready, be_ready, rest_ready) = sems[:16]

        @block.sync
        def _(sp):
            sp.dma_start(w_ab[:, :, :], columns(w, GCH + GHK, 2 * GH)).then_inc(loaded, 16)
            sp.dma_start(resets[:, :], c.const("resets", GH)).then_inc(loaded, 16)
            sp.dma_start(scalars[:, 0:1], c.ins["gdn_a_log"].rearrange("a h -> h a")).then_inc(loaded, 16)
            sp.dma_start(scalars[:, 1:2], c.ins["gdn_dt_bias"].rearrange("a h -> h a")).then_inc(loaded, 16)

        @block.gpsimd
        def _(pool):
            nc.gpsimd.memset(stacked[:, :], 0.0).then_inc(cleared, 1)

        @block.tensor
        def _(pe):
            pe.wait_ge(loaded, 64)
            for part in range(2):
                for k in range(KT):
                    last = nc.tensor.matmul(c.ps[0:GH, part, :], w_ab[:, k, part * GH:(part + 1) * GH], c.h[:, k, :],
                                            start=(k == 0), stop=(k == KT - 1))
                last.then_inc(projected, 1)
            pe.wait_ge(rows_stacked, 4)
            for t in range(TT):
                last = nc.tensor.transpose(c.ps[:, 2, t * P:(t + 1) * P], stacked[:, t * P:(t + 1) * P], c.ident[:, :])
            last.then_inc(turned, 1)

        @block.scalar
        def _(act):
            link = Links(act, act_link)
            act.wait_ge(loaded, 64)
            link.do(nc.scalar.activation(scalars[:, 2:3], scalars[:, 0:1], ACT.Exp))
            nc.scalar.activation(scalars[:, 3:4], scalars[:, 2:3], ACT.Copy, scale=-1.0).then_inc(rate_ready, 1)
            act.wait_ge(sum_ready, 1)
            link.do(nc.scalar.activation(work[:, 1, :], work[:, 0, :], ACT.Abs))
            link.do(nc.scalar.activation(work[:, 1, :], work[:, 1, :], ACT.Exp, scale=-1.0))
            nc.scalar.activation(work[:, 1, :], work[:, 1, :], ACT.Ln, bias=1.0).then_inc(log_ready, 1)
            act.wait_ge(scanned, 1)
            nc.scalar.activation(decay_rows[:, E, :], decay_rows[:, G, :], ACT.Exp).then_inc(e_ready, 1)
            act.wait_ge(rest_ready, 1)
            act.wait_ge(cleared, 1)
            nc.scalar.activation(stacked[96:96 + GH, :], work[:, 3, :], ACT.Exp).then_inc(rows_stacked, 1)
            act.wait_ge(projected, 2)
            nc.scalar.activation(decay_rows[:, B, :], c.ps[0:GH, 1, :], ACT.Sigmoid).then_inc(beta_ready, 1)
            act.wait_ge(beta_ready, 1)
            nc.scalar.activation(stacked[32:32 + GH, :], decay_rows[:, B, :], ACT.Copy).then_inc(rows_stacked, 1)
            act.wait_ge(be_ready, 1)
            nc.scalar.activation(stacked[64:64 + GH, :], work[:, 2, :], ACT.Copy).then_inc(rows_stacked, 1)
            nc.scalar.activation(stacked[0:GH, :], decay_rows[:, G, :], ACT.Copy).then_inc(rows_stacked, 1)

        @block.vector
        def _(dve):
            link = Links(dve, dve_link)
            dve.wait_ge(loaded, 64)
            dve.wait_ge(projected, 1)
            nc.vector.tensor_scalar(work[:, 0, :], c.ps[0:GH, 0, :], scalars[:, 1:2], None, ALU.add).then_inc(sum_ready, 1)
            dve.wait_ge(log_ready, 1)
            link.do(nc.vector.scalar_tensor_tensor(work[:, 0, :], work[:, 0, :], 0.0, work[:, 1, :], ALU.max, ALU.add))
            dve.wait_ge(rate_ready, 1)
            link.do(nc.vector.tensor_scalar(work[:, 0, :], work[:, 0, :], scalars[:, 3:4], None, ALU.mult))
            nc.vector.tensor_tensor_scan(decay_rows[:, G, :], resets[:, :], work[:, 0, :], 0.0,
                                         ALU.mult, ALU.add).then_inc(scanned, 1)
            dve.wait_ge(scanned, 1)
            g = decay_rows[:, G, :].rearrange("h (n t) -> h n t", t=GC)
            nc.vector.tensor_tensor(work[:, 3, :].rearrange("h (n t) -> h n t", t=GC),
                                    g[:, :, GC - 1:GC].to_broadcast([GH, NCH, GC]), g, ALU.subtract).then_inc(rest_ready, 1)
            dve.wait_ge(e_ready, 1)
            dve.wait_ge(beta_ready, 1)
            nc.vector.tensor_tensor(work[:, 2, :], decay_rows[:, B, :], decay_rows[:, E, :], ALU.mult).then_inc(be_ready, 1)
            dve.wait_ge(turned, 1)
            nc.vector.tensor_copy(decay_cols[:, :, :].rearrange("p t (q h) -> p t q h", h=GH),
                                  c.ps[:, 2, :].rearrange("p (t q n) -> p t q n", t=TT, q=4)[:, :, :, 0:GH])


def gdn_heads(c, st, decay_rows, decay_cols):
    nc, w = c.nc, c.ins["gdn_w_in"][0, :, :]
    G, E, B = range(3)
    with c.stage(two_qkv=[P, 2, 3, S], root=[P, 2, S], picks=[GH, 2, P], hot=[GH, GH], chunkmask=[P, P]) as (
            block, sems, two_qkv, root, picks, hot, chunkmask):
        square = root
        decay = root[:, 0, :].rearrange("p (t n) -> p t n", t=TT)
        kb = root[:, 1, :]
        (load0, load1, consts, projected, freed, filtered, convolved, silued, z_ready, squared, summed, rooted, normed,
         picked, spread, kb_ready, exponent, decayed, products, k_turned, v_turned, q_decayed, dve_link,
         ends_ready) = sems[:24]
        loaded = (load0, load1)
        TILES = 4
        LINKS = 3 * (GCONV - 2) + 2 + 1

        @block.sync
        def _(sp):
            sp.dma_start(hot[:, :], c.const("hot8", GH)).then_inc(consts, 16)
            sp.dma_start(chunkmask[:, :], c.const("chunkmask")).then_inc(consts, 16)
            with sp.Fori(0, GH // 2) as i:
                for s in range(2):
                    n = i * 2 + s
                    tiles = c.slots[s][:, :].rearrange("p (g k n) -> p g k n", g=TILES, k=KT)
                    sp.wait_ge(projected, n * TILES + TILES)
                    for t in range(TILES):
                        sp.dma_start(tiles[:, t, :, :], columns(w, n * P + t * GHK, P)).then_inc(loaded[s], 16)

        @block.tensor
        def _(pe):
            pe.sem_inc(projected, 2 * TILES)
            pe.wait_ge(consts, 32)

            def project(s, t):
                for k in range(KT):
                    last = nc.tensor.matmul(c.ps[:, t, :], c.slots[s][:, (t * KT + k) * P:(t * KT + k + 1) * P],
                                            c.h[:, k, :], start=(k == 0), stop=(k == KT - 1))
                last.then_inc(projected, 1)

            def head(n, s, next_rounds):
                qkv = two_qkv[:, s, :, :]
                if next_rounds is not None:
                    pe.wait_ge(loaded[1 - s], next_rounds * (16 * TILES))
                    pe.wait_ge(convolved, n * 3 + 1)
                    project(1 - s, 0)
                pe.wait_ge(freed, n + 1)
                pe.wait_ge(squared, n * 2 + 2)
                for t in range(2):
                    last = nc.tensor.matmul(c.ps[:, 4 + t, :], c.ones[:, :], square[:, t, :], start=True, stop=True)
                last.then_inc(summed, 1)
                if next_rounds is not None:
                    pe.wait_ge(convolved, n * 3 + 2)
                    project(1 - s, 1)
                pe.wait_ge(picked, n + 1)
                pe.wait_ge(rooted, n * 2 + 1)
                for r, bank in ((G, 6), (E, 7), (B, 4)):
                    last = nc.tensor.matmul(c.ps[:, bank, :], picks[:, s, :], decay_rows[:, r, :], start=True, stop=True)
                last.then_inc(spread, 1)
                if next_rounds is not None:
                    pe.wait_ge(convolved, n * 3 + 3)
                    project(1 - s, 2)
                pe.wait_ge(normed, n * 2 + 2)
                for t in range(TT):
                    last = nc.tensor.transpose(c.ps[:, 5, t * P:(t + 1) * P], qkv[:, 1, t * P:(t + 1) * P], c.ident[:, :])
                last.then_inc(k_turned, 1)
                pe.wait_ge(silued, n * 3 + 3)
                pe.wait_ge(exponent, n + 1)
                for t in range(TT):
                    last = nc.tensor.transpose(c.ps[:, 6, t * P:(t + 1) * P], qkv[:, 2, t * P:(t + 1) * P], c.ident[:, :])
                last.then_inc(v_turned, 1)
                if next_rounds is not None:
                    pe.wait_ge(z_ready, n + 1)
                    project(1 - s, 3)
                pe.wait_ge(kb_ready, n + 1)
                pe.wait_ge(q_decayed, n + 1)
                for t in range(TT):
                    at = slice(t * P, (t + 1) * P)
                    nc.tensor.matmul(c.ps[:, 7, at], qkv[:, 1, at], qkv[:, 0, at], start=True, stop=True)
                for t in range(TT):
                    at = slice(t * P, (t + 1) * P)
                    last = nc.tensor.matmul(c.ps[:, 4, at], qkv[:, 1, at], kb[:, at], start=True, stop=True)
                last.then_inc(products, 1)

            pe.wait_ge(loaded[0], 16 * TILES)
            for t in range(TILES):
                project(0, t)
            with pe.Fori(0, GH // 2 - 1) as i:
                head(i * 2, 0, i + 1)
                head(i * 2 + 1, 1, i + 2)
            head(GH - 2, 0, GH // 2)
            head(GH - 1, 1, None)

        @block.scalar
        def _(act):
            cw = c.column("gdn_conv")
            act.wait_ge(consts, 32)
            with act.Fori(0, GH // 2) as i:
                for s in range(2):
                    n = i * 2 + s
                    qkv = two_qkv[:, s, :, :]
                    for t in range(3):
                        act.wait_ge(projected, n * TILES + (2 * TILES + t + 1))
                        if t == 0:
                            act.wait_ge(freed, n + 1)
                        nc.scalar.activation(qkv[:, t, :], c.ps[:, t, :], ACT.Copy,
                                             scale=c.vec[:, ds(n + (cw + 3 * 24 + t * GH), 1)]).then_inc(filtered, 1)
                    nc.scalar.activation(picks[:, s, :], c.ones[0:GH, :], ACT.Copy, scale=hot[:, ds(n, 1)]).then_inc(picked, 1)
                    act.wait_ge(projected, n * TILES + 3 * TILES)
                    nc.scalar.activation(st["z"][:, ds(n, 1), :], c.ps[:, 3, :], ACT.Silu).then_inc(z_ready, 1)
                    for t in range(3):
                        act.wait_ge(convolved, n * 3 + t + 1)
                        nc.scalar.activation(qkv[:, t, :], qkv[:, t, :], ACT.Silu).then_inc(silued, 1)
                    for t in range(2):
                        act.wait_ge(silued, n * 3 + t + 1)
                        nc.scalar.activation(square[:, t, :], qkv[:, t, :], ACT.Square).then_inc(squared, 1)
                    act.wait_ge(summed, n + 1)
                    for t in range(2):
                        nc.scalar.activation(root[:, t, :], c.ps[:, 4 + t, :], ACT.Sqrt, bias=c.eps[:, :]).then_inc(rooted, 1)
                    act.wait_ge(spread, n + 1)
                    nc.scalar.activation(st["ends"][:, ds(n, 1), :], c.ps[:, 7, GC - 1:S:GC], ACT.Copy).then_inc(ends_ready, 1)
                    act.wait_ge(exponent, n + 1)
                    nc.scalar.activation(decay, decay, ACT.Exp).then_inc(decayed, 1)

        @block.vector
        def _(dve):
            cw = c.column("gdn_conv")
            dve.sem_inc(freed, 1)
            dve.wait_ge(consts, 32)
            with dve.Fori(0, GH // 2) as i:
                for s in range(2):
                    n = i * 2 + s
                    qkv = two_qkv[:, s, :, :]
                    link = Links(dve, dve_link, n * LINKS)
                    for t in range(3):
                        dve.wait_ge(filtered, n * 3 + t + 1)
                        for back in range(1, GCONV):
                            ins = nc.vector.scalar_tensor_tensor(
                                qkv[:, t, back:S], c.ps[:, t, 0:S - back],
                                c.vec[:, ds(n + (cw + (GCONV - 1 - back) * 24 + t * GH), 1)], qkv[:, t, back:S],
                                ALU.mult, ALU.add)
                            if back < GCONV - 1:
                                link.do(ins)
                            else:
                                ins.then_inc(convolved, 1)
                    for t in range(2):
                        dve.wait_ge(rooted, n * 2 + t + 1)
                        link.do(nc.vector.reciprocal(root[:, t, :], root[:, t, :]))
                        nc.vector.scalar_tensor_tensor(qkv[:, t, :], qkv[:, t, :], (GDK ** -0.5, 1.0)[t], root[:, t, :],
                                                       ALU.mult, ALU.mult).then_inc(normed, 1)
                    dve.wait_ge(spread, n + 1)
                    dve.wait_ge(normed, n * 2 + 2)
                    nc.vector.tensor_tensor(kb, qkv[:, 1, :], c.ps[:, 4, :], ALU.mult).then_inc(kb_ready, 1)
                    for t in range(TT):
                        last = nc.vector.tensor_scalar(decay[:, t, :], c.ps[:, 6, t * P:(t + 1) * P],
                                                       decay_cols[:, t, ds(n, 1)], 0.0, ALU.subtract, ALU.min)
                    last.then_inc(exponent, 1)
                    dve.wait_ge(ends_ready, n + 1)
                    nc.vector.tensor_tensor(st["qd"][:, ds(n, 1), :], qkv[:, 0, :], c.ps[:, 7, :], ALU.mult).then_inc(q_decayed, 1)
                    dve.wait_ge(k_turned, n + 1)
                    for t in range(TT):
                        at = slice(t * P, (t + 1) * P)
                        nc.vector.tensor_scalar(st["kbg"][:, ds(n, 1), at], c.ps[:, 5, at], decay_cols[:, t, ds(n + 2 * GH, 1)], None, ALU.mult)
                        nc.vector.tensor_scalar(st["kd"][:, ds(n, 1), at], c.ps[:, 5, at], decay_cols[:, t, ds(n + 3 * GH, 1)], None, ALU.mult)
                    dve.wait_ge(v_turned, n + 1)
                    for t in range(TT):
                        at = slice(t * P, (t + 1) * P)
                        nc.vector.tensor_scalar(st["vb"][:, ds(n, 1), at], c.ps[:, 6, at], decay_cols[:, t, ds(n + 1 * GH, 1)], None, ALU.mult)
                    dve.wait_ge(decayed, n + 1)
                    link.do(nc.vector.tensor_tensor(decay, decay,
                                                    chunkmask[:, :].unsqueeze(1).to_broadcast([P, TT, P]), ALU.mult))
                    dve.wait_ge(products, n + 1)
                    flat = decay.rearrange("p t n -> p (t n)")
                    nc.vector.tensor_tensor(st["qk"][:, ds(n, 1), :], c.ps[:, 7, :], flat, ALU.mult)
                    nc.vector.tensor_tensor(st["lt"][:, ds(n, 1), :], c.ps[:, 4, :], flat, ALU.mult).then_inc(freed, 1)
                    assert link.n == LINKS


def gdn_inverse(c, st, tt, uu):
    nc = c.nc
    with c.stage(levels=[P, LEVELS, P], masked=[P, 2, S], inner=[P, 2, S]) as (block, sems, levels, masked, inner):
        consts, mask_ready, started, x_done, x_copied, y_done, z_done, t_ready, u_ready, mask_begun = sems[:10]

        @block.sync
        def _(sp):
            sp.dma_start(levels[:, :, :], c.const("levels").rearrange("p (l n) -> p l n", l=LEVELS)).then_inc(consts, 16)

        @block.gpsimd
        def _(pool):
            pool.wait_ge(consts, 16)
            with pool.Fori(0, LEVELS) as lv:
                for h in range(GH):
                    pool.wait_ge(x_done, lv * GH + h + 1)
                    pool.sem_inc(mask_begun, 1)
                    nc.gpsimd.tensor_tensor(masked[:, h % 2, :].rearrange("p (t n) -> p t n", t=TT),
                                            st["lt"][:, h, :].rearrange("p (t n) -> p t n", t=TT),
                                            levels[:, ds(lv, 1), :].to_broadcast([P, TT, P]), ALU.mult).then_inc(mask_ready, 1)

        @block.tensor
        def _(pe):
            pe.sem_inc(x_done, 2)
            pe.wait_ge(started, 2 * GH)

            def inner_product(lv, h):
                pe.wait_ge(mask_ready, lv * GH + h + 1)
                pe.wait_ge(t_ready, lv * GH + h + 1)
                pe.wait_ge(x_copied, lv * GH + h + 1)
                for t in range(TT):
                    at = slice(t * P, (t + 1) * P)
                    last = nc.tensor.matmul(c.ps[:, h % 2, at], masked[:, h % 2, at], tt[:, h, at], start=True, stop=True)
                last.then_inc(x_done, 1)

            def outer_products(lv, h):
                pe.wait_ge(x_copied, lv * GH + h + 3)
                pe.wait_ge(u_ready, lv * GH + h - 1 + GH)
                for t in range(TT):
                    at = slice(t * P, (t + 1) * P)
                    last = nc.tensor.matmul(c.ps[:, 2 + h % 2, at], uu[:, h, at], inner[:, h % 2, at], start=True, stop=True)
                last.then_inc(y_done, 1)
                for t in range(TT):
                    at = slice(t * P, (t + 1) * P)
                    last = nc.tensor.matmul(c.ps[:, 4 + h % 2, at], inner[:, h % 2, at], uu[:, h, at], start=True, stop=True)
                last.then_inc(z_done, 1)

            with pe.Fori(0, LEVELS) as lv:
                for h in range(GH + 1):
                    if h < GH:
                        inner_product(lv, h)
                    if h >= 1:
                        outer_products(lv, h - 1)

        @block.scalar
        def _(act):
            act.sem_inc(x_copied, 2)
            for h in range(GH):
                nc.scalar.activation(uu[:, h, :].rearrange("p (t n) -> p t n", t=TT),
                                     c.ident[:, :].unsqueeze(1).to_broadcast([P, TT, P]), ACT.Copy).then_inc(started, 1)
            with act.Fori(0, LEVELS) as lv:
                for h in range(GH):
                    act.wait_ge(x_done, lv * GH + h + 3)
                    act.wait_ge(z_done, lv * GH + h + 1)
                    nc.scalar.activation(inner[:, h % 2, :], c.ps[:, h % 2, :], ACT.Copy).then_inc(x_copied, 1)

        @block.vector
        def _(dve):
            dve.sem_inc(t_ready, GH)
            dve.sem_inc(u_ready, GH)
            dve.sem_inc(z_done, 2)
            for h in range(GH):
                nc.vector.tensor_copy(tt[:, h, :].rearrange("p (t n) -> p t n", t=TT),
                                      c.ident[:, :].unsqueeze(1).to_broadcast([P, TT, P])).then_inc(started, 1)
            dve.wait_ge(started, 2 * GH)
            with dve.Fori(0, LEVELS) as lv:
                for h in range(GH):
                    dve.wait_ge(y_done, lv * GH + h + 1)
                    nc.vector.tensor_tensor(tt[:, h, :], tt[:, h, :], c.ps[:, 2 + h % 2, :], ALU.subtract).then_inc(t_ready, 1)
                    dve.wait_ge(z_done, lv * GH + h + 3)
                    nc.vector.tensor_tensor(uu[:, h, :], uu[:, h, :], c.ps[:, 4 + h % 2, :], ALU.subtract).then_inc(u_ready, 1)


def gdn_scan(c, st, uu, o):
    nc = c.nc
    nw = st["lt"]
    with c.stage(state=[P, GH, P], v_new=[P, GH, P]) as (block, sems, state, v_new):
        w_done, w_copied, v_done, v_copied, o_done, o_copied, s_done, s_decayed, s_ready, cleared = sems[:10]

        @block.gpsimd
        def _(pool):
            nc.gpsimd.memset(state[:, :, :], 0.0).then_inc(s_ready, 1)

        @block.tensor
        def _(pe):
            for h in range(GH):
                if h >= 2:
                    pe.wait_ge(w_copied, h - 1)
                for t in range(TT):
                    at = slice(t * P, (t + 1) * P)
                    last = nc.tensor.matmul(c.ps[:, h % 2, at], st["kbg"][:, h, at], uu[:, h, at], start=True, stop=True)
                last.then_inc(w_done, 1)
            pe.wait_ge(w_copied, GH)
            for n in range(NCH):
                b, pair = 64 * (n % 2), n // 2
                rows, at = slice(b, b + 64), slice(n * GC, (n + 1) * GC)
                pr = slice(pair * P, (pair + 1) * P)
                pe.wait_ge(s_ready, 2 * n + 1)
                if n:
                    pe.wait_ge(v_copied, 2 * n)
                for h in range(GH):
                    out = c.ps[rows, 2 + h // 4, (h % 4) * P:(h % 4 + 1) * P]
                    nc.tensor.matmul(out, uu[rows, h, at], st["vb"][rows, h, pr], start=True, stop=False)
                    last = nc.tensor.matmul(out, nw[:, h, at], state[:, h, :], start=False, stop=True)
                    if h % 4 == 3:
                        last.then_inc(v_done, 1)
                if n:
                    pe.wait_ge(o_copied, n)
                pe.wait_ge(v_copied, 2 * n + 2)
                for h in range(GH):
                    out = c.ps[:, 4, h * GC:(h + 1) * GC]
                    nc.tensor.matmul(out, state[:, h, :], st["qd"][:, h, at], start=True, stop=False)
                    last = nc.tensor.matmul(out, v_new[rows, h, :], st["qk"][rows, h, at], start=False, stop=True)
                last.then_inc(o_done, 1)
                for h in range(GH):
                    last = nc.tensor.matmul(c.ps[:, 6 + h // 4, (h % 4) * P:(h % 4 + 1) * P], st["kd"][rows, h, pr],
                                            v_new[rows, h, :], start=True, stop=True)
                    if h % 4 == 3:
                        last.then_inc(s_done, 1)

        @block.scalar
        def _(act):
            for h in range(GH):
                act.wait_ge(w_done, h + 1)
                nc.scalar.activation(nw[:, h, :], c.ps[:, h % 2, :], ACT.Copy, scale=-1.0).then_inc(w_copied, 1)
            for n in range(NCH):
                b = 64 * (n % 2)
                rows, at = slice(b, b + 64), slice(n * GC, (n + 1) * GC)
                if n >= 2:
                    act.wait_ge(s_done, 2 * n - 2)
                for half in range(2):
                    act.wait_ge(v_done, 2 * n + half + 1)
                    nc.scalar.activation(v_new[rows, 4 * half:4 * half + 4, :],
                                         c.ps[rows, 2 + half, :].rearrange("p (h d) -> p h d", h=4), ACT.Copy).then_inc(v_copied, 1)
                act.wait_ge(o_done, n + 1)
                nc.scalar.activation(o[:, :, at], c.ps[:, 4, :].rearrange("p (h t) -> p h t", h=GH), ACT.Copy).then_inc(o_copied, 1)

        @block.vector
        def _(dve):
            dve.wait_ge(s_ready, 1)
            for n in range(NCH):
                dve.wait_ge(o_done, n + 1)
                for half in range(2):
                    hs = slice(4 * half, 4 * half + 4)
                    ends = st["ends"][:, hs, n:n + 1].to_broadcast([P, 4, P])
                    if n:
                        dve.wait_ge(s_ready, 2 * n + half)
                    nc.vector.tensor_tensor(state[:, hs, :], state[:, hs, :], ends, ALU.mult).then_inc(s_decayed, 1)
                for half in range(2):
                    hs = slice(4 * half, 4 * half + 4)
                    dve.wait_ge(s_decayed, 2 * n + half + 1)
                    dve.wait_ge(s_done, 2 * n + half + 1)
                    nc.vector.tensor_tensor(state[:, hs, :], state[:, hs, :],
                                            c.ps[:, 6 + half, :].rearrange("p (h d) -> p h d", h=4), ALU.add).then_inc(s_ready, 1)


def gdn_out_norm(c, st, o):
    nc = c.nc
    with c.stage(square=[P, 2, S], root=[P, 2, S]) as (block, sems, square, root):
        squared, summed, rooted, inverted, normed, gated = sems[:6]

        def root_of(act, h):
            act.wait_ge(summed, h + 1)
            if h >= 2:
                act.wait_ge(normed, h - 1)
            nc.scalar.activation(root[:, h % 2, :], c.ps[:, h % 2, :], ACT.Sqrt, bias=c.eps[:, :], scale=1.0 / P).then_inc(rooted, 1)

        @block.scalar
        def _(act):
            for h in range(GH):
                if h >= 2:
                    act.wait_ge(summed, h - 1)
                nc.scalar.activation(square[:, h % 2, :], o[:, h, :], ACT.Square).then_inc(squared, 1)
                if h >= 1:
                    root_of(act, h - 1)
            root_of(act, GH - 1)

        @block.tensor
        def _(pe):
            for h in range(GH):
                pe.wait_ge(squared, h + 1)
                if h >= 2:
                    pe.wait_ge(rooted, h - 1)
                nc.tensor.matmul(c.ps[:, h % 2, :], c.ones[:, :], square[:, h % 2, :], start=True, stop=True).then_inc(summed, 1)

        @block.vector
        def _(dve):
            gain = c.column("gdn_out_norm")
            for h in range(GH):
                dve.wait_ge(rooted, h + 1)
                nc.vector.reciprocal(root[:, h % 2, :], root[:, h % 2, :]).then_inc(inverted, 1)
                dve.wait_ge(inverted, h + 1)
                nc.vector.scalar_tensor_tensor(o[:, h, :], o[:, h, :], c.vec[:, gain:gain + 1], root[:, h % 2, :],
                                               ALU.mult, ALU.mult).then_inc(normed, 1)

        @block.gpsimd
        def _(pool):
            for h in range(GH):
                pool.wait_ge(normed, h + 1)
                nc.gpsimd.tensor_tensor(o[:, h, :], o[:, h, :], st["z"][:, h, :], ALU.mult).then_inc(gated, 1)
            pool.wait_ge(gated, GH)


def gated_deltanet(c, layer):
    nc = c.nc
    with ExitStack() as ctx:
        sb = lambda name, shape: ctx.enter_context(nc.sbuf_tensor(name, shape, F32))
        st = {"z": sb("silu_z", [P, GH, S]), "qd": sb("q_decayed", [P, GH, S]), "qk": sb("qk_decayed", [P, GH, S]),
              "lt": sb("l_transposed", [P, GH, S]), "kbg": sb("keys_beta_decay", [P, GH, S]),
              "kd": sb("keys_to_end", [P, GH, S]), "vb": sb("values_beta", [P, GH, S]),
              "ends": sb("decay_of_chunks", [P, GH, NCH])}
        with nc.sbuf_tensor("decay_rows", [GH, 3, S], F32) as rows, nc.sbuf_tensor("decay_cols", [P, TT, 4 * GH], F32) as cols:
            gdn_rows(c, rows, cols)
            gdn_heads(c, st, rows, cols)
        uu = c.h
        gdn_inverse(c, st, c.slots[0][:, :].rearrange("p (h n) -> p h n", h=GH), uu)
        o = st["qd"]
        gdn_scan(c, st, uu, o)
        gdn_out_norm(c, st, o)
        project_out(c, c.ins["gdn_w_out"][0, :, :], GH, lambda k: o[:, k, :], add_gated(c, layer, 2))


def window_biases(c, scratch, biases):
    nc = c.nc
    planes = ((0, 0), (1, 1), (2, 2), (3, 0))
    with c.stage(table=[BUCKETS + 1, WG * WH], hot=[BUCKETS + 1, 4, 256], rows=[WH, 4, 256],
                 classmask=[P, P], flip=[P, P]) as (block, sems, table, hot, rows, classmask, flip):
        loaded, cleared, done, copied, stored, spread, flipped, turned = sems[:8]
        falling = c.slots[0][:, :].rearrange("p (h j n) -> p h j n", h=WH, j=4)

        @block.gpsimd
        def _(pool):
            nc.gpsimd.memset(table[BUCKETS:BUCKETS + 1, :], NEG).then_inc(cleared, 1)

        @block.sync
        def _(sp):
            sp.dma_start(table[0:BUCKETS, :], c.ins["rel_bias"]).then_inc(loaded, 16)
            sp.dma_start(hot[:, :, :], c.const("buckets", BUCKETS + 1).rearrange("b (g n) -> b g n", g=4)).then_inc(loaded, 16)
            sp.dma_start(classmask[:, :], c.const("classmask")).then_inc(loaded, 16)
            sp.dma_start(flip[:, :], c.const("flip")).then_inc(loaded, 16)
            sp.wait_ge(copied, 4)
            sp.dma_start(scratch.rearrange("g h n -> h g n"), rows[:, :, :]).then_inc(stored, 16)
            sp.wait_ge(stored, 16)
            for tile, plane in enumerate((3, 0, 1, 2)):
                src = bass.AP(tensor=scratch.tensor, offset=plane * WH * 256, ap=[[1, P], [256, WH], [1, P]])
                sp.dma_start(falling[:, :, tile, :], src).then_inc(spread, 16)

        @block.tensor
        def _(pe):
            pe.wait_ge(loaded, 64)
            pe.wait_ge(cleared, 1)
            for plane, g in planes:
                nc.tensor.matmul(c.ps[0:WH, plane, 0:256], table[:, g * WH:(g + 1) * WH], hot[:, plane, :],
                                 start=True, stop=True).then_inc(done, 1)
            pe.wait_ge(spread, 64)
            for h in range(WH):
                if h < 4:
                    pe.wait_ge(copied, h + 1)
                nc.tensor.matmul(c.ps[:, h, :], flip[:, :], falling[:, h, :, :].rearrange("p j n -> p (j n)"),
                                 start=True, stop=True).then_inc(flipped, 1)

        @block.vector
        def _(dve):
            for plane, _ in planes:
                dve.wait_ge(done, plane + 1)
                nc.vector.tensor_copy(rows[:, plane, :], c.ps[0:WH, plane, 0:256]).then_inc(copied, 1)
            for h in range(WH):
                dve.wait_ge(flipped, h + 1)
                last = nc.vector.tensor_copy(biases[:, h, :, :], c.ps[:, h, :].rearrange("p (j n) -> p j n", j=4))
            last.then_inc(turned, 1)
            dve.wait_ge(turned, 1)
            dve.wait_ge(loaded, 64)
            nc.vector.tensor_tensor(biases[:, :, 3, :], biases[:, :, 3, :],
                                    classmask[:, :].unsqueeze(1).to_broadcast([P, WH, P]), ALU.add)


def by_class(ap, dilation):
    return ap.rearrange("p (r i) -> p i r", r=dilation)


def by_token(ap, dilation):
    return ap.rearrange("p (i r) -> p i r", r=dilation)


def window_attention(c, biases, o_groups, neg_max, sums):
    nc, w = c.nc, c.ins["dsw_w_in"][0, :, :]
    NP, NU = WH // 2, 8
    PAIRS = WG * NP
    with c.stage(square=[P, 2, S], root=[P, 2, S], q=[P, S], k=[P, S], v=[P, S],
                 v_rows=[P, TT, P], probs=[P, 2, 2 * P], probs_t=[P, 2, 2, P], inverse=[P, 2], eps64=[P, 1]) as (
            block, sems, square, root, q, k, v, v_rows, probs, probs_t, inverse, eps64):
        (w0, w1, projected, v_projected, squared, v_copied, summed, rooted, inverted, normed, v_turned,
         v_ready, scored, biased, maxed, exped, inverse_ready, weighed, turned, turned_copied, attended, o_copied,
         cleared) = sems[:23]
        w_loaded = (w0, w1)

        def units(g):
            return [(a, b, b - (g == 0 and b > 0), 1 + (g == 0 and b > 0)) for a in range(2) for b in range(TT)]

        def pairs(engine, body):
            for g in range(WG):
                with engine.Fori(0, NP // 2) as i:
                    for s in range(2):
                        body(g, i * 2 + s, s)

        @block.gpsimd
        def _(pool):
            nc.gpsimd.memset(eps64[:, :], 64 * EPS).then_inc(cleared, 1)
            pool.wait_ge(cleared, 1)

        @block.sync
        def _(sp):
            def load(g, n, s):
                m = n + NP * g
                sp.wait_ge(v_projected, m + 1)
                for part in range(3):
                    sp.dma_start(c.slots[s][:, part * D:(part + 1) * D].rearrange("p (k n) -> p k n", k=KT),
                                 columns(w, n * P + (part * WG + g) * WHG, P)).then_inc(w_loaded[s], 16)
            pairs(sp, load)

        @block.tensor
        def _(pe):
            pe.sem_inc(v_projected, 2)
            pe.sem_inc(v_turned, 1)
            pe.sem_inc(turned, 2)
            pe.sem_inc(attended, 2)

            def project(s, part, ks):
                for kk in ks:
                    last = nc.tensor.matmul(c.ps[:, part, :], c.slots[s][:, (part * KT + kk) * P:(part * KT + kk + 1) * P],
                                            c.h[:, kk, :], start=(kk == 0), stop=(kk == KT - 1))
                return last

            def pair(g, n, s, follow):
                m = n + NP * g
                pe.wait_ge(squared, m * 2 + 2)
                for part in range(2):
                    nc.tensor.matmul(c.ps[:, 3 + part, :], c.halves[:, :], square[:, part, :],
                                     start=True, stop=True).then_inc(summed, 1)
                project(s, 2, range(KT)).then_inc(v_projected, 1)
                pe.wait_ge(v_copied, m + 1)
                pe.wait_ge(o_copied, m + 1)
                for t in range(TT):
                    last = nc.tensor.transpose(c.ps[:, 5, t * P:(t + 1) * P], v[:, t * P:(t + 1) * P], c.ident[:, :])
                last.then_inc(v_turned, 1)
                pe.wait_ge(normed, m * 2 + 2)
                us = units(g)
                for t in range(NU + 2):
                    if t < NU:
                        a, b, kb, nk = us[t]
                        h = slice(64 * a, 64 * a + 64)
                        pe.wait_ge(exped, m * NU + t + 1)
                        nc.tensor.matmul(c.ps[:, 6 + t % 2, 0:nk * P], q[h, b * P:(b + 1) * P],
                                         k[h, kb * P:(kb + nk) * P], start=True, stop=True).then_inc(scored, 1)
                    if follow and t < NU:
                        if t == 0:
                            follow(pe)
                        for j in range(2 * t, 2 * t + 2):
                            last = project(1 - s, j // KT, [j % KT])
                        if t == NU - 1:
                            last.then_inc(projected, 1)
                    if 1 <= t <= NU:
                        u = t - 1
                        a, b, kb, nk = us[u]
                        pe.wait_ge(weighed, m * NU + u + 1)
                        pe.wait_ge(turned_copied, m * NU + u + 1)
                        for j in range(nk):
                            last = nc.tensor.transpose(c.ps[:, 3 + u % 2, j * P:(j + 1) * P],
                                                       probs[:, u % 2, j * P:(j + 1) * P], c.ident[:, :])
                        last.then_inc(turned, 1)
                    if t >= 2:
                        u = t - 2
                        a, b, kb, nk = us[u]
                        if u == 0:
                            pe.wait_ge(v_ready, m + 1)
                        pe.wait_ge(turned_copied, m * NU + u + 3)
                        for j in range(nk):
                            last = nc.tensor.matmul(c.ps[64 * a:64 * a + 64, 5, b * P:(b + 1) * P],
                                                    v_rows[:, kb + j, 64 * a:64 * a + 64], probs_t[:, u % 2, j, :],
                                                    start=(j == 0), stop=(j == nk - 1))
                        last.then_inc(attended, 1)

            def weights_landed(s, rounds):
                def wait(engine):
                    engine.wait_ge(w_loaded[s], rounds * 48)
                return wait

            pe.wait_ge(w_loaded[0], 48)
            for part in range(2):
                last = project(0, part, range(KT))
            last.then_inc(projected, 1)
            for g in range(WG - 1):
                with pe.Fori(0, NP // 2) as i:
                    pair(g, i * 2, 0, weights_landed(1, i + (g * 2 + 1)))
                    pair(g, i * 2 + 1, 1, weights_landed(0, i + (g * 2 + 2)))
            g = WG - 1
            pair(g, 0, 0, weights_landed(1, 2 * g + 1))
            pair(g, 1, 1, weights_landed(0, 2 * g + 2))
            pair(g, 2, 0, weights_landed(1, 2 * g + 2))
            pair(g, 3, 1, None)

        @block.scalar
        def _(act):
            act.sem_inc(exped, 2)
            act.sem_inc(turned_copied, 2)
            act.wait_ge(cleared, 1)

            def pair(g, n, s):
                m = n + NP * g
                dil = DILATIONS[g]
                act.wait_ge(projected, m + 1)
                for part in range(2):
                    nc.scalar.activation(square[:, part, :], c.ps[:, part, :], ACT.Square).then_inc(squared, 1)
                act.wait_ge(summed, m * 2 + 1)
                nc.scalar.activation(root[:, 0, :], c.ps[:, 3, :], ACT.Sqrt, bias=eps64[:, :]).then_inc(rooted, 1)
                act.wait_ge(summed, m * 2 + 2)
                nc.scalar.activation(root[:, 1, :], c.ps[:, 4, :], ACT.Sqrt, bias=c.eps[:, :], scale=1.0 / WD).then_inc(rooted, 1)
                act.wait_ge(v_projected, m + 3)
                act.wait_ge(v_turned, m + 1)
                nc.scalar.activation(by_class(v[:, :], dil), by_token(c.ps[:, 2, :], dil), ACT.Copy).then_inc(v_copied, 1)
                act.wait_ge(v_turned, m + 2)
                nc.scalar.activation(v_rows[:, :, :], c.ps[:, 5, :].rearrange("p (t n) -> p t n", t=TT), ACT.Copy).then_inc(v_ready, 1)
                us = units(g)
                for t in range(NU + 1):
                    if t < NU:
                        nk = us[t][3]
                        col = n * NU + (g * NP * NU + t)
                        act.wait_ge(maxed, m * NU + t + 1)
                        act.wait_ge(turned, m * NU + t + 1)
                        nc.scalar.activation(probs[:, t % 2, 0:nk * P], c.ps[:, 6 + t % 2, 0:nk * P], ACT.Exp,
                                             bias=neg_max[:, ds(col, 1)], accum_out=sums[:, ds(col, 1)]).then_inc(exped, 1)
                    if t >= 1:
                        u = t - 1
                        nk = us[u][3]
                        act.wait_ge(turned, m * NU + u + 3)
                        act.wait_ge(attended, m * NU + u + 1)
                        nc.scalar.activation(probs_t[:, u % 2, 0:nk, :],
                                             c.ps[:, 3 + u % 2, 0:nk * P].rearrange("p (j n) -> p j n", j=nk),
                                             ACT.Copy).then_inc(turned_copied, 1)
            pairs(act, pair)

        @block.vector
        def _(dve):
            dve.sem_inc(o_copied, 1)

            def pair(g, n, s):
                m = n + NP * g
                dil = DILATIONS[g]
                for part, (name, to) in enumerate((("dsw_q_norm", q), ("dsw_k_norm", k))):
                    gain = c.column(name)
                    dve.wait_ge(rooted, m * 2 + part + 1)
                    nc.vector.reciprocal(root[:, part, :], root[:, part, :]).then_inc(inverted, 1)
                    dve.wait_ge(inverted, m * 2 + part + 1)
                    nc.vector.scalar_tensor_tensor(by_class(to[:, :], dil), by_token(c.ps[:, part, :], dil),
                                                   c.vec[:, gain:gain + 1], by_token(root[:, part, :], dil),
                                                   ALU.mult, ALU.mult).then_inc(normed, 1)
                us = units(g)
                for t in range(NU + 1):
                    if t < NU:
                        a, b, kb, nk = us[t]
                        col = n * NU + (g * NP * NU + t)
                        dve.wait_ge(scored, m * NU + t + 1)
                        nc.vector.tensor_tensor(c.ps[:, 6 + t % 2, 0:nk * P], c.ps[:, 6 + t % 2, 0:nk * P],
                                                biases[:, ds(n * 2 + a, 1), g + 2 - nk:g + 2, :].rearrange("p h j n -> p (h j n)"),
                                                ALU.add).then_inc(biased, 1)
                        dve.wait_ge(biased, m * NU + t + 1)
                        nc.vector.tensor_reduce(neg_max[:, ds(col, 1)], c.ps[:, 6 + t % 2, 0:nk * P], AX.X, ALU.max,
                                                negate=True).then_inc(maxed, 1)
                    if t >= 1:
                        u = t - 1
                        nk = us[u][3]
                        col = n * NU + (g * NP * NU + u)
                        dve.wait_ge(exped, m * NU + u + 3)
                        nc.vector.reciprocal(inverse[:, u % 2:u % 2 + 1], sums[:, ds(col, 1)]).then_inc(inverse_ready, 1)
                        dve.wait_ge(inverse_ready, m * NU + u + 1)
                        nc.vector.tensor_scalar(probs[:, u % 2, 0:nk * P], probs[:, u % 2, 0:nk * P],
                                                inverse[:, u % 2:u % 2 + 1], None, ALU.mult).then_inc(weighed, 1)
                dve.wait_ge(attended, m * NU + NU + 2)
                nc.vector.tensor_copy(by_token(o_groups[:, ds(n + NP * g, 1), :].rearrange("p a t -> p (a t)"), dil),
                                      by_class(c.ps[:, 5, :], dil)).then_inc(o_copied, 1)

            pairs(dve, pair)


def window_combine(c, o_groups, neg_max, sums, o):
    nc = c.nc
    with c.stage(lse=[P, WG, WH, TT], rows=[WH, WG, S], top=[WH, S], total=[WH, S], pairsel=[WH, 4, P],
                 part=[P, 2, S]) as (block, sems, lse, rows, top, total, pairsel, part):
        consts, log_ready, lse_ready, turned, copied, act_link, dve_link, exped, weighed, spread, scaled = sems[:11]

        @block.sync
        def _(sp):
            sp.dma_start(pairsel[:, :, :], c.const("pairsel", WH).rearrange("h (j n) -> h j n", j=4)).then_inc(consts, 16)

        @block.scalar
        def _(act):
            nc.scalar.activation(lse[:, :, :, :], sums[:, :].rearrange("p (g h b) -> p g h b", g=WG, h=WH), ACT.Ln).then_inc(log_ready, 1)
            for g in range(WG):
                act.wait_ge(lse_ready, 2 + g)
                nc.scalar.activation(rows[:, g, :], rows[:, g, :], ACT.Exp).then_inc(exped, 1)

        @block.tensor
        def _(pe):
            pe.wait_ge(lse_ready, 1)
            for g in range(WG):
                for b in range(TT):
                    last = nc.tensor.transpose(c.ps[0:WH, g, b * P:(b + 1) * P], lse[:, g, :, b], c.ident[:, :])
                last.then_inc(turned, 1)
            pe.wait_ge(consts, 16)
            pe.wait_ge(weighed, WG)
            n = 0
            for pair in range(4):
                for g in range(WG):
                    if n >= 4:
                        pe.wait_ge(scaled, n - 3)
                    nc.tensor.matmul(c.ps[:, 3 + n % 4, :], pairsel[:, pair, :], rows[:, g, :], start=True, stop=True).then_inc(spread, 1)
                    n += 1

        @block.vector
        def _(dve):
            link = Links(dve, dve_link)
            dve.wait_ge(log_ready, 1)
            nc.vector.tensor_tensor(lse[:, :, :, :], lse[:, :, :, :], neg_max[:, :].rearrange("p (g h b) -> p g h b", g=WG, h=WH),
                                    ALU.subtract).then_inc(lse_ready, 1)
            for g in range(WG):
                dve.wait_ge(turned, g + 1)
                ins = nc.vector.tensor_copy(by_token(rows[:, g, :], DILATIONS[g]), by_class(c.ps[0:WH, g, :], DILATIONS[g]))
                link.do(ins)
            link.do(nc.vector.tensor_tensor(top[:, :], rows[:, 0, :], rows[:, 1, :], ALU.max))
            link.do(nc.vector.tensor_tensor(top[:, :], top[:, :], rows[:, 2, :], ALU.max))
            for g in range(WG):
                nc.vector.tensor_tensor(rows[:, g, :], rows[:, g, :], top[:, :], ALU.subtract).then_inc(lse_ready, 1)
            dve.wait_ge(exped, WG)
            link.do(nc.vector.tensor_tensor(total[:, :], rows[:, 0, :], rows[:, 1, :], ALU.add))
            link.do(nc.vector.tensor_tensor(total[:, :], total[:, :], rows[:, 2, :], ALU.add))
            link.do(nc.vector.reciprocal(total[:, :], total[:, :]))
            for g in range(WG):
                nc.vector.tensor_tensor(rows[:, g, :], rows[:, g, :], total[:, :], ALU.mult).then_inc(weighed, 1)
            n = 0
            for pair in range(4):
                for g in range(WG):
                    dve.wait_ge(spread, n + 1)
                    if g == 0:
                        nc.vector.tensor_tensor(o[:, pair, :], o_groups[:, pair, :], c.ps[:, 3 + n % 4, :], ALU.mult).then_inc(scaled, 1)
                    else:
                        nc.vector.tensor_tensor(part[:, g - 1, :], o_groups[:, g * 4 + pair, :], c.ps[:, 3 + n % 4, :], ALU.mult).then_inc(scaled, 1)
                        dve.wait_ge(scaled, n + 1)
                        link.do(nc.vector.tensor_tensor(o[:, pair, :], o[:, pair, :], part[:, g - 1, :], ALU.add))
                    n += 1


def dilated_attention(c, layer):
    nc = c.nc
    scratch = nc.dram_tensor("bias_rows", (4, WH, 256), F32, kind="Internal").ap()
    with ExitStack() as ctx:
        sb = lambda name, shape: ctx.enter_context(nc.sbuf_tensor(name, shape, F32))
        o_groups, o = sb("o_groups", [P, WG * 4, S]), sb("o_windows", [P, 4, S])
        neg_max, sums = sb("neg_max", [P, WG * 32]), sb("sums", [P, WG * 32])
        with nc.sbuf_tensor("biases", [P, WH, 4, P], F32) as biases:
            window_biases(c, scratch, biases)
            window_attention(c, biases, o_groups, neg_max, sums)
        window_combine(c, o_groups, neg_max, sums, o)
        project_out(c, c.ins["dsw_w_out"][0, :, :], WHG // P, lambda k: o[:, k, :], add_gated(c, layer, 2))


def layer_columns(w, layer, n0, n):
    return w.rearrange("l (k p) n -> p l k n", p=P)[:, ds(layer, 1), :, ds(n0, n)].rearrange("p l k n -> p (l k) n")


def layer_gain(c, name, layer):
    at = c.column(name)
    return lambda k: c.vec[:, ds(layer * KT + (at + k), 1)]


Q_A, KV_A, GATE_A, Q_D, KV_D, IN_B, IN_C = 0, 512, 1280, 1304, 1816, 2072, 3096


def nsa_gates(c, layer, gates):
    nc = c.nc
    n = 24
    with c.stage(w=[P, KT, n], rows=[n, S]) as (block, sems, w, rows):
        loaded, done, squashed, turned = sems[:4]

        @block.sync
        def _(sp):
            sp.dma_start(w[:, :, :], layer_columns(c.ins["w_in_2"], layer, GATE_A, n)).then_inc(loaded, 16)

        @block.tensor
        def _(pe):
            pe.wait_ge(loaded, 16)
            for k in range(KT):
                last = nc.tensor.matmul(c.ps[0:n, 0, :], w[:, k, :], c.h[:, k, :], start=(k == 0), stop=(k == KT - 1))
            last.then_inc(done, 1)
            pe.wait_ge(squashed, 1)
            for t in range(TT):
                last = nc.tensor.transpose(c.ps[:, 1, t * n:(t + 1) * n], rows[:, t * P:(t + 1) * P], c.ident[0:n, 0:n])
            last.then_inc(turned, 1)

        @block.scalar
        def _(act):
            act.wait_ge(done, 1)
            nc.scalar.activation(rows[:, :], c.ps[0:n, 0, :], ACT.Sigmoid).then_inc(squashed, 1)

        @block.vector
        def _(dve):
            dve.wait_ge(turned, 1)
            nc.vector.tensor_copy(gates[:, :, :], c.ps[:, 1, 0:TT * n].rearrange("p (t n) -> p t n", t=TT))


def attend(c, layer, gates, o_nsa, o_swa):
    nc, w_in = c.nc, c.ins["w_in_2"]
    GROUPS = 2
    KC, KS, KW, VSW, KD, VD, QA0, QA1, QD0, QD1 = range(10)
    STEPS = ((KC, KS, KW), (VSW, KD, VD), (QA0, QA1), (QD0, QD1))
    HALVES = {KC: (KV_A, KV_A + 128), KS: (KV_A + 256,) * 2, KW: (KV_A + 512,) * 2, VSW: (KV_A + 384, KV_A + 640),
              KD: (KV_D,) * 2, VD: (KV_D + 128,) * 2}
    WIDE = {QA0: Q_A, QA1: Q_A + P, QD0: Q_D, QD1: Q_D + P}
    DMAS = [sum(2 if t in HALVES else 1 for t in step) for step in STEPS]
    BANK_OF = {KC: 0, KS: 1, KW: 2, VSW: 3, KD: 4, VD: 5, QA0: 6, QA1: 7, QD0: 0, QD1: 1}
    ROPED = (KS, KW, KD, QA0, QA1, QD0, QD1)
    CMP, SLC, WIN, SWA = range(4)
    rounds = [(NCMP, [(CMP, pr, qt) for qt in range(TT)]) for pr in range(2)]
    rounds += [(P, [(br, pr, 0) for br in (SLC, WIN) for pr in range(2)])]
    rounds += [(2 * P, [(br, pr, 1) for pr in range(2)]) for br in (SLC, WIN)]
    rounds += [((qt + 1) * P, [(br, pr, qt)]) for qt in (2, 3) for br in (SLC, WIN) for pr in range(2)]
    NSA_ROUNDS = len(rounds)
    rounds += [(min(qt + 1, 2) * P, [(SWA, pr, qt) for pr in range(2)]) for qt in range(TT)]
    NR, NSWA = len(rounds), TT
    RING = 3
    assert all(w * len(tiles) <= S for w, tiles in rounds)

    def first_key_tile(br, qt):
        return max(qt - 1, 0) if br == SWA else 0

    def key_tiles(w):
        return -(-w // P)

    with c.stage(w1=[P, CMP_LEN, CMP_HID], w2=[P, 2, 2, 64], rope=[P, 2, S], swap=[P, P], band=[P, 2 * P],
                 cmpadd=[P, TT * NCMP], cmpmul=[P, TT * NCMP], sinks=[P, DEPTH * 8], minus_sinks=[P, DEPTH * 8],
                 raw=[P, 10, S], turned_q=[P, 7, S], cross=[P, 2, S], blocks=[P, CMP_LEN, NCMP],
                 hidden=[P, 2, 2, NCMP], k_cmp=[P, NCMP], v_cmp=[NCMP, 64], v_rows=[P, 2, TT, P],
                 probs=[P, RING, 2, S], probs_t=[P, 2, 2, TT, P], stats=[P, 4, RING, 2, TT]) as (
            block, sems, w1, w2, rope, swap, band, cmpadd, cmpmul, sinks, minus_sinks, raw, roped, cross, blocks,
            hidden, k_cmp, v_cmp, v_rows, probs, probs_t, stats):
        (w0_loaded, w1_loaded, consts, projected, copied, swapped, crossed, turned_with_cos, rotated, v_turned, v_ready,
         blocks_ready, hid_done, hid_ready, cmp_done, cmp_ready, scored, masked, topped, maxed, exped, sink_ready,
         summed, inverse_ready, weighed, turned, turned_copied, attended, o_copied, sink_negated, whole_seen) = sems[:31]
        loaded = (w0_loaded, w1_loaded)
        CONSTS = 16 * 11
        FIRST = (16 * DMAS[0], 16 * DMAS[1])
        ROUND = (16 * (DMAS[0] + DMAS[2]), 16 * (DMAS[1] + DMAS[3]))

        @block.sync
        def _(sp):
            def load(g, j):
                sp.wait_ge(projected, g * 4 + (j + 1))
                for i, t in enumerate(STEPS[j]):
                    tile = c.slots[j % 2][:, i * D:(i + 1) * D].rearrange("p (k n) -> p k n", k=KT)
                    if t in HALVES:
                        for half, n0 in enumerate(HALVES[t]):
                            sp.dma_start(tile[:, :, 64 * half:64 * half + 64],
                                         layer_columns(w_in, layer, g * 64 + n0, 64)).then_inc(loaded[j % 2], 16)
                    else:
                        sp.dma_start(tile, layer_columns(w_in, layer, g * 256 + WIDE[t], P)).then_inc(loaded[j % 2], 16)

            with sp.Fori(0, GROUPS) as g:
                for j in range(4):
                    load(g, j)

        @block.gpsimd
        def _(pool):
            pool.wait_ge(consts, CONSTS)
            with pool.Fori(0, GROUPS) as g:
                for i, t in enumerate(ROPED):
                    pool.wait_ge(copied, g * 10 + (t + 1))
                    if i == 0:
                        pool.wait_ge(o_copied, g * 4 + 1)
                    nc.gpsimd.tensor_tensor(roped[:, i, :], raw[:, t, :], rope[:, 0, :], ALU.mult).then_inc(turned_with_cos, 1)

        @block.tensor
        def _(pe):
            pe.sem_inc(projected, 2)
            pe.sem_inc(turned, RING)
            pe.sem_inc(attended, 2)
            with pe.Fori(0, GROUPS) as g:
                for j, step in enumerate(STEPS):
                    pe.wait_ge(loaded[j % 2], g * ROUND[j % 2] + (FIRST[j % 2] if j < 2 else ROUND[j % 2]))
                    if j == 0:
                        pe.wait_ge(o_copied, g * 4 + 1)
                    if j == 3:
                        pe.wait_ge(copied, g * 10 + 2)
                    for i, t in enumerate(step):
                        for k in range(KT):
                            last = nc.tensor.matmul(c.ps[:, BANK_OF[t], :], c.slots[j % 2][:, (i * KT + k) * P:(i * KT + k + 1) * P],
                                                    c.h[:, k, :], start=(k == 0), stop=(k == KT - 1))
                    last.then_inc(projected, 1)
                pe.wait_ge(consts, CONSTS)
                for i, t in enumerate(ROPED):
                    pe.wait_ge(copied, g * 10 + (max(t, VSW) + 1))
                    if i >= 2:
                        pe.wait_ge(crossed, g * 7 + (i - 1))
                    nc.tensor.matmul(c.ps[:, 2 + i % 2, :], swap[:, :], raw[:, t, :], start=True, stop=True).then_inc(swapped, 1)
                for i, t in enumerate((VSW, VD)):
                    pe.wait_ge(copied, g * 10 + 6)
                    for tt in range(TT):
                        last = nc.tensor.transpose(c.ps[:, 4 + i, tt * P:(tt + 1) * P], raw[:, t, tt * P:(tt + 1) * P], c.ident[:, :])
                    last.then_inc(v_turned, 1)
                pe.wait_ge(blocks_ready, g + 1)
                pe.wait_ge(copied, g * 10 + 10)
                for kv in range(2):
                    r = slice(64 * kv, 64 * kv + 64)
                    for half in range(2):
                        col = half * 32
                        for pos in range(CMP_LEN):
                            last = nc.tensor.matmul(c.ps[:, 6 + kv, col:col + NCMP], w1[r, pos, half * P:(half + 1) * P],
                                                    blocks[r, pos, :], start=(pos == 0), stop=(pos == CMP_LEN - 1))
                last.then_inc(hid_done, 1)
                pe.wait_ge(hid_ready, g + 1)
                for r in range(2):
                    for half in range(2):
                        nc.tensor.matmul(c.ps[64 * r:64 * r + 64, 0, 0:NCMP], w2[:, 0, half, :], hidden[:, 0, half, :],
                                         start=(half == 0), stop=(half == 1))
                for half in range(2):
                    last = nc.tensor.matmul(c.ps[0:NCMP, 0, 64:128], hidden[:, 1, half, :], w2[:, 1, half, :],
                                            start=(half == 0), stop=(half == 1))
                last.then_inc(cmp_done, 1)
                pe.wait_ge(cmp_ready, g + 1)
                pe.wait_ge(rotated, g * 7 + 7)
                pe.wait_ge(v_ready, g * 2 + 2)
                for t in range(NR + 3):
                    if t < NR:
                        w, tiles = rounds[t]
                        pe.wait_ge(turned_copied, g * NR + (t + 1))
                        for a in range(2):
                            h = slice(64 * a, 64 * a + 64)
                            for i, (br, pr, qt) in enumerate(tiles):
                                q_at, k0 = slice(qt * P, (qt + 1) * P), first_key_tile(br, qt) * P
                                if br == CMP:
                                    q, k = raw[h, QA0 + pr, q_at], k_cmp[h, :]
                                else:
                                    q = roped[h, (5 if br == SWA else 3) + pr, q_at]
                                    k = roped[h, {SLC: 0, WIN: 1, SWA: 2}[br], k0:k0 + w]
                                last = nc.tensor.matmul(c.ps[:, 2 * (t % RING) + a, i * w:(i + 1) * w], q, k, start=True, stop=True)
                        last.then_inc(scored, 1)
                    if 2 <= t <= NR + 1:
                        u = t - 2
                        w, tiles = rounds[u]
                        pe.wait_ge(weighed, g * NR + (u + 1))
                        for a in range(2):
                            for i in range(len(tiles)):
                                for j in range(key_tiles(w)):
                                    m, at = min(P, w), (i * key_tiles(w) + j) * P
                                    last = nc.tensor.transpose(c.ps[0:m, 2 * (u % RING) + a, at:at + P],
                                                               probs[:, u % RING, a, i * w + j * P:i * w + j * P + m], c.ident[:, :])
                        last.then_inc(turned, 1)
                    if t >= 3:
                        u = t - 3
                        w, tiles = rounds[u]
                        nk = key_tiles(w)
                        pe.wait_ge(turned_copied, g * NR + (u + 1 + RING))
                        if u == NSA_ROUNDS:
                            pe.wait_ge(o_copied, g * 4 + 3)
                        for a in range(2):
                            h = slice(64 * a, 64 * a + 64)
                            if tiles[0][0] == CMP:
                                last = nc.tensor.matmul(c.ps[h, 6 + tiles[0][1], :], v_cmp[:, :],
                                                        probs_t[0:NCMP, u % 2, a, :, :].rearrange("p t n -> p (t n)"),
                                                        start=True, stop=False)
                                continue
                            for i, (br, pr, qt) in enumerate(tiles):
                                for j in range(nk):
                                    v_at = 64 if br == WIN else 0
                                    last = nc.tensor.matmul(c.ps[h, 6 + pr, qt * P:(qt + 1) * P],
                                                            v_rows[:, br == SWA, first_key_tile(br, qt) + j, v_at:v_at + 64],
                                                            probs_t[:, u % 2, a, i * nk + j, :],
                                                            start=(j == 0 and br == SWA),
                                                            stop=(j == nk - 1 and (br == SWA or (br, qt) == (WIN, TT - 1))))
                        last.then_inc(attended, 1)

        @block.scalar
        def _(act):
            def const(dst, src):
                act.dma_start(dst, src).then_inc(consts, 16)
            const(rope[:, 0, :], c.const("cos"))
            const(rope[:, 1, :], c.const("sin"))
            const(swap[:, :], c.const("swap"))
            const(band[:, :], c.const("band"))
            const(cmpadd[:, :], c.const("cmpadd"))
            const(cmpmul[:, :], c.const("cmpmul"))
            const(sinks[:, :], c.ins["swa_sinks_2"].rearrange("l h -> (l h)").partition_broadcast(P))
            for kv in range(2):
                const(w1[64 * kv:64 * kv + 64, :, :],
                      c.ins["nsa_cmp_w1_2"].rearrange("a v (l d) n -> d a v l n", d=64)[:, ds(layer, 1), kv, :, :]
                      .rearrange("d a l n -> d (a l) n"))
                const(w2[:, kv, :, :],
                      c.ins["nsa_cmp_w2_2"].rearrange("a v (f p) n -> p a v f n", p=P)[:, ds(layer, 1), kv, :, :]
                      .rearrange("p a f n -> p (a f) n"))
            act.sem_inc(turned_copied, RING)
            act.sem_inc(o_copied, 1)
            act.wait_ge(consts, CONSTS)
            nc.scalar.activation(minus_sinks[:, :], sinks[:, :], ACT.Copy, scale=-1.0).then_inc(sink_negated, 1)
            with act.Fori(0, GROUPS) as g:
                for j, step in enumerate(STEPS):
                    act.wait_ge(projected, g * 4 + (j + 3))
                    for t in step:
                        nc.scalar.activation(raw[:, t, :], c.ps[:, BANK_OF[t], :], ACT.Copy,
                                             scale=(0.125 if t >= QA0 else 1.0)).then_inc(copied, 1)
                for i in range(2):
                    act.wait_ge(v_turned, g * 2 + (i + 1))
                    nc.scalar.activation(v_rows[:, i, :, :], c.ps[:, 4 + i, :].rearrange("p (t n) -> p t n", t=TT),
                                         ACT.Copy).then_inc(v_ready, 1)
                act.wait_ge(hid_done, g + 1)
                nc.scalar.activation(hidden[:, :, :, :], c.ps[:, 6:8, 0:64].rearrange("p b (j n) -> p b j n", j=2)[:, :, :, 0:NCMP],
                                     ACT.Gelu_apprx_tanh).then_inc(hid_ready, 1)
                def copy_sums(o):
                    for pr in range(2):
                        nc.scalar.activation(o[:, ds(g * 2 + pr, 1), :], c.ps[:, 6 + pr, :], ACT.Copy).then_inc(o_copied, 1)

                for t in range(NR + 2):
                    if t < NR:
                        w, tiles = rounds[t]
                        act.wait_ge(maxed, g * NR + (t + 1))
                        act.wait_ge(turned, g * NR + (t + 1))
                        for a in range(2):
                            for i in range(len(tiles)):
                                st = stats[:, :, t % RING, a, i:i + 1]
                                last = nc.scalar.activation(probs[:, t % RING, a, i * w:(i + 1) * w],
                                                            c.ps[:, 2 * (t % RING) + a, i * w:(i + 1) * w], ACT.Exp,
                                                            bias=st[:, 0, :], accum_out=st[:, 1, :])
                        last.then_inc(exped, 1)
                        if t >= NSA_ROUNDS:
                            rest = stats[:, 3, t % RING, :, 0:2]
                            nc.scalar.activation(rest, rest, ACT.Exp).then_inc(sink_ready, 1)
                    if t >= 2:
                        u = t - 2
                        w, tiles = rounds[u]
                        rows, n, at = min(w, P), len(tiles) * key_tiles(w), 2 * (u % RING)
                        act.wait_ge(turned, g * NR + (u + 1 + RING))
                        act.wait_ge(attended, g * NR + (u + 1))
                        nc.scalar.activation(probs_t[0:rows, u % 2, :, 0:n, :],
                                             c.ps[0:rows, at:at + 2, 0:n * P].rearrange("p a (j n) -> p a j n", j=n),
                                             ACT.Copy).then_inc(turned_copied, 1)
                    if t == NSA_ROUNDS + 2:
                        act.wait_ge(attended, g * NR + (NSA_ROUNDS + 2))
                        copy_sums(o_nsa)
                act.wait_ge(attended, g * NR + (NR + 2))
                copy_sums(o_swa)

        @block.vector
        def _(dve):
            pos_at = c.column("cmp_pos0")
            assert c.column("cmp_pos1") == pos_at + CMP_LEN
            dve.wait_ge(consts, CONSTS)
            dve.wait_ge(sink_negated, 1)
            with dve.Fori(0, GROUPS) as g:
                dve.wait_ge(copied, g * 10 + 1)
                line = raw[:, KC, :]
                strided = bass.AP(tensor=line.tensor, offset=line.offset, ap=[list(line.ap[0]), [1, CMP_LEN], [CMP_STRIDE, NCMP]])
                nc.vector.tensor_tensor(blocks[:, :, :], strided,
                                        c.vec[:, ds(layer * CMP_LEN + pos_at, CMP_LEN)].unsqueeze(2).to_broadcast([P, CMP_LEN, NCMP]),
                                        ALU.add).then_inc(blocks_ready, 1)
                for i in range(7):
                    dve.wait_ge(swapped, g * 7 + (i + 1))
                    if i >= 2:
                        dve.wait_ge(rotated, g * 7 + (i - 1))
                    nc.vector.tensor_tensor(cross[:, i % 2, :], c.ps[:, 2 + i % 2, :], rope[:, 1, :], ALU.mult).then_inc(crossed, 1)
                    dve.wait_ge(crossed, g * 7 + (i + 1))
                    dve.wait_ge(turned_with_cos, g * 7 + (i + 1))
                    nc.vector.tensor_tensor(roped[:, i, :], roped[:, i, :], cross[:, i % 2, :], ALU.add).then_inc(rotated, 1)
                dve.wait_ge(cmp_done, g + 1)
                nc.vector.tensor_copy(k_cmp[:, :], c.ps[:, 0, 0:NCMP])
                nc.vector.tensor_copy(v_cmp[:, :], c.ps[0:NCMP, 0, 64:128]).then_inc(cmp_ready, 1)
                def group_sinks(of):
                    return of[:, ds(layer * 8 + g * 4, 4)].rearrange("p (r a) -> p a r", a=2)

                for t in range(NR + 1):
                    if t < NR:
                        w, tiles = rounds[t]
                        n, br = len(tiles), tiles[0][0]
                        st = stats[:, :, t % RING, :, 0:n]
                        scores = c.ps[:, 2 * (t % RING):2 * (t % RING) + 2, 0:n * w].rearrange("p a (i w) -> p a i w", i=n)
                        if br == CMP:
                            part, mask = scores, cmpadd[:, :].rearrange("p (t w) -> p t w", t=TT).unsqueeze(1)
                        elif br == SWA:
                            part, mask = scores, band[:, 2 * P - w:2 * P].unsqueeze(1).unsqueeze(1)
                        else:
                            part, mask = scores[:, :, :, w - P:w], band[:, P:2 * P].unsqueeze(1).unsqueeze(1)
                        dve.wait_ge(scored, g * NR + (t + 1))
                        nc.vector.tensor_tensor(part, part, mask.to_broadcast(list(part.shape)), ALU.add).then_inc(masked, 1)
                        dve.wait_ge(masked, g * NR + (t + 1))
                        top = nc.vector.tensor_reduce(st[:, 0, :, :], scores, AX.X, ALU.max, negate=True)
                        if br == SWA:
                            top.then_inc(topped, 1)
                            dve.wait_ge(topped, g * (2 * NSWA) + (2 * (t - NSA_ROUNDS) + 1))
                            nc.vector.tensor_tensor(st[:, 0, :, :], st[:, 0, :, :], group_sinks(minus_sinks), ALU.min).then_inc(topped, 1)
                            dve.wait_ge(topped, g * (2 * NSWA) + (2 * (t - NSA_ROUNDS) + 2))
                            top = nc.vector.tensor_tensor(st[:, 3, :, :], st[:, 0, :, :], group_sinks(sinks), ALU.add)
                        top.then_inc(maxed, 1)
                    if t >= 1:
                        u = t - 1
                        w, tiles = rounds[u]
                        n, br = len(tiles), tiles[0][0]
                        st = stats[:, :, u % RING, :, 0:n]
                        dve.wait_ge(exped, g * NR + (u + 1))
                        if br == SWA:
                            dve.wait_ge(sink_ready, g * NSWA + (u - NSA_ROUNDS + 1))
                            nc.vector.tensor_tensor(st[:, 1, :, :], st[:, 1, :, :], st[:, 3, :, :], ALU.add).then_inc(summed, 1)
                            dve.wait_ge(summed, g * NSWA + (u - NSA_ROUNDS + 1))
                        nc.vector.reciprocal(st[:, 2, :, :], st[:, 1, :, :]).then_inc(inverse_ready, 1)
                        dve.wait_ge(inverse_ready, g * NR + (u + 1))
                        for a in range(2):
                            for i, (br, pr, qt) in enumerate(tiles):
                                p, inverse = probs[:, u % RING, a, i * w:(i + 1) * w], st[:, 2, a, i:i + 1]
                                if br == SWA:
                                    ins = nc.vector.tensor_scalar(p, p, inverse, None, ALU.mult)
                                else:
                                    gate = gates[:, qt, ds(g * 4 + (br * 8 + pr * 2 + a), 1)]
                                    ins = nc.vector.tensor_scalar(p, p, inverse, gate, ALU.mult, ALU.mult)
                        if br == CMP:
                            ins.then_inc(whole_seen, 1)
                            dve.wait_ge(whole_seen, g * 2 + (u + 1))
                            p = probs[:, u % RING, :, 0:NCMP]
                            ins = nc.vector.tensor_tensor(p, p, cmpmul[:, 0:NCMP].unsqueeze(1).to_broadcast([P, 2, NCMP]), ALU.mult)
                        ins.then_inc(weighed, 1)


def conv_pool_gates(c, layer, o_conv, o_pool, gates, pooled_in):
    nc, w_in, w_gate = c.nc, c.ins["w_in_2"], c.ins["w_gate_2"]
    CT = BW // P
    PAD, PPAD = CONVW - 1, POOLW[-1] - 1
    STEPS = CT + CT // 2 + 16
    with c.stage(padded=[P, CT, PAD + S], pool_in=[P, CT, PPAD + S], windows=[P, 2, PPAD + S], poolinv=[P, 64],
                 sig=[P, 2, S]) as (block, sems, padded, pool_in, windows, poolinv, sig):
        (load0, load1, consts, done, freed, zeroed, squashed, glued, tapped, pool_copied, pool_link, means_ready,
         pooled) = sems[:13]
        loaded = (load0, load1)

        @block.gpsimd
        def _(pool):
            nc.gpsimd.memset(padded[:, :, 0:PAD], 0.0).then_inc(zeroed, 1)
            nc.gpsimd.memset(pool_in[:, :, 0:PPAD], 0.0).then_inc(zeroed, 1)
            nc.gpsimd.memset(windows[:, :, :], 0.0).then_inc(zeroed, 1)
            pool.wait_ge(zeroed, 3)
            pool.wait_ge(consts, 16)
            pool.wait_ge(pool_copied, CT)
            link = Links(pool, pool_link)
            for j, wide in enumerate(POOLW):
                src, span, turn = pool_in[:, j, :], 1, 0
                while span < wide:
                    link.do(nc.gpsimd.tensor_tensor(windows[:, turn, span:], src[:, span:], src[:, 0:PPAD + S - span], ALU.add))
                    src, span, turn = windows[:, turn, :], span * 2, 1 - turn
                at = src[:, PPAD:]
                out = pooled_in[:, j, :]
                link.do(nc.gpsimd.tensor_tensor(out[:, 0:16], at[:, 0:16], poolinv[:, j * 16:(j + 1) * 16], ALU.mult))
                link.do(nc.gpsimd.tensor_scalar(out[:, 16:], at[:, 16:], 1.0 / wide, 1.0, ALU.mult, ALU.mult))
                link.do(nc.gpsimd.tensor_tensor(out, out, pool_in[:, j, PPAD:], ALU.subtract))
                if j < CT - 1:
                    link.do(nc.gpsimd.memset(windows[:, :, 0:PPAD], 0.0))

        @block.sync
        def _(sp):
            sp.dma_start(poolinv[:, :], c.const("poolinv")).then_inc(consts, 16)

            def tile(s, t):
                return c.slots[s][:, t * D:(t + 1) * D].rearrange("p (k n) -> p k n", k=KT)

            with sp.Fori(0, CT // 2) as i:
                for s in range(2):
                    sp.wait_ge(done, i * 2 + (s + 1))
                    for t in range(2):
                        sp.dma_start(tile(s, t), layer_columns(w_in, layer, i * (2 * P) + (s * P + IN_B + t * BW), P)).then_inc(loaded[s], 16)
            for s in range(2):
                sp.wait_ge(done, CT + s + 1)
                for t in range(2):
                    sp.dma_start(tile(s, t), layer_columns(w_in, layer, IN_C + (2 * s + t) * P, P)).then_inc(loaded[s], 16)
            with sp.Fori(0, 8) as i:
                for s in range(2):
                    sp.wait_ge(done, i * 2 + (s + CT + 2 + 1))
                    for t in range(2):
                        sp.dma_start(tile(s, t), layer_columns(w_gate, layer, i * (4 * P) + (2 * s + t) * P, P)).then_inc(loaded[s], 16)

        @block.tensor
        def _(pe):
            multiply_steps(pe, c, STEPS, 2, loaded, done, freed, 2, KT,
                           lambda slot, t, k: slot[:, (t * KT + k) * P:(t * KT + k + 1) * P], lambda k: c.h[:, k, :])

        @block.scalar
        def _(act):
            act.sem_inc(freed, 2)
            for n in range(CT):
                act.wait_ge(done, n + 3)
                if n >= 2:
                    act.wait_ge(glued, n - 1)
                nc.scalar.activation(sig[:, n % 2, :], c.ps[:, 4 * (n % 2) + 1, :], ACT.Sigmoid).then_inc(squashed, 1)
                act.wait_ge(glued, n + 1)
                act.sem_inc(freed, 1)
            act.wait_ge(zeroed, 3)
            for n in range(2):
                act.wait_ge(done, CT + n + 3)
                for t in range(2):
                    last = nc.scalar.activation(pool_in[:, 2 * n + t, PPAD:], c.ps[:, 4 * n + t, :], ACT.Copy)
                    last.then_inc(pool_copied, 1)
                act.wait_ge(pool_copied, 2 * n + 2)
                act.sem_inc(freed, 1)
            with act.Fori(0, 8) as i:
                for s in range(2):
                    act.wait_ge(done, i * 2 + (s + CT + 2 + 3))
                    for t in range(2):
                        last = nc.scalar.activation(gates[:, ds(i * 4 + (2 * s + t), 1), :], c.ps[:, 4 * s + t, :], ACT.Sigmoid)
                    last.then_inc(freed, 1)

        @block.vector
        def _(dve):
            dve.wait_ge(zeroed, 3)
            for n in range(CT):
                dve.wait_ge(squashed, n + 1)
                nc.vector.tensor_tensor(padded[:, n, PAD:], c.ps[:, 4 * (n % 2), :], sig[:, n % 2, :], ALU.mult).then_inc(glued, 1)
            dve.wait_ge(glued, CT)
            cw, cb = c.column("conv_w_2"), c.column("conv_b_2")
            for t in range(CT):
                nc.vector.tensor_scalar(o_conv[:, t, :], padded[:, t, 0:S], c.vec[:, ds(layer * (CONVW * CT) + (cw + t), 1)],
                                        c.vec[:, ds(layer * CT + (cb + t), 1)], ALU.mult, ALU.add).then_inc(tapped, 1)
            with dve.Fori(1, CONVW) as k:
                for t in range(CT):
                    dve.wait_ge(tapped, k * CT + (t - CT + 1))
                    nc.vector.scalar_tensor_tensor(o_conv[:, t, :], padded[:, t, ds(k, S)],
                                                   c.vec[:, ds(layer * (CONVW * CT) + k * CT + (cw + t), 1)], o_conv[:, t, :],
                                                   ALU.mult, ALU.add).then_inc(tapped, 1)


def conv_norm_pool_mix(c, layer, o_conv, o_pool, pooled_in):
    nc = c.nc
    CT = BW // P
    with c.stage(square=[P, CT, S], root=[P, S], w=[P, CT, P]) as (block, sems, square, root, w):
        loaded, mean_done, centred, squared, var_done, rooted, inverted, normed, mixed, act_link = sems[:10]

        @block.sync
        def _(sp):
            sp.dma_start(w[:, :, :], c.ins["pool_w_2"].rearrange("l g c d -> c l g d")[:, ds(layer, 1), :, :]
                         .rearrange("c l g d -> c (l g) d")).then_inc(loaded, 16)

        @block.tensor
        def _(pe):
            for t in range(CT):
                last = nc.tensor.matmul(c.ps[:, 0, :], c.ones[:, :], o_conv[:, t, :], start=(t == 0), stop=(t == CT - 1))
            last.then_inc(mean_done, 1)
            pe.wait_ge(loaded, 16)
            for t in range(CT):
                nc.tensor.matmul(c.ps[:, 2 + t, :], w[:, t, :], pooled_in[:, t, :], start=True, stop=True).then_inc(mixed, 1)
            for t in range(CT):
                pe.wait_ge(squared, t + 1)
                last = nc.tensor.matmul(c.ps[:, 1, :], c.ones[:, :], square[:, t, :], start=(t == 0), stop=(t == CT - 1))
            last.then_inc(var_done, 1)

        @block.vector
        def _(dve):
            dve.wait_ge(mean_done, 1)
            for t in range(CT):
                nc.vector.scalar_tensor_tensor(o_conv[:, t, :], c.ps[:, 0, :], -1.0 / BW, o_conv[:, t, :],
                                               ALU.mult, ALU.add).then_inc(centred, 1)
            dve.wait_ge(rooted, 1)
            nc.vector.reciprocal(root[:, :], root[:, :]).then_inc(inverted, 1)
            dve.wait_ge(inverted, 1)
            g = c.column("conv_ln_g_2")
            for t in range(CT):
                nc.vector.scalar_tensor_tensor(o_conv[:, t, :], o_conv[:, t, :], c.vec[:, ds(layer * CT + (g + t), 1)], root[:, :],
                                               ALU.mult, ALU.mult).then_inc(normed, 1)

        @block.scalar
        def _(act):
            for t in range(CT):
                act.wait_ge(centred, t + 1)
                nc.scalar.activation(square[:, t, :], o_conv[:, t, :], ACT.Square).then_inc(squared, 1)
            ps_at = c.column("pool_scale_2")
            for t in range(CT):
                act.wait_ge(mixed, t + 1)
                nc.scalar.activation(o_pool[:, t, :], c.ps[:, 2 + t, :], ACT.Copy, scale=c.vec[:, ds(layer * CT + (ps_at + t), 1)])
            act.wait_ge(var_done, 1)
            nc.scalar.activation(root[:, :], c.ps[:, 1, :], ACT.Sqrt, bias=c.eps[:, :], scale=1.0 / BW).then_inc(rooted, 1)
            b = c.column("conv_ln_b_2")
            for t in range(CT):
                act.wait_ge(normed, t + 1)
                nc.scalar.activation(o_conv[:, t, :], o_conv[:, t, :], ACT.Silu, bias=c.vec[:, ds(layer * CT + (b + t), 1)])


def merge_branches(c, layer, branches, gates):
    nc, w = c.nc, c.ins["w_branch_2"]
    NB, CT = 4, BW // P
    with c.stage(part=[P, 3, S]) as (block, sems, part):
        loaded, done, freed, gated, dve_link = sems[0:2], sems[2], sems[3], sems[4], sems[5]
        LINKS = 3

        @block.sync
        def _(sp):
            wv = w.rearrange("l b (k p) n -> p l (b k) n", p=P)
            stream_weights(sp, c, KT, lambda n, slot: [
                (slot[:, 0:NB * CT * P].rearrange("p (j n) -> p j n", n=P),
                 wv[:, ds(layer, 1), :, ds(n * P, P)].rearrange("p l j n -> p (l j) n"))], loaded, done)

        @block.tensor
        def _(pe):
            pe.sem_inc(done, 2)
            with pe.Fori(0, KT // 2) as i:
                for s in range(2):
                    pe.wait_ge(loaded[s], i * 16 + 16)
                    pe.wait_ge(freed, i * 2 + (s + 1))
                    for b in range(NB):
                        for k in range(CT):
                            last = nc.tensor.matmul(c.ps[:, 4 * s + b, :], c.slots[s][:, (b * CT + k) * P:(b * CT + k + 1) * P],
                                                    branches[b][:, k, :], start=(k == 0), stop=(k == CT - 1))
                    last.then_inc(done, 1)

        @block.vector
        def _(dve):
            dve.sem_inc(freed, 2)
            with dve.Fori(0, KT // 2) as i:
                for s in range(2):
                    n = i * 2 + s
                    dve.wait_ge(done, n + 3)
                    for b in range(1, NB):
                        nc.vector.tensor_tensor(part[:, b - 1, :], c.ps[:, 4 * s + b, :], gates[:, ds(n + b * KT, 1), :],
                                                ALU.mult).then_inc(gated, 1)
                    sum_ = gates[:, ds(n, 1), :]
                    nc.vector.tensor_tensor(sum_, c.ps[:, 4 * s, :], sum_, ALU.mult).then_inc(gated, 1)
                    link = Links(dve, dve_link, n * LINKS)
                    dve.wait_ge(gated, n * NB + NB)
                    for b in range(1, NB):
                        link.do(nc.vector.tensor_tensor(sum_, sum_, part[:, b - 1, :], ALU.add))
                    assert link.n == LINKS
                    dve.sem_inc(freed, 1)


def add_normed(c, gain):
    nc = c.nc
    with c.stage(square=[P, 2, S], root=[P, S]) as (block, sems, square, root):
        squared, turned, summed, rooted, inverted, scaled, added = sems[:7]

        @block.scalar
        def _(act):
            for k in range(KT):
                if k >= 2:
                    act.wait_ge(turned, k - 1)
                nc.scalar.activation(square[:, k % 2, :], c.h[:, k, :], ACT.Square).then_inc(squared, 1)
            act.wait_ge(turned, KT)
            nc.scalar.activation(root[:, :], c.ps[:, 0, :], ACT.Sqrt, bias=c.eps[:, :], scale=1.0 / D).then_inc(rooted, 1)

        @block.tensor
        def _(pe):
            for k in range(KT):
                pe.wait_ge(squared, k + 1)
                nc.tensor.matmul(c.ps[:, 0, :], c.ones[:, :], square[:, k % 2, :], start=(k == 0), stop=(k == KT - 1)).then_inc(turned, 1)

        @block.vector
        def _(dve):
            dve.wait_ge(rooted, 1)
            nc.vector.reciprocal(root[:, :], root[:, :]).then_inc(inverted, 1)
            dve.wait_ge(inverted, 1)
            for k in range(KT):
                nc.vector.scalar_tensor_tensor(c.h[:, k, :], c.h[:, k, :], gain(k), root[:, :], ALU.mult, ALU.mult).then_inc(scaled, 1)

        @block.gpsimd
        def _(pool):
            for k in range(KT):
                pool.wait_ge(scaled, k + 1)
                nc.gpsimd.tensor_tensor(c.x[:, k, :], c.x[:, k, :], c.h[:, k, :], ALU.add).then_inc(added, 1)
            pool.wait_ge(added, KT)


def conv_ffn(c, layer):
    nc = c.nc
    w_up, w_down = c.ins["ffn_w_up_2"], c.ins["ffn_w_down_2"]
    with c.nc.sbuf_tensor("conv_ffn_hidden", [P, FT, S], F32) as hidden:
        with c.stage(u=[P, 2, 2, S]) as (block, sems, u):
            loaded, done, freed, filtered, convolved, dve_link, gelued = sems[0:2], *sems[2:8]
            TAPS, LINKS = 3, 2
            cw, cb = c.column("ffn_conv_w_2"), c.column("ffn_conv_b_2")

            @block.sync
            def _(sp):
                def loads(n, slot):
                    v = slot[:, 0:2 * KT * P].rearrange("p (g k n) -> p g k n", g=2, k=KT)
                    return [(v[:, g, :, :], layer_columns(w_up, layer, n * P + g * F2, P)) for g in range(2)]
                stream_weights(sp, c, FT, loads, loaded, done)

            @block.tensor
            def _(pe):
                multiply_steps(pe, c, FT, 2, loaded, done, freed, 2, KT,
                               lambda slot, t, k: slot[:, (t * KT + k) * P:(t * KT + k + 1) * P], lambda k: c.h[:, k, :])

            @block.scalar
            def _(act):
                with act.Fori(0, FT // 2) as i:
                    for s in range(2):
                        n = i * 2 + s
                        act.wait_ge(done, n + 3)
                        act.wait_ge(freed, n + 1)
                        for t in range(2):
                            nc.scalar.activation(
                                u[:, s, t, :], c.ps[:, 4 * s + t, :], ACT.Identity,
                                bias=c.vec[:, ds(layer * (2 * FT) + n + (cb + t * FT), 1)],
                                scale=c.vec[:, ds(layer * (TAPS * 2 * FT) + n + (cw + 2 * 2 * FT + t * FT), 1)]).then_inc(filtered, 1)
                        act.wait_ge(convolved, n * 2 + 1)
                        nc.scalar.activation(u[:, s, 0, :], u[:, s, 0, :], ACT.Gelu_apprx_tanh).then_inc(gelued, 1)

            @block.vector
            def _(dve):
                dve.sem_inc(freed, 2)
                with dve.Fori(0, FT // 2) as i:
                    for s in range(2):
                        n = i * 2 + s
                        link = Links(dve, dve_link, n * LINKS)
                        for t in range(2):
                            dve.wait_ge(filtered, n * 2 + (t + 1))
                            for back in (1, 2):
                                ins = nc.vector.scalar_tensor_tensor(
                                    u[:, s, t, back:], c.ps[:, 4 * s + t, 0:S - back],
                                    c.vec[:, ds(layer * (TAPS * 2 * FT) + n + (cw + (2 - back) * 2 * FT + t * FT), 1)],
                                    u[:, s, t, back:], ALU.mult, ALU.add)
                                if back == 1:
                                    link.do(ins)
                                else:
                                    ins.then_inc(convolved, 1)
                        assert link.n == LINKS
                        dve.wait_ge(gelued, n + 1)
                        dve.wait_ge(convolved, n * 2 + 2)
                        nc.vector.tensor_tensor(hidden[:, ds(n, 1), :], u[:, s, 0, :], u[:, s, 1, :], ALU.mult).then_inc(freed, 1)

        def load_down(n):
            return layer_columns(w_down, layer, n * P, P)
        project_layer_out(c, load_down, FT, lambda k: hidden[:, k, :])


def project_layer_out(c, load, kt, moving):
    nc = c.nc
    with c.stage() as (block, sems):
        loaded, done, freed = sems[0:2], sems[2], sems[3]

        @block.sync
        def _(sp):
            stream_weights(sp, c, KT, lambda n, slot: [
                (slot[:, 0:kt * P].rearrange("p (k n) -> p k n", k=kt), load(n))], loaded, done)

        @block.tensor
        def _(pe):
            multiply_steps(pe, c, KT, 1, loaded, done, freed, 1, kt, lambda slot, t, k: slot[:, k * P:(k + 1) * P], moving)

        @block.vector
        def _(dve):
            dve.sem_inc(freed, 2)
            with dve.Fori(0, KT // 2) as i:
                for s in range(2):
                    dve.wait_ge(done, i * 2 + s + 3)
                    nc.vector.tensor_copy(c.h[:, ds(i * 2 + s, 1), :], c.ps[:, 4 * s, :]).then_inc(freed, 1)


def second_block(c):
    nc = c.nc
    before = c.turn
    with nc.Fori(0, DEPTH) as layer:
        norm(c, layer_gain(c, "norm_mix_pre_2", layer))
        with ExitStack() as ctx:
            sb = lambda name, shape: ctx.enter_context(nc.sbuf_tensor(name, shape, F32))
            o_nsa, o_swa = sb("o_nsa", [P, 4, S]), sb("o_swa", [P, 4, S])
            with nc.sbuf_tensor("nsa_gates", [P, TT, 24], F32) as nsa_gate:
                nsa_gates(c, layer, nsa_gate)
                attend(c, layer, nsa_gate, o_nsa, o_swa)
            o_conv, o_pool = sb("o_conv", [P, 4, S]), sb("o_pool", [P, 4, S])
            gates = sb("branch_gates", [P, 32, S])
            with nc.sbuf_tensor("pooled", [P, 4, S], F32) as pooled_in:
                conv_pool_gates(c, layer, o_conv, o_pool, gates, pooled_in)
                conv_norm_pool_mix(c, layer, o_conv, o_pool, pooled_in)
            merge_branches(c, layer, (o_nsa, o_conv, o_pool, o_swa), gates)
            project_layer_out(c, lambda n: layer_columns(c.ins["w_o_2"], layer, n * P, P), KT, lambda k: gates[:, k, :])
        add_normed(c, layer_gain(c, "norm_mix_post_2", layer))
        norm(c, layer_gain(c, "norm_ffn_pre_2", layer))
        conv_ffn(c, layer)
        add_normed(c, layer_gain(c, "norm_ffn_post_2", layer))
        if c.turn != before:
            with c.stage():
                pass


def build(nc, ins, out):
    with ExitStack() as ctx:
        c = Core(nc, ctx, ins, out)
        set_up(c)
        for layer, mixer in enumerate((gated_deltanet, dilated_attention)):
            norm(c, lambda k: c.gains[:, layer * 2 * KT + k:layer * 2 * KT + k + 1],
                 lambda k: c.mod[:, modulation(c, layer, 0) + k:modulation(c, layer, 0) + k + 1])
            mixer(c, layer)
            swiglu(c, layer)
        second_block(c)
        write_out(c)


def kernel(**inputs):
    import concourse.bacc as bacc
    from concourse.bass_utils import run_bass_kernel_spmd as run

    nc = bacc.Bacc("TRN2", target_bir_lowering=False, num_devices=1)
    arrays = {f"in_{k}": np.ascontiguousarray(v) for k, v in inputs.items()}
    arrays["in_constants"] = packed_constants()
    ins = {k[3:]: nc.dram_tensor(k, a.shape, F32, kind="ExternalInput").ap() for k, a in arrays.items()}
    out = nc.dram_tensor("out_x", (1, S, D), F32, kind="ExternalOutput").ap()
    build(nc, ins, out)
    return run(nc, [arrays], core_ids=[0]).results[0]["out_x"]
```

```python
import math
from contextlib import ExitStack, contextmanager

import numpy as np
import concourse.bass as bass
from concourse import mybir
from concourse.alu_op_type import AluOpType as ALU

F32 = mybir.dt.float32
ACT = mybir.ActivationFunctionType
AX = mybir.AxisListType
ds = bass.ds

P = 128
S = 512
D = 1024
KT = D // P
TT = S // P
EPS = 1e-6
NEG = -1e30
DEPTH = 2

GH, GDK, GCONV, GC = 8, 128, 4, 64
GHK = GH * GDK
GCH = 3 * GHK
NCH = S // GC
LEVELS = 6
WG, WH, WD = 3, 8, 64
WHG = WH * WD
DILATIONS = (1, 4, 16)
BUCKETS = 32
F1 = 2816
F2 = 2816
FT = F1 // P
BW = 512
IN2 = 3608
CMP_LEN, CMP_STRIDE, CMP_HID = 32, 16, 256
NCMP = (S - CMP_LEN) // CMP_STRIDE + 1
CONVW = 31
POOLW = (2, 4, 8, 16)

SLOT = 4096
BANK = 40


def bucket_of(dist):
    exact = BUCKETS // 2
    d = np.maximum(dist, 1).astype(np.float32)
    scaled = np.log(d / np.float32(exact)) / np.float32(math.log(2048 / exact))
    large = exact + (scaled * np.float32(BUCKETS - exact)).astype(np.int32)
    return np.where(dist < exact, dist, np.minimum(large, BUCKETS - 1))


def constant_tables():
    p = np.arange(P)
    row, col = p[:, None], p[None, :]
    t = {}
    t["ident"] = np.eye(P)
    t["ones"] = np.ones((P, P))
    t["halves"] = (row // 64 == col // 64) * 1.0
    levels = []
    for lv in range(LEVELS):
        same = (row >> (lv + 1)) == (col >> (lv + 1))
        levels.append(same & ((col >> lv) & 1 == 1) & ((row >> lv) & 1 == 0))
    t["levels"] = np.concatenate(levels, 1) * 1.0
    t["chunkmask"] = ((row // GC == col // GC) & (row <= col)) * 1.0
    t["resets"] = np.broadcast_to((np.arange(S) % GC != 0) * 1.0, (GH, S))
    t["hot8"] = np.eye(GH)
    hot = []
    for dil, off in ((1, 0), (4, 0), (16, 0), (1, P)):
        limit = 31 if dil == 16 else P
        dist = 127 - np.arange(256) + off
        valid = (dist >= 0) & (dist <= limit) & (np.arange(256) < 255)
        b = np.where(valid, bucket_of(np.maximum(dist, 0) * dil), BUCKETS)
        hot.append((np.arange(BUCKETS + 1)[:, None] == b[None, :]) * 1.0)
    t["buckets"] = np.concatenate(hot, 1)
    t["classmask"] = np.where(row // 32 == col // 32, 0.0, NEG)
    t["flip"] = np.eye(P)[::-1]
    pairs = [(np.arange(WH)[:, None] == 2 * j + col // 64) * 1.0 for j in range(4)]
    t["pairsel"] = np.concatenate(pairs, 1)
    inv = (1.0 / (np.float32(10000.0) ** (np.arange(0, 64, 2, dtype=np.float32) / np.float32(64)))).astype(np.float32)
    ang = np.arange(S, dtype=np.float32)[None, :] * inv[p % 32][:, None]
    t["cos"] = np.cos(ang)
    t["sin"] = np.sin(ang) * np.where(p % 64 < 32, -1.0, 1.0)[:, None]
    t["swap"] = ((row // 64 == col // 64) & ((row - col) % 64 == 32)) * 1.0
    t["band"] = np.concatenate([np.where(col > row, 0.0, NEG), np.where(col <= row, 0.0, NEG)], 1)
    end = np.arange(NCMP) * CMP_STRIDE + CMP_LEN - 1
    seen = [end[None, :] <= (i * P + row) for i in range(TT)]
    t["cmpadd"] = np.concatenate([np.where(m, 0.0, NEG) for m in seen], 1)
    t["cmpmul"] = np.concatenate(seen, 1) * 1.0
    t["poolinv"] = np.broadcast_to(
        np.concatenate([1.0 / np.minimum(np.arange(16) + 1, w) for w in POOLW]), (P, 64))
    return {k: np.ascontiguousarray(v, dtype=np.float32) for k, v in t.items()}


TABLES = constant_tables()
PLACES, CW = {}, 0
for _name, _t in TABLES.items():
    PLACES[_name] = CW
    CW += _t.shape[1]


def packed_constants():
    out = np.zeros((P, CW), np.float32)
    for name, t in TABLES.items():
        out[:t.shape[0], PLACES[name]:PLACES[name] + t.shape[1]] = t
    return out


class Links:

    def __init__(self, engine, sem, base=0):
        self.engine, self.sem, self.base, self.n = engine, sem, base, 0

    def do(self, instruction):
        self.n += 1
        instruction.then_inc(self.sem, 1)
        self.engine.wait_ge(self.sem, self.base + self.n)


class Core:

    def __init__(self, nc, ctx, ins, out):
        self.nc, self.ins, self.out = nc, ins, out
        self.turn = 0
        sb = lambda name, shape: ctx.enter_context(nc.sbuf_tensor(name, shape, F32))
        self.banks = [[ctx.enter_context(nc.semaphore(f"bank{b}_{i}")) for i in range(BANK)] for b in range(2)]
        self.x = sb("x_residual", [P, KT, S])
        self.h = sb("h_normed", [P, KT, S])
        self.slots = [sb(f"weight_slot{i}", [P, SLOT]) for i in range(2)]
        self.vec = sb("vectors", [P, 8 * P])
        self.mod = sb("modulation", [P, DEPTH * 48])
        self.gains = sb("modulated_gains", [P, DEPTH * 2 * KT])
        self.ident = sb("ident", [P, P])
        self.ones = sb("ones", [P, P])
        self.halves = sb("halves", [P, P])
        self.eps = sb("eps", [P, 1])
        self.ps = ctx.enter_context(nc.psum_tensor("psum", [P, 8, 512], F32))
        self.places = {}

    def const(self, name, rows=P):
        w = TABLES[name].shape[1]
        return self.ins["constants"][0:rows, PLACES[name]:PLACES[name] + w]

    def column(self, name, n=0):
        return self.places[name] + n

    @contextmanager
    def stage(self, **buffers):
        self.turn ^= 1
        bank, used = self.banks[self.turn], self.banks[1 - self.turn]
        numbers = [s.num for s in used]
        assert numbers == list(range(numbers[0], numbers[0] + BANK))
        with ExitStack() as ctx:
            made = [ctx.enter_context(self.nc.sbuf_tensor(f"{k}_{self.nc.next_id()}", list(v), F32))
                    for k, v in buffers.items()]
            block = ctx.enter_context(self.nc.Block(no_gpsimd_drain=True))

            @block.gpsimd
            def _(pool):
                pool.sem_clear(range(numbers[0], numbers[-1] + 1))

            yield (block, list(bank), *made)


def stream_weights(sp, c, steps, loads, loaded, done, first=0):
    with sp.Fori(0, steps // 2) as i:
        for s in range(2):
            sp.wait_ge(done, i * 2 + (first + s + 1))
            for dst, src in loads(i * 2 + s, c.slots[s]):
                sp.dma_start(dst, src).then_inc(loaded[s], 16)


def multiply_steps(pe, c, steps, dmas, loaded, done, freed, tiles, kt, weights, moving, ready=None, ready_from=0,
                   first=0, landed=0):
    if not first:
        pe.sem_inc(done, 2)
    with pe.Fori(0, steps // 2) as i:
        for s in range(2):
            pe.wait_ge(loaded[s], i * (16 * dmas) + (landed + 16 * dmas))
            pe.wait_ge(freed, i * 2 + (first + s + 1))
            for t in range(tiles):
                for k in range(kt):
                    if ready is not None and t == 0 and s == 0:
                        pe.wait_ge(ready, ready_from + k + 1)
                    last = c.nc.tensor.matmul(c.ps[:, 4 * s + t, :], weights(c.slots[s], t, k),
                                              moving(k), start=(k == 0), stop=(k == kt - 1))
            last.then_inc(done, 1)


def columns(w, n0, n):
    return w.rearrange("(k p) n -> p k n", p=P)[:, :, ds(n0, n)]


def set_up(c):
    nc, ins = c.nc, c.ins
    rows = []

    def vectors(name, ap, half=None):
        rows.append((name, ap, half))

    def flat(name):
        a = ins[name]
        letters = " ".join("abcdef"[:len(a.shape)])
        f = a if len(a.shape) == 1 else a.rearrange(f"{letters} -> ({letters})")
        return f.rearrange("(n p) -> n p", p=P)

    for name in ("c", "b_ada", "norm_mix", "norm_ffn", "gdn_conv", "gdn_out_norm", "norm_mix_pre_2",
                 "norm_mix_post_2", "norm_ffn_pre_2", "norm_ffn_post_2", "conv_w_2", "conv_b_2",
                 "conv_ln_g_2", "conv_ln_b_2", "pool_scale_2", "ffn_conv_w_2", "ffn_conv_b_2"):
        vectors(name, flat(name))
    for name in ("dsw_q_norm", "dsw_k_norm"):
        vectors(name, (ins[name], ins[name]))
    for layer in range(DEPTH):
        pos = ins["nsa_cmp_pos_2"]
        vectors(f"cmp_pos{layer}", (pos[layer, 0, :, :], pos[layer, 1, :, :]))
    loads, at = [], 0
    for name, ap, _ in rows:
        c.places[name] = at
        parts = [(ap, 0, P)] if not isinstance(ap, tuple) else [(ap[0], 0, 64), (ap[1], 64, 64)]
        n = parts[0][0].shape[0]
        for part, c0, w in parts:
            done = 0
            while done < n:
                r = at + done
                k = min(n - done, P - r % P)
                loads.append((r // P, r % P, k, c0, w, part[done:done + k, :]))
                done += k
        at += n
    assert 7 * P < at <= 8 * P
    early = [x for x in loads if x[0] < 7]
    late = [x for x in loads if x[0] == 7]

    w_ada, ADA, STEPS = ins["w_ada"], 6, 6 * D // 512
    assert STEPS % ADA == 0
    with c.stage(x_rows=[P, TT, D], vec_rows=[P, 8, P], cond=[P, KT], tiles=[P, ADA, KT, 512],
                 scaled=[P, 2, 2, 512]) as (block, sems, x_rows, vec_rows, cond, tiles, scaled):
        x_loaded, consts_loaded, vecs_loaded, cleared, turned, copied, cond_ready, done, mod_ready, added, summed = sems[:11]
        loaded = sems[11:11 + ADA]

        @block.gpsimd
        def _(pool):
            nc.gpsimd.memset(vec_rows[:, 7, :], 0.0).then_inc(cleared, 1)
            nc.gpsimd.memset(c.eps[:, :], EPS).then_inc(cleared, 1)
            pool.wait_ge(cleared, 2)

        @block.sync
        def _(sp):
            sp.dma_start(c.ident[:, :], c.const("ident")).then_inc(consts_loaded, 16)
            sp.dma_start(c.ones[:, :], c.const("ones")).then_inc(consts_loaded, 16)
            sp.dma_start(c.halves[:, :], c.const("halves")).then_inc(consts_loaded, 16)
            sp.dma_start(x_rows[:, :, :], ins["x"][0, :, :].rearrange("(t p) d -> p t d", p=P)).then_inc(x_loaded, 16)
            for tile, r, k, c0, w, src in early:
                sp.dma_start(vec_rows[r:r + k, tile, c0:c0 + w], src).then_inc(vecs_loaded, 16)
            sp.wait_ge(cleared, 1)
            for tile, r, k, c0, w, src in late:
                sp.dma_start(vec_rows[r:r + k, tile, c0:c0 + w], src).then_inc(vecs_loaded, 16)

        @block.tensor
        def _(pe):
            pe.wait_ge(consts_loaded, 48)
            pe.wait_ge(x_loaded, 16)
            for k in range(KT):
                for t in range(TT):
                    last = nc.tensor.transpose(c.ps[:, k, t * P:(t + 1) * P],
                                               x_rows[:, t, k * P:(k + 1) * P], c.ident[:, :])
                last.then_inc(turned, 1)
            pe.wait_ge(vecs_loaded, 16 * len(loads))
            for b in range(2):
                pe.wait_ge(copied, b + 1)
                for t in range(4):
                    last = nc.tensor.transpose(c.ps[:, b, t * P:(t + 1) * P], vec_rows[:, 4 * b + t, :], c.ident[:, :])
                last.then_inc(turned, 1)
            pe.wait_ge(cond_ready, 1)
            with pe.Fori(0, DEPTH * STEPS // 2) as i:
                for s in range(2):
                    pe.wait_ge(done, i * 2 + (s + 1 + ADA))
                    for t in range(4):
                        for part in range(2):
                            last = nc.tensor.matmul(c.ps[:, 0, ds(i * 8 + (4 * s + t), 1)],
                                                    scaled[:, s, part, t * P:(t + 1) * P], c.ones[:, 0:1],
                                                    start=(part == 0), stop=(part == 1))
                    last.then_inc(summed, 1)

        @block.scalar
        def _(act):
            def load(layer, i):
                for s in range(ADA):
                    act.wait_ge(done, i * ADA + (layer * STEPS + s + 1))
                    act.dma_start(tiles[:, s, :, :], columns(w_ada[layer, :, :], i * (512 * ADA) + 512 * s, 512)).then_inc(loaded[s], 16)

            load(0, 0)
            act.wait_ge(copied, KT + 2)
            cc = c.column("c")
            nc.scalar.activation(cond[:, :], c.vec[:, cc:cc + KT], ACT.Silu).then_inc(cond_ready, 1)
            for i in range(1, STEPS // ADA):
                load(0, i)
            for layer in range(1, DEPTH):
                with act.Fori(0, STEPS // ADA) as i:
                    load(layer, i)

        @block.vector
        def _(dve):
            dve.sem_inc(done, ADA)
            dve.sem_inc(summed, 2)
            for k in range(KT):
                dve.wait_ge(turned, k + 1)
                nc.vector.tensor_copy(c.x[:, k, :], c.ps[:, k, :]).then_inc(copied, 1)
            for b in range(2):
                dve.wait_ge(turned, KT + b + 1)
                nc.vector.tensor_copy(c.vec[:, b * 512:(b + 1) * 512], c.ps[:, b, :]).then_inc(copied, 1)
            dve.wait_ge(copied, KT + 2)
            dve.wait_ge(cond_ready, 1)
            with dve.Fori(0, DEPTH * STEPS // ADA) as i:
                for s in range(ADA):
                    n = i * ADA + s
                    dve.wait_ge(loaded[s], i * 16 + 16)
                    dve.wait_ge(summed, n + 1)
                    for k in range(KT):
                        to = scaled[:, s % 2, k % 2, :]
                        if k < 2:
                            ins = nc.vector.tensor_scalar(to, tiles[:, s, k, :], cond[:, k:k + 1], None, ALU.mult)
                        else:
                            dve.wait_ge(added, n * (KT - 1) + (k - 1))
                            ins = nc.vector.scalar_tensor_tensor(to, tiles[:, s, k, :], cond[:, k:k + 1], to, ALU.mult, ALU.add)
                        ins.then_inc(added if k < KT - 1 else done, 1)
            dve.wait_ge(summed, DEPTH * STEPS + 2)
            at = c.column("b_ada")
            nc.vector.tensor_tensor(c.mod[:, :], c.ps[:, 0, 0:DEPTH * 48], c.vec[:, at:at + DEPTH * 48],
                                    ALU.add).then_inc(mod_ready, 1)
            dve.wait_ge(mod_ready, 1)
            for layer in range(DEPTH):
                for j, (name, part) in enumerate((("norm_mix", 1), ("norm_ffn", 4))):
                    g = c.column(name, layer * KT)
                    m = layer * 48 + part * KT
                    o = (layer * 2 + j) * KT
                    nc.vector.scalar_tensor_tensor(c.gains[:, o:o + KT], c.mod[:, m:m + KT], 1.0,
                                                   c.vec[:, g:g + KT], ALU.add, ALU.mult)


def modulation(c, layer, part):
    return layer * 48 + part * KT


class Norm:

    def __init__(self, c, sems, root, gain, shift=None, bank=0):
        self.c, self.root, self.gain, self.shift, self.bank = c, root, gain, shift, bank
        self.squared, self.rooted, self.inverted, self.scaled, self.ready, self.summed = sems

    def scalar(self, act):
        c, nc = self.c, self.c.nc
        for k in range(KT):
            nc.scalar.activation(c.h[:, k, :], c.x[:, k, :], ACT.Square).then_inc(self.squared, 1)
        act.wait_ge(self.summed, 1)
        nc.scalar.activation(self.root[:, :], c.ps[:, self.bank, :], ACT.Sqrt, bias=c.eps[:, :], scale=1.0 / D).then_inc(self.rooted, 1)
        if self.shift is not None:
            for k in range(KT):
                act.wait_ge(self.scaled, k + 1)
                nc.scalar.activation(c.h[:, k, :], c.h[:, k, :], ACT.Identity, bias=self.shift(k)).then_inc(self.ready, 1)

    def tensor(self, pe):
        c, nc = self.c, self.c.nc
        for k in range(KT):
            pe.wait_ge(self.squared, k + 1)
            last = nc.tensor.matmul(c.ps[:, self.bank, :], c.ones[:, :], c.h[:, k, :], start=(k == 0), stop=(k == KT - 1))
        last.then_inc(self.summed, 1)

    def vector(self, dve):
        c, nc = self.c, self.c.nc
        dve.wait_ge(self.rooted, 1)
        nc.vector.reciprocal(self.root[:, :], self.root[:, :]).then_inc(self.inverted, 1)
        dve.wait_ge(self.inverted, 1)
        for k in range(KT):
            nc.vector.scalar_tensor_tensor(c.h[:, k, :], c.x[:, k, :], self.gain(k), self.root[:, :], ALU.mult, ALU.mult
                                           ).then_inc(self.ready if self.shift is None else self.scaled, 1)


def modulated(c, layer, half):
    gain, shift = (layer * 2 + half) * KT, modulation(c, layer, 3 * half)
    return lambda k: c.gains[:, gain + k:gain + k + 1], lambda k: c.mod[:, shift + k:shift + k + 1]


class ProjectOut:

    def __init__(self, c, load, kt, moving, loaded, done, freed, **before):
        self.c, self.load, self.kt, self.moving = c, load, kt, moving
        self.loaded, self.done, self.freed, self.before = loaded, done, freed, before
        self.first = before.get("first", 0)

    def sync(self, sp):
        stream_weights(sp, self.c, KT, lambda n, slot: [
            (slot[:, 0:self.kt * P].rearrange("p (k n) -> p k n", k=self.kt), self.load(n))],
            self.loaded, self.done, self.first)

    def tensor(self, pe):
        multiply_steps(pe, self.c, KT, 1, self.loaded, self.done, self.freed, 1, self.kt,
                       lambda slot, t, k: slot[:, k * P:(k + 1) * P], self.moving, **self.before)

    def vector(self, dve, finish):
        with dve.Fori(0, KT // 2) as i:
            for s in range(2):
                dve.wait_ge(self.done, i * 2 + (self.first + s + 3))
                finish(i * 2 + s, self.c.ps[:, 4 * s, :]).then_inc(self.freed, 1)


def project_out(c, w, kt, moving, finish):
    with c.stage() as (block, sems):
        out = ProjectOut(c, lambda n: columns(w, n * P, P), kt, moving, sems[0:2], sems[2], sems[3])

        @block.sync
        def _(sp):
            out.sync(sp)

        @block.tensor
        def _(pe):
            out.tensor(pe)

        @block.vector
        def _(dve):
            dve.sem_inc(out.freed, 2)
            out.vector(dve, finish)


def add_gated(c, layer, part):
    g = modulation(c, layer, part)
    return lambda n, psum: c.nc.vector.scalar_tensor_tensor(
        c.x[:, ds(n, 1), :], psum, c.mod[:, ds(n + g, 1)], c.x[:, ds(n, 1), :], ALU.mult, ALU.add)


def swiglu(c, layer):
    nc = c.nc
    w_in, w_out = c.ins["w_ffn_in"][layer, :, :], c.ins["w_ffn_out"][layer, :, :]
    with c.nc.sbuf_tensor(f"ffn_hidden{layer}", [P, FT, S], F32) as hidden:
        with c.stage(gate=[P, 2, S], root=[P, S]) as (block, sems, gate, root):
            loaded, done, freed, gated = sems[0:2], sems[2], sems[3], sems[4]
            norm = Norm(c, sems[5:11], root, *modulated(c, layer, 1))
            out = ProjectOut(c, lambda n: columns(w_out, n * P, P), FT, lambda k: hidden[:, k, :], loaded, done, freed,
                             ready=freed, ready_from=2, first=FT, landed=32 * FT // 2)

            @block.sync
            def _(sp):
                def loads(n, slot):
                    v = slot[:, 0:2 * KT * P].rearrange("p (g k n) -> p g k n", g=2, k=KT)
                    return [(v[:, g, :, :], columns(w_in, n * P + g * F1, P)) for g in range(2)]
                stream_weights(sp, c, FT, loads, loaded, done)
                out.sync(sp)

            @block.tensor
            def _(pe):
                norm.tensor(pe)
                multiply_steps(pe, c, FT, 2, loaded, done, freed, 2, KT,
                               lambda slot, t, k: slot[:, (t * KT + k) * P:(t * KT + k + 1) * P],
                               lambda k: c.h[:, k, :], norm.ready)
                out.tensor(pe)

            @block.scalar
            def _(act):
                norm.scalar(act)
                with act.Fori(0, FT // 2) as i:
                    for s in range(2):
                        act.wait_ge(done, i * 2 + s + 3)
                        act.wait_ge(freed, i * 2 + s + 1)
                        nc.scalar.activation(gate[:, s, :], c.ps[:, 4 * s, :], ACT.Silu).then_inc(gated, 1)

            @block.vector
            def _(dve):
                dve.sem_inc(freed, 2)
                norm.vector(dve)
                with dve.Fori(0, FT // 2) as i:
                    for s in range(2):
                        dve.wait_ge(gated, i * 2 + s + 1)
                        nc.vector.tensor_tensor(hidden[:, ds(i * 2 + s, 1), :], c.ps[:, 4 * s + 1, :],
                                                gate[:, s, :], ALU.mult).then_inc(freed, 1)
                out.vector(dve, add_gated(c, layer, 5))


def write_out(c):
    nc = c.nc
    with c.stage(x_rows=[P, TT, D]) as (block, sems, x_rows):
        turned, copied, stored = sems[:3]

        @block.tensor
        def _(pe):
            for b in range(8):
                t, half = b // 2, b % 2
                for j in range(4):
                    last = nc.tensor.transpose(c.ps[:, b, j * P:(j + 1) * P],
                                               c.x[:, half * 4 + j, t * P:(t + 1) * P], c.ident[:, :])
                last.then_inc(turned, 1)

        @block.vector
        def _(dve):
            for b in range(8):
                dve.wait_ge(turned, b + 1)
                nc.vector.tensor_copy(x_rows[:, b // 2, (b % 2) * 512:(b % 2 + 1) * 512], c.ps[:, b, :]).then_inc(copied, 1)

        @block.sync
        def _(sp):
            for t in range(TT):
                sp.wait_ge(copied, 2 * t + 2)
                sp.dma_start(c.out[0, t * P:(t + 1) * P, :], x_rows[:, t, :]).then_inc(stored, 16)
            sp.wait_ge(stored, 16 * TT)


def gdn_rows(c, layer, decay_rows, decay_cols):
    nc, w = c.nc, c.ins["gdn_w_in"][0, :, :]
    G, E, B = range(3)
    with c.stage(w_ab=[P, KT, 2 * GH], stacked=[P, S], work=[GH, 4, S], resets=[GH, S],
                 scalars=[GH, 4], root=[P, S]) as (block, sems, w_ab, stacked, work, resets, scalars, root):
        (loaded, projected, cleared, rows_stacked, turned, act_link, dve_link, rate_ready, exp_ready,
         log_ready, scanned, e_ready, sum_ready, beta_ready, be_ready, rest_ready) = sems[:16]
        norm = Norm(c, sems[16:22], root, *modulated(c, layer, 0), bank=3)

        @block.sync
        def _(sp):
            sp.dma_start(w_ab[:, :, :], columns(w, GCH + GHK, 2 * GH)).then_inc(loaded, 16)
            sp.dma_start(resets[:, :], c.const("resets", GH)).then_inc(loaded, 16)
            sp.dma_start(scalars[:, 0:1], c.ins["gdn_a_log"].rearrange("a h -> h a")).then_inc(loaded, 16)
            sp.dma_start(scalars[:, 1:2], c.ins["gdn_dt_bias"].rearrange("a h -> h a")).then_inc(loaded, 16)

        @block.gpsimd
        def _(pool):
            nc.gpsimd.memset(stacked[:, :], 0.0).then_inc(cleared, 1)

        @block.tensor
        def _(pe):
            norm.tensor(pe)
            pe.wait_ge(loaded, 64)
            for part in range(2):
                for k in range(KT):
                    pe.wait_ge(norm.ready, k + 1)
                    last = nc.tensor.matmul(c.ps[0:GH, part, :], w_ab[:, k, part * GH:(part + 1) * GH], c.h[:, k, :],
                                            start=(k == 0), stop=(k == KT - 1))
                last.then_inc(projected, 1)
            pe.wait_ge(rows_stacked, 4)
            for t in range(TT):
                last = nc.tensor.transpose(c.ps[:, 2, t * P:(t + 1) * P], stacked[:, t * P:(t + 1) * P], c.ident[:, :])
            last.then_inc(turned, 1)

        @block.scalar
        def _(act):
            link = Links(act, act_link)
            norm.scalar(act)
            act.wait_ge(loaded, 64)
            link.do(nc.scalar.activation(scalars[:, 2:3], scalars[:, 0:1], ACT.Exp))
            nc.scalar.activation(scalars[:, 3:4], scalars[:, 2:3], ACT.Copy, scale=-1.0).then_inc(rate_ready, 1)
            act.wait_ge(sum_ready, 1)
            link.do(nc.scalar.activation(work[:, 1, :], work[:, 0, :], ACT.Abs))
            link.do(nc.scalar.activation(work[:, 1, :], work[:, 1, :], ACT.Exp, scale=-1.0))
            nc.scalar.activation(work[:, 1, :], work[:, 1, :], ACT.Ln, bias=1.0).then_inc(log_ready, 1)
            act.wait_ge(scanned, 1)
            nc.scalar.activation(decay_rows[:, E, :], decay_rows[:, G, :], ACT.Exp).then_inc(e_ready, 1)
            act.wait_ge(rest_ready, 1)
            act.wait_ge(cleared, 1)
            nc.scalar.activation(stacked[96:96 + GH, :], work[:, 3, :], ACT.Exp).then_inc(rows_stacked, 1)
            act.wait_ge(projected, 2)
            nc.scalar.activation(decay_rows[:, B, :], c.ps[0:GH, 1, :], ACT.Sigmoid).then_inc(beta_ready, 1)
            act.wait_ge(beta_ready, 1)
            nc.scalar.activation(stacked[32:32 + GH, :], decay_rows[:, B, :], ACT.Copy).then_inc(rows_stacked, 1)
            act.wait_ge(be_ready, 1)
            nc.scalar.activation(stacked[64:64 + GH, :], work[:, 2, :], ACT.Copy).then_inc(rows_stacked, 1)
            nc.scalar.activation(stacked[0:GH, :], decay_rows[:, G, :], ACT.Copy).then_inc(rows_stacked, 1)

        @block.vector
        def _(dve):
            link = Links(dve, dve_link)
            norm.vector(dve)
            dve.wait_ge(loaded, 64)
            dve.wait_ge(projected, 1)
            nc.vector.tensor_scalar(work[:, 0, :], c.ps[0:GH, 0, :], scalars[:, 1:2], None, ALU.add).then_inc(sum_ready, 1)
            dve.wait_ge(log_ready, 1)
            link.do(nc.vector.scalar_tensor_tensor(work[:, 0, :], work[:, 0, :], 0.0, work[:, 1, :], ALU.max, ALU.add))
            dve.wait_ge(rate_ready, 1)
            link.do(nc.vector.tensor_scalar(work[:, 0, :], work[:, 0, :], scalars[:, 3:4], None, ALU.mult))
            nc.vector.tensor_tensor_scan(decay_rows[:, G, :], resets[:, :], work[:, 0, :], 0.0,
                                         ALU.mult, ALU.add).then_inc(scanned, 1)
            dve.wait_ge(scanned, 1)
            g = decay_rows[:, G, :].rearrange("h (n t) -> h n t", t=GC)
            nc.vector.tensor_tensor(work[:, 3, :].rearrange("h (n t) -> h n t", t=GC),
                                    g[:, :, GC - 1:GC].to_broadcast([GH, NCH, GC]), g, ALU.subtract).then_inc(rest_ready, 1)
            dve.wait_ge(e_ready, 1)
            dve.wait_ge(beta_ready, 1)
            nc.vector.tensor_tensor(work[:, 2, :], decay_rows[:, B, :], decay_rows[:, E, :], ALU.mult).then_inc(be_ready, 1)
            dve.wait_ge(turned, 1)
            nc.vector.tensor_copy(decay_cols[:, :, :].rearrange("p t (q h) -> p t q h", h=GH),
                                  c.ps[:, 2, :].rearrange("p (t q n) -> p t q n", t=TT, q=4)[:, :, :, 0:GH])


def gdn_heads(c, st, decay_rows, decay_cols):
    nc, w = c.nc, c.ins["gdn_w_in"][0, :, :]
    G, E, B = range(3)
    with c.stage(two_qkv=[P, 2, 3, S], root=[P, 2, S], picks=[GH, 2, P], hot=[GH, GH], chunkmask=[P, P]) as (
            block, sems, two_qkv, root, picks, hot, chunkmask):
        square = root
        decay = root[:, 0, :].rearrange("p (t n) -> p t n", t=TT)
        kb = root[:, 1, :]
        (load0, load1, consts, projected, freed, filtered, convolved, silued, z_ready, squared, summed, rooted, normed,
         picked, spread, kb_ready, exponent, decayed, products, k_turned, v_turned, q_decayed, dve_link,
         ends_ready) = sems[:24]
        loaded = (load0, load1)
        TILES = 4
        LINKS = 3 * (GCONV - 2) + 2 + 1

        @block.sync
        def _(sp):
            sp.dma_start(hot[:, :], c.const("hot8", GH)).then_inc(consts, 16)
            sp.dma_start(chunkmask[:, :], c.const("chunkmask")).then_inc(consts, 16)
            with sp.Fori(0, GH // 2) as i:
                for s in range(2):
                    n = i * 2 + s
                    tiles = c.slots[s][:, :].rearrange("p (g k n) -> p g k n", g=TILES, k=KT)
                    sp.wait_ge(projected, n * TILES + TILES)
                    for t in range(TILES):
                        sp.dma_start(tiles[:, t, :, :], columns(w, n * P + t * GHK, P)).then_inc(loaded[s], 16)

        @block.tensor
        def _(pe):
            pe.sem_inc(projected, 2 * TILES)
            pe.wait_ge(consts, 32)

            def project(s, t):
                for k in range(KT):
                    last = nc.tensor.matmul(c.ps[:, t, :], c.slots[s][:, (t * KT + k) * P:(t * KT + k + 1) * P],
                                            c.h[:, k, :], start=(k == 0), stop=(k == KT - 1))
                last.then_inc(projected, 1)

            def head(n, s, next_rounds):
                qkv = two_qkv[:, s, :, :]
                if next_rounds is not None:
                    pe.wait_ge(loaded[1 - s], next_rounds * (16 * TILES))
                    pe.wait_ge(convolved, n * 3 + 1)
                    project(1 - s, 0)
                pe.wait_ge(freed, n + 1)
                pe.wait_ge(squared, n * 2 + 2)
                for t in range(2):
                    last = nc.tensor.matmul(c.ps[:, 4 + t, :], c.ones[:, :], square[:, t, :], start=True, stop=True)
                last.then_inc(summed, 1)
                if next_rounds is not None:
                    pe.wait_ge(convolved, n * 3 + 2)
                    project(1 - s, 1)
                pe.wait_ge(picked, n + 1)
                pe.wait_ge(rooted, n * 2 + 1)
                for r, bank in ((G, 6), (E, 7), (B, 4)):
                    last = nc.tensor.matmul(c.ps[:, bank, :], picks[:, s, :], decay_rows[:, r, :], start=True, stop=True)
                last.then_inc(spread, 1)
                if next_rounds is not None:
                    pe.wait_ge(convolved, n * 3 + 3)
                    project(1 - s, 2)
                pe.wait_ge(normed, n * 2 + 2)
                for t in range(TT):
                    last = nc.tensor.transpose(c.ps[:, 5, t * P:(t + 1) * P], qkv[:, 1, t * P:(t + 1) * P], c.ident[:, :])
                last.then_inc(k_turned, 1)
                pe.wait_ge(silued, n * 3 + 3)
                pe.wait_ge(exponent, n + 1)
                for t in range(TT):
                    last = nc.tensor.transpose(c.ps[:, 6, t * P:(t + 1) * P], qkv[:, 2, t * P:(t + 1) * P], c.ident[:, :])
                last.then_inc(v_turned, 1)
                if next_rounds is not None:
                    pe.wait_ge(z_ready, n + 1)
                    project(1 - s, 3)
                pe.wait_ge(kb_ready, n + 1)
                pe.wait_ge(q_decayed, n + 1)
                for t in range(TT):
                    at = slice(t * P, (t + 1) * P)
                    nc.tensor.matmul(c.ps[:, 7, at], qkv[:, 1, at], qkv[:, 0, at], start=True, stop=True)
                for t in range(TT):
                    at = slice(t * P, (t + 1) * P)
                    last = nc.tensor.matmul(c.ps[:, 4, at], qkv[:, 1, at], kb[:, at], start=True, stop=True)
                last.then_inc(products, 1)

            pe.wait_ge(loaded[0], 16 * TILES)
            for t in range(TILES):
                project(0, t)
            with pe.Fori(0, GH // 2 - 1) as i:
                head(i * 2, 0, i + 1)
                head(i * 2 + 1, 1, i + 2)
            head(GH - 2, 0, GH // 2)
            head(GH - 1, 1, None)

        @block.scalar
        def _(act):
            cw = c.column("gdn_conv")
            act.wait_ge(consts, 32)
            with act.Fori(0, GH // 2) as i:
                for s in range(2):
                    n = i * 2 + s
                    qkv = two_qkv[:, s, :, :]
                    for t in range(3):
                        act.wait_ge(projected, n * TILES + (2 * TILES + t + 1))
                        if t == 0:
                            act.wait_ge(freed, n + 1)
                        nc.scalar.activation(qkv[:, t, :], c.ps[:, t, :], ACT.Copy,
                                             scale=c.vec[:, ds(n + (cw + 3 * 24 + t * GH), 1)]).then_inc(filtered, 1)
                    nc.scalar.activation(picks[:, s, :], c.ones[0:GH, :], ACT.Copy, scale=hot[:, ds(n, 1)]).then_inc(picked, 1)
                    act.wait_ge(projected, n * TILES + 3 * TILES)
                    nc.scalar.activation(st["z"][:, ds(n, 1), :], c.ps[:, 3, :], ACT.Silu).then_inc(z_ready, 1)
                    for t in range(3):
                        act.wait_ge(convolved, n * 3 + t + 1)
                        nc.scalar.activation(qkv[:, t, :], qkv[:, t, :], ACT.Silu).then_inc(silued, 1)
                    for t in range(2):
                        act.wait_ge(silued, n * 3 + t + 1)
                        nc.scalar.activation(square[:, t, :], qkv[:, t, :], ACT.Square).then_inc(squared, 1)
                    act.wait_ge(summed, n + 1)
                    for t in range(2):
                        nc.scalar.activation(root[:, t, :], c.ps[:, 4 + t, :], ACT.Sqrt, bias=c.eps[:, :]).then_inc(rooted, 1)
                    act.wait_ge(spread, n + 1)
                    nc.scalar.activation(st["ends"][:, ds(n, 1), :], c.ps[:, 7, GC - 1:S:GC], ACT.Copy).then_inc(ends_ready, 1)
                    act.wait_ge(exponent, n + 1)
                    nc.scalar.activation(decay, decay, ACT.Exp).then_inc(decayed, 1)

        @block.vector
        def _(dve):
            cw = c.column("gdn_conv")
            dve.sem_inc(freed, 1)
            dve.wait_ge(consts, 32)
            with dve.Fori(0, GH // 2) as i:
                for s in range(2):
                    n = i * 2 + s
                    qkv = two_qkv[:, s, :, :]
                    link = Links(dve, dve_link, n * LINKS)
                    for t in range(3):
                        dve.wait_ge(filtered, n * 3 + t + 1)
                        for back in range(1, GCONV):
                            ins = nc.vector.scalar_tensor_tensor(
                                qkv[:, t, back:S], c.ps[:, t, 0:S - back],
                                c.vec[:, ds(n + (cw + (GCONV - 1 - back) * 24 + t * GH), 1)], qkv[:, t, back:S],
                                ALU.mult, ALU.add)
                            if back < GCONV - 1:
                                link.do(ins)
                            else:
                                ins.then_inc(convolved, 1)
                    for t in range(2):
                        dve.wait_ge(rooted, n * 2 + t + 1)
                        link.do(nc.vector.reciprocal(root[:, t, :], root[:, t, :]))
                        nc.vector.scalar_tensor_tensor(qkv[:, t, :], qkv[:, t, :], (GDK ** -0.5, 1.0)[t], root[:, t, :],
                                                       ALU.mult, ALU.mult).then_inc(normed, 1)
                    dve.wait_ge(spread, n + 1)
                    dve.wait_ge(normed, n * 2 + 2)
                    nc.vector.tensor_tensor(kb, qkv[:, 1, :], c.ps[:, 4, :], ALU.mult).then_inc(kb_ready, 1)
                    for t in range(TT):
                        last = nc.vector.tensor_scalar(decay[:, t, :], c.ps[:, 6, t * P:(t + 1) * P],
                                                       decay_cols[:, t, ds(n, 1)], 0.0, ALU.subtract, ALU.min)
                    last.then_inc(exponent, 1)
                    dve.wait_ge(ends_ready, n + 1)
                    nc.vector.tensor_tensor(st["qd"][:, ds(n, 1), :], qkv[:, 0, :], c.ps[:, 7, :], ALU.mult).then_inc(q_decayed, 1)
                    dve.wait_ge(k_turned, n + 1)
                    for t in range(TT):
                        at = slice(t * P, (t + 1) * P)
                        nc.vector.tensor_scalar(st["kbg"][:, ds(n, 1), at], c.ps[:, 5, at], decay_cols[:, t, ds(n + 2 * GH, 1)], None, ALU.mult)
                        nc.vector.tensor_scalar(st["kd"][:, ds(n, 1), at], c.ps[:, 5, at], decay_cols[:, t, ds(n + 3 * GH, 1)], None, ALU.mult)
                    dve.wait_ge(v_turned, n + 1)
                    for t in range(TT):
                        at = slice(t * P, (t + 1) * P)
                        nc.vector.tensor_scalar(st["vb"][:, ds(n, 1), at], c.ps[:, 6, at], decay_cols[:, t, ds(n + 1 * GH, 1)], None, ALU.mult)
                    dve.wait_ge(decayed, n + 1)
                    link.do(nc.vector.tensor_tensor(decay, decay,
                                                    chunkmask[:, :].unsqueeze(1).to_broadcast([P, TT, P]), ALU.mult))
                    dve.wait_ge(products, n + 1)
                    flat = decay.rearrange("p t n -> p (t n)")
                    nc.vector.tensor_tensor(st["qk"][:, ds(n, 1), :], c.ps[:, 7, :], flat, ALU.mult)
                    nc.vector.tensor_tensor(st["lt"][:, ds(n, 1), :], c.ps[:, 4, :], flat, ALU.mult).then_inc(freed, 1)
                    assert link.n == LINKS


def gdn_inverse(c, st, tt, uu):
    nc = c.nc
    with c.stage(levels=[P, LEVELS, P], masked=[P, 2, S], inner=[P, 2, S]) as (block, sems, levels, masked, inner):
        consts, mask_ready, started, x_done, x_copied, y_done, z_done, t_ready, u_ready, mask_begun = sems[:10]

        @block.sync
        def _(sp):
            sp.dma_start(levels[:, :, :], c.const("levels").rearrange("p (l n) -> p l n", l=LEVELS)).then_inc(consts, 16)

        @block.gpsimd
        def _(pool):
            pool.wait_ge(consts, 16)
            with pool.Fori(0, LEVELS) as lv:
                for h in range(GH):
                    pool.wait_ge(x_done, lv * GH + h + 1)
                    pool.sem_inc(mask_begun, 1)
                    nc.gpsimd.tensor_tensor(masked[:, h % 2, :].rearrange("p (t n) -> p t n", t=TT),
                                            st["lt"][:, h, :].rearrange("p (t n) -> p t n", t=TT),
                                            levels[:, ds(lv, 1), :].to_broadcast([P, TT, P]), ALU.mult).then_inc(mask_ready, 1)

        @block.tensor
        def _(pe):
            pe.sem_inc(x_done, 2)
            pe.wait_ge(started, 2 * GH)

            def inner_product(lv, h):
                pe.wait_ge(mask_ready, lv * GH + h + 1)
                pe.wait_ge(t_ready, lv * GH + h + 1)
                pe.wait_ge(x_copied, lv * GH + h + 1)
                for t in range(TT):
                    at = slice(t * P, (t + 1) * P)
                    last = nc.tensor.matmul(c.ps[:, h % 2, at], masked[:, h % 2, at], tt[:, h, at], start=True, stop=True)
                last.then_inc(x_done, 1)

            def outer_products(lv, h):
                pe.wait_ge(x_copied, lv * GH + h + 3)
                pe.wait_ge(u_ready, lv * GH + h - 1 + GH)
                for t in range(TT):
                    at = slice(t * P, (t + 1) * P)
                    last = nc.tensor.matmul(c.ps[:, 2 + h % 2, at], uu[:, h, at], inner[:, h % 2, at], start=True, stop=True)
                last.then_inc(y_done, 1)
                for t in range(TT):
                    at = slice(t * P, (t + 1) * P)
                    last = nc.tensor.matmul(c.ps[:, 4 + h % 2, at], inner[:, h % 2, at], uu[:, h, at], start=True, stop=True)
                last.then_inc(z_done, 1)

            with pe.Fori(0, LEVELS) as lv:
                for h in range(GH + 1):
                    if h < GH:
                        inner_product(lv, h)
                    if h >= 1:
                        outer_products(lv, h - 1)

        @block.scalar
        def _(act):
            act.sem_inc(x_copied, 2)
            for h in range(GH):
                nc.scalar.activation(uu[:, h, :].rearrange("p (t n) -> p t n", t=TT),
                                     c.ident[:, :].unsqueeze(1).to_broadcast([P, TT, P]), ACT.Copy).then_inc(started, 1)
            with act.Fori(0, LEVELS) as lv:
                for h in range(GH):
                    act.wait_ge(x_done, lv * GH + h + 3)
                    act.wait_ge(z_done, lv * GH + h + 1)
                    nc.scalar.activation(inner[:, h % 2, :], c.ps[:, h % 2, :], ACT.Copy).then_inc(x_copied, 1)

        @block.vector
        def _(dve):
            dve.sem_inc(t_ready, GH)
            dve.sem_inc(u_ready, GH)
            dve.sem_inc(z_done, 2)
            for h in range(GH):
                nc.vector.tensor_copy(tt[:, h, :].rearrange("p (t n) -> p t n", t=TT),
                                      c.ident[:, :].unsqueeze(1).to_broadcast([P, TT, P])).then_inc(started, 1)
            dve.wait_ge(started, 2 * GH)
            with dve.Fori(0, LEVELS) as lv:
                for h in range(GH):
                    dve.wait_ge(y_done, lv * GH + h + 1)
                    nc.vector.tensor_tensor(tt[:, h, :], tt[:, h, :], c.ps[:, 2 + h % 2, :], ALU.subtract).then_inc(t_ready, 1)
                    dve.wait_ge(z_done, lv * GH + h + 3)
                    nc.vector.tensor_tensor(uu[:, h, :], uu[:, h, :], c.ps[:, 4 + h % 2, :], ALU.subtract).then_inc(u_ready, 1)


def gdn_scan(c, st, uu, o):
    nc = c.nc
    nw = st["lt"]
    with c.stage(state=[P, GH, P], v_new=[P, GH, P]) as (block, sems, state, v_new):
        w_done, w_copied, v_done, v_copied, o_done, o_copied, s_done, s_decayed, s_ready, cleared = sems[:10]

        @block.gpsimd
        def _(pool):
            nc.gpsimd.memset(state[:, :, :], 0.0).then_inc(s_ready, 1)

        @block.tensor
        def _(pe):
            for h in range(GH):
                if h >= 2:
                    pe.wait_ge(w_copied, h - 1)
                for t in range(TT):
                    at = slice(t * P, (t + 1) * P)
                    last = nc.tensor.matmul(c.ps[:, h % 2, at], st["kbg"][:, h, at], uu[:, h, at], start=True, stop=True)
                last.then_inc(w_done, 1)
            pe.wait_ge(w_copied, GH)
            for n in range(NCH):
                b, pair = 64 * (n % 2), n // 2
                rows, at = slice(b, b + 64), slice(n * GC, (n + 1) * GC)
                pr = slice(pair * P, (pair + 1) * P)
                pe.wait_ge(s_ready, 2 * n + 1)
                if n:
                    pe.wait_ge(v_copied, 2 * n)
                for h in range(GH):
                    out = c.ps[rows, 2 + h // 4, (h % 4) * P:(h % 4 + 1) * P]
                    nc.tensor.matmul(out, uu[rows, h, at], st["vb"][rows, h, pr], start=True, stop=False)
                    last = nc.tensor.matmul(out, nw[:, h, at], state[:, h, :], start=False, stop=True)
                    if h % 4 == 3:
                        last.then_inc(v_done, 1)
                if n:
                    pe.wait_ge(o_copied, n)
                pe.wait_ge(v_copied, 2 * n + 2)
                for h in range(GH):
                    out = c.ps[:, 4, h * GC:(h + 1) * GC]
                    nc.tensor.matmul(out, state[:, h, :], st["qd"][:, h, at], start=True, stop=False)
                    last = nc.tensor.matmul(out, v_new[rows, h, :], st["qk"][rows, h, at], start=False, stop=True)
                last.then_inc(o_done, 1)
                for h in range(GH):
                    last = nc.tensor.matmul(c.ps[:, 6 + h // 4, (h % 4) * P:(h % 4 + 1) * P], st["kd"][rows, h, pr],
                                            v_new[rows, h, :], start=True, stop=True)
                    if h % 4 == 3:
                        last.then_inc(s_done, 1)

        @block.scalar
        def _(act):
            for h in range(GH):
                act.wait_ge(w_done, h + 1)
                nc.scalar.activation(nw[:, h, :], c.ps[:, h % 2, :], ACT.Copy, scale=-1.0).then_inc(w_copied, 1)
            for n in range(NCH):
                b = 64 * (n % 2)
                rows, at = slice(b, b + 64), slice(n * GC, (n + 1) * GC)
                if n >= 2:
                    act.wait_ge(s_done, 2 * n - 2)
                for half in range(2):
                    act.wait_ge(v_done, 2 * n + half + 1)
                    nc.scalar.activation(v_new[rows, 4 * half:4 * half + 4, :],
                                         c.ps[rows, 2 + half, :].rearrange("p (h d) -> p h d", h=4), ACT.Copy).then_inc(v_copied, 1)
                act.wait_ge(o_done, n + 1)
                nc.scalar.activation(o[:, :, at], c.ps[:, 4, :].rearrange("p (h t) -> p h t", h=GH), ACT.Copy).then_inc(o_copied, 1)

        @block.vector
        def _(dve):
            dve.wait_ge(s_ready, 1)
            for n in range(NCH):
                dve.wait_ge(o_done, n + 1)
                for half in range(2):
                    hs = slice(4 * half, 4 * half + 4)
                    ends = st["ends"][:, hs, n:n + 1].to_broadcast([P, 4, P])
                    if n:
                        dve.wait_ge(s_ready, 2 * n + half)
                    nc.vector.tensor_tensor(state[:, hs, :], state[:, hs, :], ends, ALU.mult).then_inc(s_decayed, 1)
                for half in range(2):
                    hs = slice(4 * half, 4 * half + 4)
                    dve.wait_ge(s_decayed, 2 * n + half + 1)
                    dve.wait_ge(s_done, 2 * n + half + 1)
                    nc.vector.tensor_tensor(state[:, hs, :], state[:, hs, :],
                                            c.ps[:, 6 + half, :].rearrange("p (h d) -> p h d", h=4), ALU.add).then_inc(s_ready, 1)


def gdn_out(c, layer, st, o):
    nc = c.nc
    with c.stage(square=[P, 2, S], root=[P, 2, S]) as (block, sems, square, root):
        squared, summed, rooted, inverted, normed, gated = sems[:6]
        out = ProjectOut(c, lambda n: columns(c.ins["gdn_w_out"][0, :, :], n * P, P), GH, lambda k: o[:, k, :],
                         sems[6:8], sems[8], sems[9], ready=gated)

        @block.sync
        def _(sp):
            out.sync(sp)

        def root_of(act, h):
            act.wait_ge(summed, h + 1)
            if h >= 2:
                act.wait_ge(normed, h - 1)
            nc.scalar.activation(root[:, h % 2, :], c.ps[:, 2 + h % 2, :], ACT.Sqrt, bias=c.eps[:, :], scale=1.0 / P).then_inc(rooted, 1)

        @block.scalar
        def _(act):
            for h in range(GH):
                if h >= 2:
                    act.wait_ge(summed, h - 1)
                nc.scalar.activation(square[:, h % 2, :], o[:, h, :], ACT.Square).then_inc(squared, 1)
                if h >= 1:
                    root_of(act, h - 1)
            root_of(act, GH - 1)

        @block.tensor
        def _(pe):
            for h in range(GH):
                pe.wait_ge(squared, h + 1)
                if h >= 2:
                    pe.wait_ge(rooted, h - 1)
                nc.tensor.matmul(c.ps[:, 2 + h % 2, :], c.ones[:, :], square[:, h % 2, :], start=True, stop=True).then_inc(summed, 1)
            out.tensor(pe)

        @block.vector
        def _(dve):
            gain = c.column("gdn_out_norm")
            dve.sem_inc(out.freed, 2)
            for h in range(GH):
                dve.wait_ge(rooted, h + 1)
                nc.vector.reciprocal(root[:, h % 2, :], root[:, h % 2, :]).then_inc(inverted, 1)
                dve.wait_ge(inverted, h + 1)
                nc.vector.scalar_tensor_tensor(o[:, h, :], o[:, h, :], c.vec[:, gain:gain + 1], root[:, h % 2, :],
                                               ALU.mult, ALU.mult).then_inc(normed, 1)
            out.vector(dve, add_gated(c, layer, 2))

        @block.gpsimd
        def _(pool):
            for h in range(GH):
                pool.wait_ge(normed, h + 1)
                nc.gpsimd.tensor_tensor(o[:, h, :], o[:, h, :], st["z"][:, h, :], ALU.mult).then_inc(gated, 1)
            pool.wait_ge(gated, GH)


def gated_deltanet(c, layer):
    nc = c.nc
    with ExitStack() as ctx:
        sb = lambda name, shape: ctx.enter_context(nc.sbuf_tensor(name, shape, F32))
        st = {"z": sb("silu_z", [P, GH, S]), "qd": sb("q_decayed", [P, GH, S]), "qk": sb("qk_decayed", [P, GH, S]),
              "lt": sb("l_transposed", [P, GH, S]), "kbg": sb("keys_beta_decay", [P, GH, S]),
              "kd": sb("keys_to_end", [P, GH, S]), "vb": sb("values_beta", [P, GH, S]),
              "ends": sb("decay_of_chunks", [P, GH, NCH])}
        with nc.sbuf_tensor("decay_rows", [GH, 3, S], F32) as rows, nc.sbuf_tensor("decay_cols", [P, TT, 4 * GH], F32) as cols:
            gdn_rows(c, layer, rows, cols)
            gdn_heads(c, st, rows, cols)
        uu = c.h
        gdn_inverse(c, st, c.slots[0][:, :].rearrange("p (h n) -> p h n", h=GH), uu)
        o = st["qd"]
        gdn_scan(c, st, uu, o)
        gdn_out(c, layer, st, o)


def window_biases(c, layer, scratch, biases):
    nc = c.nc
    planes = ((0, 0), (1, 1), (2, 2), (3, 0))
    with c.stage(table=[BUCKETS + 1, WG * WH], hot=[BUCKETS + 1, 4, 256], rows=[WH, 4, 256],
                 classmask=[P, P], flip=[P, P], root=[P, S]) as (block, sems, table, hot, rows, classmask, flip, root):
        loaded, cleared, done, copied, stored, spread, flipped, turned = sems[:8]
        norm = Norm(c, sems[8:14], root, *modulated(c, layer, 0), bank=4)
        falling = c.slots[0][:, :].rearrange("p (h j n) -> p h j n", h=WH, j=4)

        @block.gpsimd
        def _(pool):
            nc.gpsimd.memset(table[BUCKETS:BUCKETS + 1, :], NEG).then_inc(cleared, 1)

        @block.sync
        def _(sp):
            sp.dma_start(table[0:BUCKETS, :], c.ins["rel_bias"]).then_inc(loaded, 16)
            sp.dma_start(hot[:, :, :], c.const("buckets", BUCKETS + 1).rearrange("b (g n) -> b g n", g=4)).then_inc(loaded, 16)
            sp.dma_start(classmask[:, :], c.const("classmask")).then_inc(loaded, 16)
            sp.dma_start(flip[:, :], c.const("flip")).then_inc(loaded, 16)
            sp.wait_ge(copied, 4)
            sp.dma_start(scratch.rearrange("g h n -> h g n"), rows[:, :, :]).then_inc(stored, 16)
            sp.wait_ge(stored, 16)
            for tile, plane in enumerate((3, 0, 1, 2)):
                src = bass.AP(tensor=scratch.tensor, offset=plane * WH * 256, ap=[[1, P], [256, WH], [1, P]])
                sp.dma_start(falling[:, :, tile, :], src).then_inc(spread, 16)

        @block.tensor
        def _(pe):
            pe.wait_ge(loaded, 64)
            pe.wait_ge(cleared, 1)
            for plane, g in planes:
                nc.tensor.matmul(c.ps[0:WH, plane, 0:256], table[:, g * WH:(g + 1) * WH], hot[:, plane, :],
                                 start=True, stop=True).then_inc(done, 1)
            norm.tensor(pe)
            pe.wait_ge(spread, 64)
            pe.wait_ge(norm.rooted, 1)
            for h in range(WH):
                if h < 4:
                    pe.wait_ge(copied, h + 1)
                nc.tensor.matmul(c.ps[:, h, :], flip[:, :], falling[:, h, :, :].rearrange("p j n -> p (j n)"),
                                 start=True, stop=True).then_inc(flipped, 1)

        @block.scalar
        def _(act):
            norm.scalar(act)

        @block.vector
        def _(dve):
            for plane, _ in planes:
                dve.wait_ge(done, plane + 1)
                nc.vector.tensor_copy(rows[:, plane, :], c.ps[0:WH, plane, 0:256]).then_inc(copied, 1)
            norm.vector(dve)
            for h in range(WH):
                dve.wait_ge(flipped, h + 1)
                last = nc.vector.tensor_copy(biases[:, h, :, :], c.ps[:, h, :].rearrange("p (j n) -> p j n", j=4))
            last.then_inc(turned, 1)
            dve.wait_ge(turned, 1)
            dve.wait_ge(loaded, 64)
            nc.vector.tensor_tensor(biases[:, :, 3, :], biases[:, :, 3, :],
                                    classmask[:, :].unsqueeze(1).to_broadcast([P, WH, P]), ALU.add)


def by_class(ap, dilation):
    return ap.rearrange("p (r i) -> p i r", r=dilation)


def by_token(ap, dilation):
    return ap.rearrange("p (i r) -> p i r", r=dilation)


def window_attention(c, biases, o_groups, neg_max, sums):
    nc, w = c.nc, c.ins["dsw_w_in"][0, :, :]
    NP, NU = WH // 2, 8
    PAIRS = WG * NP
    with c.stage(square=[P, 2, S], root=[P, 2, S], q=[P, S], k=[P, S], v=[P, S],
                 v_rows=[P, TT, P], probs=[P, 2, 2 * P], probs_t=[P, 2, 2, P], inverse=[P, 2], eps64=[P, 1]) as (
            block, sems, square, root, q, k, v, v_rows, probs, probs_t, inverse, eps64):
        (w0, w1, projected, v_projected, squared, v_copied, summed, rooted, inverted, normed, v_turned,
         v_ready, scored, biased, maxed, exped, inverse_ready, weighed, turned, turned_copied, attended, o_copied,
         cleared) = sems[:23]
        w_loaded = (w0, w1)

        def units(g):
            return [(a, b, b - (g == 0 and b > 0), 1 + (g == 0 and b > 0)) for a in range(2) for b in range(TT)]

        def pairs(engine, body):
            for g in range(WG):
                with engine.Fori(0, NP // 2) as i:
                    for s in range(2):
                        body(g, i * 2 + s, s)

        @block.gpsimd
        def _(pool):
            nc.gpsimd.memset(eps64[:, :], 64 * EPS).then_inc(cleared, 1)
            pool.wait_ge(cleared, 1)

        @block.sync
        def _(sp):
            def load(g, n, s):
                m = n + NP * g
                sp.wait_ge(v_projected, m + 1)
                for part in range(3):
                    sp.dma_start(c.slots[s][:, part * D:(part + 1) * D].rearrange("p (k n) -> p k n", k=KT),
                                 columns(w, n * P + (part * WG + g) * WHG, P)).then_inc(w_loaded[s], 16)
            pairs(sp, load)

        @block.tensor
        def _(pe):
            pe.sem_inc(v_projected, 2)
            pe.sem_inc(v_turned, 1)
            pe.sem_inc(turned, 2)
            pe.sem_inc(attended, 2)

            def project(s, part, ks):
                for kk in ks:
                    last = nc.tensor.matmul(c.ps[:, part, :], c.slots[s][:, (part * KT + kk) * P:(part * KT + kk + 1) * P],
                                            c.h[:, kk, :], start=(kk == 0), stop=(kk == KT - 1))
                return last

            def pair(g, n, s, follow):
                m = n + NP * g
                pe.wait_ge(squared, m * 2 + 2)
                for part in range(2):
                    nc.tensor.matmul(c.ps[:, 3 + part, :], c.halves[:, :], square[:, part, :],
                                     start=True, stop=True).then_inc(summed, 1)
                project(s, 2, range(KT)).then_inc(v_projected, 1)
                pe.wait_ge(v_copied, m + 1)
                pe.wait_ge(o_copied, m + 1)
                for t in range(TT):
                    last = nc.tensor.transpose(c.ps[:, 5, t * P:(t + 1) * P], v[:, t * P:(t + 1) * P], c.ident[:, :])
                last.then_inc(v_turned, 1)
                pe.wait_ge(normed, m * 2 + 2)
                us = units(g)
                for t in range(NU + 2):
                    if t < NU:
                        a, b, kb, nk = us[t]
                        h = slice(64 * a, 64 * a + 64)
                        pe.wait_ge(exped, m * NU + t + 1)
                        nc.tensor.matmul(c.ps[:, 6 + t % 2, 0:nk * P], q[h, b * P:(b + 1) * P],
                                         k[h, kb * P:(kb + nk) * P], start=True, stop=True).then_inc(scored, 1)
                    if follow and t < NU:
                        if t == 0:
                            follow(pe)
                        for j in range(2 * t, 2 * t + 2):
                            last = project(1 - s, j // KT, [j % KT])
                        if t == NU - 1:
                            last.then_inc(projected, 1)
                    if 1 <= t <= NU:
                        u = t - 1
                        a, b, kb, nk = us[u]
                        pe.wait_ge(weighed, m * NU + u + 1)
                        pe.wait_ge(turned_copied, m * NU + u + 1)
                        for j in range(nk):
                            last = nc.tensor.transpose(c.ps[:, 3 + u % 2, j * P:(j + 1) * P],
                                                       probs[:, u % 2, j * P:(j + 1) * P], c.ident[:, :])
                        last.then_inc(turned, 1)
                    if t >= 2:
                        u = t - 2
                        a, b, kb, nk = us[u]
                        if u == 0:
                            pe.wait_ge(v_ready, m + 1)
                        pe.wait_ge(turned_copied, m * NU + u + 3)
                        for j in range(nk):
                            last = nc.tensor.matmul(c.ps[64 * a:64 * a + 64, 5, b * P:(b + 1) * P],
                                                    v_rows[:, kb + j, 64 * a:64 * a + 64], probs_t[:, u % 2, j, :],
                                                    start=(j == 0), stop=(j == nk - 1))
                        last.then_inc(attended, 1)

            def weights_landed(s, rounds):
                def wait(engine):
                    engine.wait_ge(w_loaded[s], rounds * 48)
                return wait

            pe.wait_ge(w_loaded[0], 48)
            for part in range(2):
                last = project(0, part, range(KT))
            last.then_inc(projected, 1)
            for g in range(WG - 1):
                with pe.Fori(0, NP // 2) as i:
                    pair(g, i * 2, 0, weights_landed(1, i + (g * 2 + 1)))
                    pair(g, i * 2 + 1, 1, weights_landed(0, i + (g * 2 + 2)))
            g = WG - 1
            pair(g, 0, 0, weights_landed(1, 2 * g + 1))
            pair(g, 1, 1, weights_landed(0, 2 * g + 2))
            pair(g, 2, 0, weights_landed(1, 2 * g + 2))
            pair(g, 3, 1, None)

        @block.scalar
        def _(act):
            act.sem_inc(exped, 2)
            act.sem_inc(turned_copied, 2)
            act.wait_ge(cleared, 1)

            def pair(g, n, s):
                m = n + NP * g
                dil = DILATIONS[g]
                act.wait_ge(projected, m + 1)
                for part in range(2):
                    nc.scalar.activation(square[:, part, :], c.ps[:, part, :], ACT.Square).then_inc(squared, 1)
                act.wait_ge(summed, m * 2 + 1)
                nc.scalar.activation(root[:, 0, :], c.ps[:, 3, :], ACT.Sqrt, bias=eps64[:, :]).then_inc(rooted, 1)
                act.wait_ge(summed, m * 2 + 2)
                nc.scalar.activation(root[:, 1, :], c.ps[:, 4, :], ACT.Sqrt, bias=c.eps[:, :], scale=1.0 / WD).then_inc(rooted, 1)
                act.wait_ge(v_projected, m + 3)
                act.wait_ge(v_turned, m + 1)
                nc.scalar.activation(by_class(v[:, :], dil), by_token(c.ps[:, 2, :], dil), ACT.Copy).then_inc(v_copied, 1)
                act.wait_ge(v_turned, m + 2)
                nc.scalar.activation(v_rows[:, :, :], c.ps[:, 5, :].rearrange("p (t n) -> p t n", t=TT), ACT.Copy).then_inc(v_ready, 1)
                us = units(g)
                for t in range(NU + 1):
                    if t < NU:
                        nk = us[t][3]
                        col = n * NU + (g * NP * NU + t)
                        act.wait_ge(maxed, m * NU + t + 1)
                        act.wait_ge(turned, m * NU + t + 1)
                        nc.scalar.activation(probs[:, t % 2, 0:nk * P], c.ps[:, 6 + t % 2, 0:nk * P], ACT.Exp,
                                             bias=neg_max[:, ds(col, 1)], accum_out=sums[:, ds(col, 1)]).then_inc(exped, 1)
                    if t >= 1:
                        u = t - 1
                        nk = us[u][3]
                        act.wait_ge(turned, m * NU + u + 3)
                        act.wait_ge(attended, m * NU + u + 1)
                        nc.scalar.activation(probs_t[:, u % 2, 0:nk, :],
                                             c.ps[:, 3 + u % 2, 0:nk * P].rearrange("p (j n) -> p j n", j=nk),
                                             ACT.Copy).then_inc(turned_copied, 1)
            pairs(act, pair)

        @block.vector
        def _(dve):
            dve.sem_inc(o_copied, 1)

            def pair(g, n, s):
                m = n + NP * g
                dil = DILATIONS[g]
                for part, (name, to) in enumerate((("dsw_q_norm", q), ("dsw_k_norm", k))):
                    gain = c.column(name)
                    dve.wait_ge(rooted, m * 2 + part + 1)
                    nc.vector.reciprocal(root[:, part, :], root[:, part, :]).then_inc(inverted, 1)
                    dve.wait_ge(inverted, m * 2 + part + 1)
                    nc.vector.scalar_tensor_tensor(by_class(to[:, :], dil), by_token(c.ps[:, part, :], dil),
                                                   c.vec[:, gain:gain + 1], by_token(root[:, part, :], dil),
                                                   ALU.mult, ALU.mult).then_inc(normed, 1)
                us = units(g)
                for t in range(NU + 1):
                    if t < NU:
                        a, b, kb, nk = us[t]
                        col = n * NU + (g * NP * NU + t)
                        dve.wait_ge(scored, m * NU + t + 1)
                        nc.vector.tensor_tensor(c.ps[:, 6 + t % 2, 0:nk * P], c.ps[:, 6 + t % 2, 0:nk * P],
                                                biases[:, ds(n * 2 + a, 1), g + 2 - nk:g + 2, :].rearrange("p h j n -> p (h j n)"),
                                                ALU.add).then_inc(biased, 1)
                        dve.wait_ge(biased, m * NU + t + 1)
                        nc.vector.tensor_reduce(neg_max[:, ds(col, 1)], c.ps[:, 6 + t % 2, 0:nk * P], AX.X, ALU.max,
                                                negate=True).then_inc(maxed, 1)
                    if t >= 1:
                        u = t - 1
                        nk = us[u][3]
                        col = n * NU + (g * NP * NU + u)
                        dve.wait_ge(exped, m * NU + u + 3)
                        nc.vector.reciprocal(inverse[:, u % 2:u % 2 + 1], sums[:, ds(col, 1)]).then_inc(inverse_ready, 1)
                        dve.wait_ge(inverse_ready, m * NU + u + 1)
                        nc.vector.tensor_scalar(probs[:, u % 2, 0:nk * P], probs[:, u % 2, 0:nk * P],
                                                inverse[:, u % 2:u % 2 + 1], None, ALU.mult).then_inc(weighed, 1)
                dve.wait_ge(attended, m * NU + NU + 2)
                nc.vector.tensor_copy(by_token(o_groups[:, ds(n + NP * g, 1), :].rearrange("p a t -> p (a t)"), dil),
                                      by_class(c.ps[:, 5, :], dil)).then_inc(o_copied, 1)

            pairs(dve, pair)


def window_combine(c, o_groups, neg_max, sums, o):
    nc = c.nc
    with c.stage(lse=[P, WG, WH, TT], rows=[WH, WG, S], top=[WH, S], total=[WH, S], pairsel=[WH, 4, P],
                 part=[P, 2, S]) as (block, sems, lse, rows, top, total, pairsel, part):
        consts, log_ready, lse_ready, turned, copied, act_link, dve_link, exped, weighed, spread, scaled = sems[:11]

        @block.sync
        def _(sp):
            sp.dma_start(pairsel[:, :, :], c.const("pairsel", WH).rearrange("h (j n) -> h j n", j=4)).then_inc(consts, 16)

        @block.scalar
        def _(act):
            nc.scalar.activation(lse[:, :, :, :], sums[:, :].rearrange("p (g h b) -> p g h b", g=WG, h=WH), ACT.Ln).then_inc(log_ready, 1)
            for g in range(WG):
                act.wait_ge(lse_ready, 2 + g)
                nc.scalar.activation(rows[:, g, :], rows[:, g, :], ACT.Exp).then_inc(exped, 1)

        @block.tensor
        def _(pe):
            pe.wait_ge(lse_ready, 1)
            for g in range(WG):
                for b in range(TT):
                    last = nc.tensor.transpose(c.ps[0:WH, g, b * P:(b + 1) * P], lse[:, g, :, b], c.ident[:, :])
                last.then_inc(turned, 1)
            pe.wait_ge(consts, 16)
            pe.wait_ge(weighed, WG)
            n = 0
            for pair in range(4):
                for g in range(WG):
                    if n >= 4:
                        pe.wait_ge(scaled, n - 3)
                    nc.tensor.matmul(c.ps[:, 3 + n % 4, :], pairsel[:, pair, :], rows[:, g, :], start=True, stop=True).then_inc(spread, 1)
                    n += 1

        @block.vector
        def _(dve):
            link = Links(dve, dve_link)
            dve.wait_ge(log_ready, 1)
            nc.vector.tensor_tensor(lse[:, :, :, :], lse[:, :, :, :], neg_max[:, :].rearrange("p (g h b) -> p g h b", g=WG, h=WH),
                                    ALU.subtract).then_inc(lse_ready, 1)
            for g in range(WG):
                dve.wait_ge(turned, g + 1)
                ins = nc.vector.tensor_copy(by_token(rows[:, g, :], DILATIONS[g]), by_class(c.ps[0:WH, g, :], DILATIONS[g]))
                link.do(ins)
            link.do(nc.vector.tensor_tensor(top[:, :], rows[:, 0, :], rows[:, 1, :], ALU.max))
            link.do(nc.vector.tensor_tensor(top[:, :], top[:, :], rows[:, 2, :], ALU.max))
            for g in range(WG):
                nc.vector.tensor_tensor(rows[:, g, :], rows[:, g, :], top[:, :], ALU.subtract).then_inc(lse_ready, 1)
            dve.wait_ge(exped, WG)
            link.do(nc.vector.tensor_tensor(total[:, :], rows[:, 0, :], rows[:, 1, :], ALU.add))
            link.do(nc.vector.tensor_tensor(total[:, :], total[:, :], rows[:, 2, :], ALU.add))
            link.do(nc.vector.reciprocal(total[:, :], total[:, :]))
            for g in range(WG):
                nc.vector.tensor_tensor(rows[:, g, :], rows[:, g, :], total[:, :], ALU.mult).then_inc(weighed, 1)
            n = 0
            for pair in range(4):
                for g in range(WG):
                    dve.wait_ge(spread, n + 1)
                    if g == 0:
                        nc.vector.tensor_tensor(o[:, pair, :], o_groups[:, pair, :], c.ps[:, 3 + n % 4, :], ALU.mult).then_inc(scaled, 1)
                    else:
                        nc.vector.tensor_tensor(part[:, g - 1, :], o_groups[:, g * 4 + pair, :], c.ps[:, 3 + n % 4, :], ALU.mult).then_inc(scaled, 1)
                        dve.wait_ge(scaled, n + 1)
                        link.do(nc.vector.tensor_tensor(o[:, pair, :], o[:, pair, :], part[:, g - 1, :], ALU.add))
                    n += 1


def dilated_attention(c, layer):
    nc = c.nc
    scratch = nc.dram_tensor("bias_rows", (4, WH, 256), F32, kind="Internal").ap()
    with ExitStack() as ctx:
        sb = lambda name, shape: ctx.enter_context(nc.sbuf_tensor(name, shape, F32))
        o_groups, o = sb("o_groups", [P, WG * 4, S]), sb("o_windows", [P, 4, S])
        neg_max, sums = sb("neg_max", [P, WG * 32]), sb("sums", [P, WG * 32])
        with nc.sbuf_tensor("biases", [P, WH, 4, P], F32) as biases:
            window_biases(c, layer, scratch, biases)
            window_attention(c, biases, o_groups, neg_max, sums)
        window_combine(c, o_groups, neg_max, sums, o)
        project_out(c, c.ins["dsw_w_out"][0, :, :], WHG // P, lambda k: o[:, k, :], add_gated(c, layer, 2))


def layer_columns(w, layer, n0, n):
    return w.rearrange("l (k p) n -> p l k n", p=P)[:, ds(layer, 1), :, ds(n0, n)].rearrange("p l k n -> p (l k) n")


def layer_gain(c, name, layer):
    at = c.column(name)
    return lambda k: c.vec[:, ds(layer * KT + (at + k), 1)]


Q_A, KV_A, GATE_A, Q_D, KV_D, IN_B, IN_C = 0, 512, 1280, 1304, 1816, 2072, 3096


def nsa_gates(c, layer, gates, w1):
    nc = c.nc
    n = 24
    with c.stage(w=[P, KT, n], rows=[n, S], root=[P, S]) as (block, sems, w, rows, root):
        loaded, done, squashed, turned, w1_loaded = sems[:5]
        norm = Norm(c, sems[5:11], root, layer_gain(c, "norm_mix_pre_2", layer), bank=2)

        @block.sync
        def _(sp):
            sp.dma_start(w[:, :, :], layer_columns(c.ins["w_in_2"], layer, GATE_A, n)).then_inc(loaded, 16)
            for kv in range(2):
                sp.dma_start(w1[64 * kv:64 * kv + 64, :, :],
                             c.ins["nsa_cmp_w1_2"].rearrange("a v (l d) n -> d a v l n", d=64)[:, ds(layer, 1), kv, :, :]
                             .rearrange("d a l n -> d (a l) n")).then_inc(w1_loaded, 16)
            sp.wait_ge(w1_loaded, 32)

        @block.tensor
        def _(pe):
            norm.tensor(pe)
            pe.wait_ge(loaded, 16)
            for k in range(KT):
                pe.wait_ge(norm.ready, k + 1)
                last = nc.tensor.matmul(c.ps[0:n, 0, :], w[:, k, :], c.h[:, k, :], start=(k == 0), stop=(k == KT - 1))
            last.then_inc(done, 1)
            pe.wait_ge(squashed, 1)
            for t in range(TT):
                last = nc.tensor.transpose(c.ps[:, 1, t * n:(t + 1) * n], rows[:, t * P:(t + 1) * P], c.ident[0:n, 0:n])
            last.then_inc(turned, 1)

        @block.scalar
        def _(act):
            norm.scalar(act)
            act.wait_ge(done, 1)
            nc.scalar.activation(rows[:, :], c.ps[0:n, 0, :], ACT.Sigmoid).then_inc(squashed, 1)

        @block.vector
        def _(dve):
            norm.vector(dve)
            dve.wait_ge(turned, 1)
            nc.vector.tensor_copy(gates[:, :, :], c.ps[:, 1, 0:TT * n].rearrange("p (t n) -> p t n", t=TT))


def attend(c, layer, gates, w1, o_nsa, o_swa):
    nc, w_in = c.nc, c.ins["w_in_2"]
    GROUPS = 2
    KS, KW, VSW, KD, VD, QA0, QA1, QD0, QD1 = range(9)
    NT = 9
    STEPS = ((KS, KW), (VSW, KD, VD), (QA0, QA1), (QD0, QD1))
    HALVES = {KS: (KV_A + 256,) * 2, KW: (KV_A + 512,) * 2, VSW: (KV_A + 384, KV_A + 640),
              KD: (KV_D,) * 2, VD: (KV_D + 128,) * 2}
    WIDE = {QA0: Q_A, QA1: Q_A + P, QD0: Q_D, QD1: Q_D + P}
    DMAS = [sum(2 if t in HALVES else 1 for t in step) for step in STEPS]
    BANK_OF = {KS: 1, KW: 2, VSW: 3, KD: 4, VD: 5, QA0: 6, QA1: 7, QD0: 0, QD1: 1}
    ROPED = (KS, KW, KD, QA0, QA1, QD0, QD1)
    CMP, SLC, WIN, SWA = range(4)
    rounds = [(NCMP, [(CMP, pr, qt) for qt in range(TT)]) for pr in range(2)]
    rounds += [(P, [(br, pr, 0) for br in (SLC, WIN) for pr in range(2)])]
    rounds += [(2 * P, [(br, pr, 1) for pr in range(2)]) for br in (SLC, WIN)]
    rounds += [((qt + 1) * P, [(br, pr, qt)]) for qt in (2, 3) for br in (SLC, WIN) for pr in range(2)]
    NSA_ROUNDS = len(rounds)
    rounds += [(min(qt + 1, 2) * P, [(SWA, pr, qt) for pr in range(2)]) for qt in range(TT)]
    NR, NSWA = len(rounds), TT
    RING = 3
    assert all(w * len(tiles) <= S for w, tiles in rounds)

    def first_key_tile(br, qt):
        return max(qt - 1, 0) if br == SWA else 0

    def key_tiles(w):
        return -(-w // P)

    with c.stage(w2=[P, 2, 2, 64], rope=[P, 2, S], swap=[P, P], band=[P, 2 * P],
                 cmpadd=[P, TT * NCMP], cmpmul=[P, TT * NCMP], sinks=[P, DEPTH * 8], minus_sinks=[P, DEPTH * 8],
                 raw=[P, NT, S], turned_q=[P, 7, S], cross=[P, 2, S], blocks=[P, CMP_LEN, GROUPS * NCMP],
                 hidden=[GROUPS * NCMP, 2, CMP_HID], hidden_t=[P, 2, 2, GROUPS * NCMP], k_all=[P, GROUPS * NCMP],
                 v_all=[NCMP, GROUPS, 64], k_cmp=[P, NCMP], v_cmp=[NCMP, 64], v_rows=[P, 2, TT, P],
                 probs=[P, RING, 2, S], probs_t=[P, 2, 2, TT, P], stats=[P, 4, RING, 2, TT]) as (
            block, sems, w2, rope, swap, band, cmpadd, cmpmul, sinks, minus_sinks, raw, roped, cross, blocks,
            hidden, hidden_t, k_all, v_all, k_cmp, v_cmp, v_rows, probs, probs_t, stats):
        (w0_loaded, w1_loaded, consts, projected, copied, swapped, crossed, turned_with_cos, rotated, v_turned, v_ready,
         blocks_ready, hid_done, hid_ready, cmp_done, cmp_ready, scored, masked, topped, maxed, exped, sink_ready,
         summed, inverse_ready, weighed, turned, turned_copied, attended, o_copied, sink_negated, whole_seen,
         kc_loaded, kc_done, kc_copied, hid_turned, hid_back, all_ready) = sems[:37]
        loaded = (w0_loaded, w1_loaded)
        kc_weights = [c.slots[g][:, 3 * D:4 * D].rearrange("p (k n) -> p k n", k=KT) for g in range(GROUPS)]
        CONSTS = 16 * 9
        FIRST = (16 * DMAS[0], 16 * DMAS[1])
        ROUND = (16 * (DMAS[0] + DMAS[2]), 16 * (DMAS[1] + DMAS[3]))

        @block.sync
        def _(sp):
            def load(g, j):
                sp.wait_ge(projected, g * 4 + (j + 1))
                for i, t in enumerate(STEPS[j]):
                    tile = c.slots[j % 2][:, i * D:(i + 1) * D].rearrange("p (k n) -> p k n", k=KT)
                    if t in HALVES:
                        for half, n0 in enumerate(HALVES[t]):
                            sp.dma_start(tile[:, :, 64 * half:64 * half + 64],
                                         layer_columns(w_in, layer, g * 64 + n0, 64)).then_inc(loaded[j % 2], 16)
                    else:
                        sp.dma_start(tile, layer_columns(w_in, layer, g * 256 + WIDE[t], P)).then_inc(loaded[j % 2], 16)

            for g in range(GROUPS):
                for half in range(2):
                    sp.dma_start(kc_weights[g][:, :, 64 * half:64 * half + 64],
                                 layer_columns(w_in, layer, KV_A + 128 * half + 64 * g, 64)).then_inc(kc_loaded, 16)
            with sp.Fori(0, GROUPS) as g:
                for j in range(4):
                    load(g, j)

        @block.gpsimd
        def _(pool):
            pool.wait_ge(consts, CONSTS)
            with pool.Fori(0, GROUPS) as g:
                for i, t in enumerate(ROPED):
                    pool.wait_ge(copied, g * NT + (t + 1))
                    if i == 0:
                        pool.wait_ge(o_copied, g * 4 + 1)
                    nc.gpsimd.tensor_tensor(roped[:, i, :], raw[:, t, :], rope[:, 0, :], ALU.mult).then_inc(turned_with_cos, 1)

        @block.tensor
        def _(pe):
            pe.sem_inc(projected, 2)
            pe.sem_inc(turned, RING)
            pe.sem_inc(attended, 2)
            pe.wait_ge(kc_loaded, 32 * GROUPS)
            for g in range(GROUPS):
                for k in range(KT):
                    last = nc.tensor.matmul(c.ps[:, g, :], kc_weights[g][:, k, :], c.h[:, k, :], start=(k == 0), stop=(k == KT - 1))
                last.then_inc(kc_done, 1)
            pe.wait_ge(consts, CONSTS)
            pe.wait_ge(blocks_ready, 1)
            for kv in range(2):
                r = slice(64 * kv, 64 * kv + 64)
                for pos in range(CMP_LEN):
                    last = nc.tensor.matmul(c.ps[0:GROUPS * NCMP, 6 + kv, 0:CMP_HID], blocks[r, pos, :], w1[r, pos, :],
                                            start=(pos == 0), stop=(pos == CMP_LEN - 1))
            last.then_inc(hid_done, 1)
            pe.wait_ge(hid_ready, 1)
            n = GROUPS * NCMP
            for j in range(4):
                last = nc.tensor.transpose(c.ps[:, 5, j * n:(j + 1) * n], hidden[:, j // 2, (j % 2) * P:(j % 2 + 1) * P], c.ident[0:n, 0:n])
            last.then_inc(hid_turned, 1)
            pe.wait_ge(hid_back, 1)
            for r in range(2):
                for half in range(2):
                    nc.tensor.matmul(c.ps[64 * r:64 * r + 64, 0, 0:n], w2[:, 0, half, :], hidden_t[:, 0, half, :],
                                     start=(half == 0), stop=(half == 1))
            for g in range(GROUPS):
                for half in range(2):
                    last = nc.tensor.matmul(c.ps[0:NCMP, 0, P + 64 * g:P + 64 * g + 64], hidden_t[:, 1, half, g * NCMP:(g + 1) * NCMP],
                                            w2[:, 1, half, :], start=(half == 0), stop=(half == 1))
            last.then_inc(cmp_done, 1)
            with pe.Fori(0, GROUPS) as g:
                for j, step in enumerate(STEPS):
                    pe.wait_ge(loaded[j % 2], g * ROUND[j % 2] + (FIRST[j % 2] if j < 2 else ROUND[j % 2]))
                    if j == 0:
                        pe.wait_ge(o_copied, g * 4 + 1)
                    if j == 3:
                        pe.wait_ge(all_ready, 1)
                        pe.wait_ge(copied, g * NT + (KS + 1))
                    for i, t in enumerate(step):
                        for k in range(KT):
                            last = nc.tensor.matmul(c.ps[:, BANK_OF[t], :], c.slots[j % 2][:, (i * KT + k) * P:(i * KT + k + 1) * P],
                                                    c.h[:, k, :], start=(k == 0), stop=(k == KT - 1))
                    last.then_inc(projected, 1)
                for i, t in enumerate(ROPED):
                    pe.wait_ge(copied, g * NT + (max(t, VSW) + 1))
                    if i >= 2:
                        pe.wait_ge(crossed, g * 7 + (i - 1))
                    nc.tensor.matmul(c.ps[:, 2 + i % 2, :], swap[:, :], raw[:, t, :], start=True, stop=True).then_inc(swapped, 1)
                for i, t in enumerate((VSW, VD)):
                    pe.wait_ge(copied, g * NT + (VD + 1))
                    for tt in range(TT):
                        last = nc.tensor.transpose(c.ps[:, 4 + i, tt * P:(tt + 1) * P], raw[:, t, tt * P:(tt + 1) * P], c.ident[:, :])
                    last.then_inc(v_turned, 1)
                pe.wait_ge(cmp_ready, g + 1)
                pe.wait_ge(rotated, g * 7 + 7)
                pe.wait_ge(v_ready, g * 2 + 2)
                for t in range(NR + 3):
                    if t < NR:
                        w, tiles = rounds[t]
                        pe.wait_ge(turned_copied, g * NR + (t + 1))
                        for a in range(2):
                            h = slice(64 * a, 64 * a + 64)
                            for i, (br, pr, qt) in enumerate(tiles):
                                q_at, k0 = slice(qt * P, (qt + 1) * P), first_key_tile(br, qt) * P
                                if br == CMP:
                                    q, k = raw[h, QA0 + pr, q_at], k_cmp[h, :]
                                else:
                                    q = roped[h, (5 if br == SWA else 3) + pr, q_at]
                                    k = roped[h, {SLC: 0, WIN: 1, SWA: 2}[br], k0:k0 + w]
                                last = nc.tensor.matmul(c.ps[:, 2 * (t % RING) + a, i * w:(i + 1) * w], q, k, start=True, stop=True)
                        last.then_inc(scored, 1)
                    if 2 <= t <= NR + 1:
                        u = t - 2
                        w, tiles = rounds[u]
                        pe.wait_ge(weighed, g * NR + (u + 1))
                        for a in range(2):
                            for i in range(len(tiles)):
                                for j in range(key_tiles(w)):
                                    m, at = min(P, w), (i * key_tiles(w) + j) * P
                                    last = nc.tensor.transpose(c.ps[0:m, 2 * (u % RING) + a, at:at + P],
                                                               probs[:, u % RING, a, i * w + j * P:i * w + j * P + m], c.ident[:, :])
                        last.then_inc(turned, 1)
                    if t >= 3:
                        u = t - 3
                        w, tiles = rounds[u]
                        nk = key_tiles(w)
                        pe.wait_ge(turned_copied, g * NR + (u + 1 + RING))
                        if u == NSA_ROUNDS:
                            pe.wait_ge(o_copied, g * 4 + 3)
                        for a in range(2):
                            h = slice(64 * a, 64 * a + 64)
                            if tiles[0][0] == CMP:
                                last = nc.tensor.matmul(c.ps[h, 6 + tiles[0][1], :], v_cmp[:, :],
                                                        probs_t[0:NCMP, u % 2, a, :, :].rearrange("p t n -> p (t n)"),
                                                        start=True, stop=False)
                                continue
                            for i, (br, pr, qt) in enumerate(tiles):
                                for j in range(nk):
                                    v_at = 64 if br == WIN else 0
                                    last = nc.tensor.matmul(c.ps[h, 6 + pr, qt * P:(qt + 1) * P],
                                                            v_rows[:, br == SWA, first_key_tile(br, qt) + j, v_at:v_at + 64],
                                                            probs_t[:, u % 2, a, i * nk + j, :],
                                                            start=(j == 0 and br == SWA),
                                                            stop=(j == nk - 1 and (br == SWA or (br, qt) == (WIN, TT - 1))))
                        last.then_inc(attended, 1)

        @block.scalar
        def _(act):
            def const(dst, src):
                act.dma_start(dst, src).then_inc(consts, 16)
            const(rope[:, 0, :], c.const("cos"))
            const(rope[:, 1, :], c.const("sin"))
            const(swap[:, :], c.const("swap"))
            const(band[:, :], c.const("band"))
            const(cmpadd[:, :], c.const("cmpadd"))
            const(cmpmul[:, :], c.const("cmpmul"))
            const(sinks[:, :], c.ins["swa_sinks_2"].rearrange("l h -> (l h)").partition_broadcast(P))
            for kv in range(2):
                const(w2[:, kv, :, :],
                      c.ins["nsa_cmp_w2_2"].rearrange("a v (f p) n -> p a v f n", p=P)[:, ds(layer, 1), kv, :, :]
                      .rearrange("p a f n -> p (a f) n"))
            act.sem_inc(turned_copied, RING)
            act.sem_inc(o_copied, 1)
            act.wait_ge(consts, CONSTS)
            nc.scalar.activation(minus_sinks[:, :], sinks[:, :], ACT.Copy, scale=-1.0).then_inc(sink_negated, 1)
            for g in range(GROUPS):
                act.wait_ge(kc_done, g + 1)
                nc.scalar.activation(raw[:, g, :], c.ps[:, g, :], ACT.Copy).then_inc(kc_copied, 1)
            act.wait_ge(hid_done, 1)
            nc.scalar.activation(hidden[:, :, :], c.ps[0:GROUPS * NCMP, 6:8, 0:CMP_HID], ACT.Gelu_apprx_tanh).then_inc(hid_ready, 1)
            act.wait_ge(hid_turned, 1)
            nc.scalar.activation(hidden_t[:, :, :, :].rearrange("p a b n -> p (a b n)"), c.ps[:, 5, 0:4 * GROUPS * NCMP],
                                 ACT.Copy).then_inc(hid_back, 1)
            act.wait_ge(blocks_ready, 1)
            with act.Fori(0, GROUPS) as g:
                for j, step in enumerate(STEPS):
                    act.wait_ge(projected, g * 4 + (j + 3))
                    for t in step:
                        nc.scalar.activation(raw[:, t, :], c.ps[:, BANK_OF[t], :], ACT.Copy,
                                             scale=(0.125 if t >= QA0 else 1.0)).then_inc(copied, 1)
                for i in range(2):
                    act.wait_ge(v_turned, g * 2 + (i + 1))
                    nc.scalar.activation(v_rows[:, i, :, :], c.ps[:, 4 + i, :].rearrange("p (t n) -> p t n", t=TT),
                                         ACT.Copy).then_inc(v_ready, 1)
                def copy_sums(o):
                    for pr in range(2):
                        nc.scalar.activation(o[:, ds(g * 2 + pr, 1), :], c.ps[:, 6 + pr, :], ACT.Copy).then_inc(o_copied, 1)

                for t in range(NR + 2):
                    if t >= 2:
                        u = t - 2
                        w, tiles = rounds[u]
                        rows, n, at = min(w, P), len(tiles) * key_tiles(w), 2 * (u % RING)
                        act.wait_ge(turned, g * NR + (u + 1 + RING))
                        act.wait_ge(attended, g * NR + (u + 1))
                        nc.scalar.activation(probs_t[0:rows, u % 2, :, 0:n, :],
                                             c.ps[0:rows, at:at + 2, 0:n * P].rearrange("p a (j n) -> p a j n", j=n),
                                             ACT.Copy).then_inc(turned_copied, 1)
                    if t == NSA_ROUNDS + 2:
                        act.wait_ge(attended, g * NR + (NSA_ROUNDS + 2))
                        copy_sums(o_nsa)
                    if t < NR:
                        w, tiles = rounds[t]
                        act.wait_ge(maxed, g * NR + (t + 1))
                        act.wait_ge(turned, g * NR + (t + 1))
                        for a in range(2):
                            for i in range(len(tiles)):
                                st = stats[:, :, t % RING, a, i:i + 1]
                                last = nc.scalar.activation(probs[:, t % RING, a, i * w:(i + 1) * w],
                                                            c.ps[:, 2 * (t % RING) + a, i * w:(i + 1) * w], ACT.Exp,
                                                            bias=st[:, 0, :], accum_out=st[:, 1, :])
                        last.then_inc(exped, 1)
                        if t >= NSA_ROUNDS:
                            rest = stats[:, 3, t % RING, :, 0:2]
                            nc.scalar.activation(rest, rest, ACT.Exp).then_inc(sink_ready, 1)
                act.wait_ge(attended, g * NR + (NR + 2))
                copy_sums(o_swa)

        @block.vector
        def _(dve):
            pos_at = c.column("cmp_pos0")
            assert c.column("cmp_pos1") == pos_at + CMP_LEN
            dve.wait_ge(consts, CONSTS)
            dve.wait_ge(sink_negated, 1)
            dve.wait_ge(kc_copied, GROUPS)
            line = raw[:, 0, :]
            strided = bass.AP(tensor=line.tensor, offset=line.offset,
                              ap=[list(line.ap[0]), [1, CMP_LEN], [S, GROUPS], [CMP_STRIDE, NCMP]])
            nc.vector.tensor_tensor(blocks[:, :, :].rearrange("p l (g n) -> p l g n", g=GROUPS), strided,
                                    c.vec[:, ds(layer * CMP_LEN + pos_at, CMP_LEN)].unsqueeze(2).unsqueeze(3)
                                    .to_broadcast([P, CMP_LEN, GROUPS, NCMP]), ALU.add).then_inc(blocks_ready, 1)
            dve.wait_ge(cmp_done, 1)
            nc.vector.tensor_copy(k_all[:, :], c.ps[:, 0, 0:GROUPS * NCMP])
            nc.vector.tensor_copy(v_all[:, :, :].rearrange("p g n -> p (g n)"), c.ps[0:NCMP, 0, P:2 * P]).then_inc(all_ready, 1)
            dve.wait_ge(all_ready, 1)
            with dve.Fori(0, GROUPS) as g:
                dve.wait_ge(o_copied, g * 4 + 1)
                nc.vector.tensor_copy(k_cmp[:, :], k_all[:, ds(g * NCMP, NCMP)])
                nc.vector.tensor_copy(v_cmp[:, :], v_all[:, ds(g, 1), :].rearrange("p a n -> p (a n)")).then_inc(cmp_ready, 1)
                for i in range(7):
                    dve.wait_ge(swapped, g * 7 + (i + 1))
                    if i >= 2:
                        dve.wait_ge(rotated, g * 7 + (i - 1))
                    nc.vector.tensor_tensor(cross[:, i % 2, :], c.ps[:, 2 + i % 2, :], rope[:, 1, :], ALU.mult).then_inc(crossed, 1)
                    dve.wait_ge(crossed, g * 7 + (i + 1))
                    dve.wait_ge(turned_with_cos, g * 7 + (i + 1))
                    nc.vector.tensor_tensor(roped[:, i, :], roped[:, i, :], cross[:, i % 2, :], ALU.add).then_inc(rotated, 1)
                def group_sinks(of):
                    return of[:, ds(layer * 8 + g * 4, 4)].rearrange("p (r a) -> p a r", a=2)

                for t in range(NR + 1):
                    if t < NR:
                        w, tiles = rounds[t]
                        n, br = len(tiles), tiles[0][0]
                        st = stats[:, :, t % RING, :, 0:n]
                        scores = c.ps[:, 2 * (t % RING):2 * (t % RING) + 2, 0:n * w].rearrange("p a (i w) -> p a i w", i=n)
                        if br == CMP:
                            part, mask = scores, cmpadd[:, :].rearrange("p (t w) -> p t w", t=TT).unsqueeze(1)
                        elif br == SWA:
                            part, mask = scores, band[:, 2 * P - w:2 * P].unsqueeze(1).unsqueeze(1)
                        else:
                            part, mask = scores[:, :, :, w - P:w], band[:, P:2 * P].unsqueeze(1).unsqueeze(1)
                        dve.wait_ge(scored, g * NR + (t + 1))
                        nc.vector.tensor_tensor(part, part, mask.to_broadcast(list(part.shape)), ALU.add).then_inc(masked, 1)
                        dve.wait_ge(masked, g * NR + (t + 1))
                        top = nc.vector.tensor_reduce(st[:, 0, :, :], scores, AX.X, ALU.max, negate=True)
                        if br == SWA:
                            top.then_inc(topped, 1)
                            dve.wait_ge(topped, g * (2 * NSWA) + (2 * (t - NSA_ROUNDS) + 1))
                            nc.vector.tensor_tensor(st[:, 0, :, :], st[:, 0, :, :], group_sinks(minus_sinks), ALU.min).then_inc(topped, 1)
                            dve.wait_ge(topped, g * (2 * NSWA) + (2 * (t - NSA_ROUNDS) + 2))
                            top = nc.vector.tensor_tensor(st[:, 3, :, :], st[:, 0, :, :], group_sinks(sinks), ALU.add)
                        top.then_inc(maxed, 1)
                    if t >= 1:
                        u = t - 1
                        w, tiles = rounds[u]
                        n, br = len(tiles), tiles[0][0]
                        st = stats[:, :, u % RING, :, 0:n]
                        dve.wait_ge(exped, g * NR + (u + 1))
                        if br == SWA:
                            dve.wait_ge(sink_ready, g * NSWA + (u - NSA_ROUNDS + 1))
                            nc.vector.tensor_tensor(st[:, 1, :, :], st[:, 1, :, :], st[:, 3, :, :], ALU.add).then_inc(summed, 1)
                            dve.wait_ge(summed, g * NSWA + (u - NSA_ROUNDS + 1))
                        nc.vector.reciprocal(st[:, 2, :, :], st[:, 1, :, :]).then_inc(inverse_ready, 1)
                        dve.wait_ge(inverse_ready, g * NR + (u + 1))
                        for a in range(2):
                            for i, (br, pr, qt) in enumerate(tiles):
                                p, inverse = probs[:, u % RING, a, i * w:(i + 1) * w], st[:, 2, a, i:i + 1]
                                if br == SWA:
                                    ins = nc.vector.tensor_scalar(p, p, inverse, None, ALU.mult)
                                else:
                                    gate = gates[:, qt, ds(g * 4 + (br * 8 + pr * 2 + a), 1)]
                                    ins = nc.vector.tensor_scalar(p, p, inverse, gate, ALU.mult, ALU.mult)
                        if br == CMP:
                            ins.then_inc(whole_seen, 1)
                            dve.wait_ge(whole_seen, g * 2 + (u + 1))
                            p = probs[:, u % RING, :, 0:NCMP]
                            ins = nc.vector.tensor_tensor(p, p, cmpmul[:, 0:NCMP].unsqueeze(1).to_broadcast([P, 2, NCMP]), ALU.mult)
                        ins.then_inc(weighed, 1)


def conv_pool_gates(c, layer, o_conv, o_pool, gates, pooled_in):
    nc, w_in, w_gate = c.nc, c.ins["w_in_2"], c.ins["w_gate_2"]
    CT = BW // P
    PAD, PPAD = CONVW - 1, POOLW[-1] - 1
    STEPS = CT + CT // 2 + 16
    with c.stage(padded=[P, CT, PAD + S], pool_in=[P, CT, PPAD + S], windows=[P, 2, PPAD + S], poolinv=[P, 64],
                 sig=[P, 2, S]) as (block, sems, padded, pool_in, windows, poolinv, sig):
        (load0, load1, consts, done, freed, zeroed, squashed, glued, tapped, pool_copied, pool_link, means_ready,
         pooled) = sems[:13]
        loaded = (load0, load1)

        @block.gpsimd
        def _(pool):
            nc.gpsimd.memset(padded[:, :, 0:PAD], 0.0).then_inc(zeroed, 1)
            nc.gpsimd.memset(pool_in[:, :, 0:PPAD], 0.0).then_inc(zeroed, 1)
            nc.gpsimd.memset(windows[:, :, :], 0.0).then_inc(zeroed, 1)
            pool.wait_ge(zeroed, 3)
            pool.wait_ge(consts, 16)
            pool.wait_ge(pool_copied, CT)
            link = Links(pool, pool_link)
            for j, wide in enumerate(POOLW):
                src, span, turn = pool_in[:, j, :], 1, 0
                while span < wide:
                    link.do(nc.gpsimd.tensor_tensor(windows[:, turn, span:], src[:, span:], src[:, 0:PPAD + S - span], ALU.add))
                    src, span, turn = windows[:, turn, :], span * 2, 1 - turn
                at = src[:, PPAD:]
                out = pooled_in[:, j, :]
                link.do(nc.gpsimd.tensor_tensor(out[:, 0:16], at[:, 0:16], poolinv[:, j * 16:(j + 1) * 16], ALU.mult))
                link.do(nc.gpsimd.tensor_scalar(out[:, 16:], at[:, 16:], 1.0 / wide, 1.0, ALU.mult, ALU.mult))
                link.do(nc.gpsimd.tensor_tensor(out, out, pool_in[:, j, PPAD:], ALU.subtract))
                if j < CT - 1:
                    link.do(nc.gpsimd.memset(windows[:, :, 0:PPAD], 0.0))

        @block.sync
        def _(sp):
            sp.dma_start(poolinv[:, :], c.const("poolinv")).then_inc(consts, 16)

            def tile(s, t):
                return c.slots[s][:, t * D:(t + 1) * D].rearrange("p (k n) -> p k n", k=KT)

            with sp.Fori(0, CT // 2) as i:
                for s in range(2):
                    sp.wait_ge(done, i * 2 + (s + 1))
                    for t in range(2):
                        sp.dma_start(tile(s, t), layer_columns(w_in, layer, i * (2 * P) + (s * P + IN_B + t * BW), P)).then_inc(loaded[s], 16)
            for s in range(2):
                sp.wait_ge(done, CT + s + 1)
                for t in range(2):
                    sp.dma_start(tile(s, t), layer_columns(w_in, layer, IN_C + (2 * s + t) * P, P)).then_inc(loaded[s], 16)
            with sp.Fori(0, 8) as i:
                for s in range(2):
                    sp.wait_ge(done, i * 2 + (s + CT + 2 + 1))
                    for t in range(2):
                        sp.dma_start(tile(s, t), layer_columns(w_gate, layer, i * (4 * P) + (2 * s + t) * P, P)).then_inc(loaded[s], 16)

        @block.tensor
        def _(pe):
            multiply_steps(pe, c, STEPS, 2, loaded, done, freed, 2, KT,
                           lambda slot, t, k: slot[:, (t * KT + k) * P:(t * KT + k + 1) * P], lambda k: c.h[:, k, :])

        @block.scalar
        def _(act):
            act.sem_inc(freed, 2)
            for n in range(CT):
                act.wait_ge(done, n + 3)
                if n >= 2:
                    act.wait_ge(glued, n - 1)
                nc.scalar.activation(sig[:, n % 2, :], c.ps[:, 4 * (n % 2) + 1, :], ACT.Sigmoid).then_inc(squashed, 1)
                act.wait_ge(glued, n + 1)
                act.sem_inc(freed, 1)
            act.wait_ge(zeroed, 3)
            for n in range(2):
                act.wait_ge(done, CT + n + 3)
                for t in range(2):
                    last = nc.scalar.activation(pool_in[:, 2 * n + t, PPAD:], c.ps[:, 4 * n + t, :], ACT.Copy)
                    last.then_inc(pool_copied, 1)
                act.wait_ge(pool_copied, 2 * n + 2)
                act.sem_inc(freed, 1)
            with act.Fori(0, 8) as i:
                for s in range(2):
                    act.wait_ge(done, i * 2 + (s + CT + 2 + 3))
                    for t in range(2):
                        last = nc.scalar.activation(gates[:, ds(i * 4 + (2 * s + t), 1), :], c.ps[:, 4 * s + t, :], ACT.Sigmoid)
                    last.then_inc(freed, 1)

        @block.vector
        def _(dve):
            dve.wait_ge(zeroed, 3)
            for n in range(CT):
                dve.wait_ge(squashed, n + 1)
                nc.vector.tensor_tensor(padded[:, n, PAD:], c.ps[:, 4 * (n % 2), :], sig[:, n % 2, :], ALU.mult).then_inc(glued, 1)
            dve.wait_ge(glued, CT)
            cw, cb = c.column("conv_w_2"), c.column("conv_b_2")
            for t in range(CT):
                nc.vector.tensor_scalar(o_conv[:, t, :], padded[:, t, 0:S], c.vec[:, ds(layer * (CONVW * CT) + (cw + t), 1)],
                                        c.vec[:, ds(layer * CT + (cb + t), 1)], ALU.mult, ALU.add).then_inc(tapped, 1)
            with dve.Fori(1, CONVW) as k:
                for t in range(CT):
                    dve.wait_ge(tapped, k * CT + (t - CT + 1))
                    nc.vector.scalar_tensor_tensor(o_conv[:, t, :], padded[:, t, ds(k, S)],
                                                   c.vec[:, ds(layer * (CONVW * CT) + k * CT + (cw + t), 1)], o_conv[:, t, :],
                                                   ALU.mult, ALU.add).then_inc(tapped, 1)


def conv_norm_pool_mix(c, layer, o_conv, o_pool, pooled_in):
    nc = c.nc
    CT = BW // P
    with c.stage(square=[P, CT, S], root=[P, S], w=[P, CT, P]) as (block, sems, square, root, w):
        loaded, mean_done, centred, squared, var_done, rooted, inverted, normed, mixed, act_link = sems[:10]

        @block.sync
        def _(sp):
            sp.dma_start(w[:, :, :], c.ins["pool_w_2"].rearrange("l g c d -> c l g d")[:, ds(layer, 1), :, :]
                         .rearrange("c l g d -> c (l g) d")).then_inc(loaded, 16)

        @block.tensor
        def _(pe):
            for t in range(CT):
                last = nc.tensor.matmul(c.ps[:, 0, :], c.ones[:, :], o_conv[:, t, :], start=(t == 0), stop=(t == CT - 1))
            last.then_inc(mean_done, 1)
            pe.wait_ge(loaded, 16)
            for t in range(CT):
                nc.tensor.matmul(c.ps[:, 2 + t, :], w[:, t, :], pooled_in[:, t, :], start=True, stop=True).then_inc(mixed, 1)
            for t in range(CT):
                pe.wait_ge(squared, t + 1)
                last = nc.tensor.matmul(c.ps[:, 1, :], c.ones[:, :], square[:, t, :], start=(t == 0), stop=(t == CT - 1))
            last.then_inc(var_done, 1)

        @block.vector
        def _(dve):
            dve.wait_ge(mean_done, 1)
            for t in range(CT):
                nc.vector.scalar_tensor_tensor(o_conv[:, t, :], c.ps[:, 0, :], -1.0 / BW, o_conv[:, t, :],
                                               ALU.mult, ALU.add).then_inc(centred, 1)
            dve.wait_ge(rooted, 1)
            nc.vector.reciprocal(root[:, :], root[:, :]).then_inc(inverted, 1)
            dve.wait_ge(inverted, 1)
            g = c.column("conv_ln_g_2")
            for t in range(CT):
                nc.vector.scalar_tensor_tensor(o_conv[:, t, :], o_conv[:, t, :], c.vec[:, ds(layer * CT + (g + t), 1)], root[:, :],
                                               ALU.mult, ALU.mult).then_inc(normed, 1)

        @block.scalar
        def _(act):
            for t in range(CT):
                act.wait_ge(centred, t + 1)
                nc.scalar.activation(square[:, t, :], o_conv[:, t, :], ACT.Square).then_inc(squared, 1)
            ps_at = c.column("pool_scale_2")
            for t in range(CT):
                act.wait_ge(mixed, t + 1)
                nc.scalar.activation(o_pool[:, t, :], c.ps[:, 2 + t, :], ACT.Copy, scale=c.vec[:, ds(layer * CT + (ps_at + t), 1)])
            act.wait_ge(var_done, 1)
            nc.scalar.activation(root[:, :], c.ps[:, 1, :], ACT.Sqrt, bias=c.eps[:, :], scale=1.0 / BW).then_inc(rooted, 1)
            b = c.column("conv_ln_b_2")
            for t in range(CT):
                act.wait_ge(normed, t + 1)
                nc.scalar.activation(o_conv[:, t, :], o_conv[:, t, :], ACT.Silu, bias=c.vec[:, ds(layer * CT + (b + t), 1)])


def merge_branches(c, layer, branches, gates):
    nc, w = c.nc, c.ins["w_branch_2"]
    NB, CT = 4, BW // P
    with c.stage(part=[P, 3, S]) as (block, sems, part):
        loaded, done, freed, gated, dve_link = sems[0:2], sems[2], sems[3], sems[4], sems[5]
        LINKS = 3

        @block.sync
        def _(sp):
            wv = w.rearrange("l b (k p) n -> p l (b k) n", p=P)
            stream_weights(sp, c, KT, lambda n, slot: [
                (slot[:, 0:NB * CT * P].rearrange("p (j n) -> p j n", n=P),
                 wv[:, ds(layer, 1), :, ds(n * P, P)].rearrange("p l j n -> p (l j) n"))], loaded, done)

        @block.tensor
        def _(pe):
            pe.sem_inc(done, 2)
            with pe.Fori(0, KT // 2) as i:
                for s in range(2):
                    pe.wait_ge(loaded[s], i * 16 + 16)
                    pe.wait_ge(freed, i * 2 + (s + 1))
                    for b in range(NB):
                        for k in range(CT):
                            last = nc.tensor.matmul(c.ps[:, 4 * s + b, :], c.slots[s][:, (b * CT + k) * P:(b * CT + k + 1) * P],
                                                    branches[b][:, k, :], start=(k == 0), stop=(k == CT - 1))
                    last.then_inc(done, 1)

        @block.vector
        def _(dve):
            dve.sem_inc(freed, 2)
            with dve.Fori(0, KT // 2) as i:
                for s in range(2):
                    n = i * 2 + s
                    dve.wait_ge(done, n + 3)
                    for b in range(1, NB):
                        nc.vector.tensor_tensor(part[:, b - 1, :], c.ps[:, 4 * s + b, :], gates[:, ds(n + b * KT, 1), :],
                                                ALU.mult).then_inc(gated, 1)
                    sum_ = gates[:, ds(n, 1), :]
                    nc.vector.tensor_tensor(sum_, c.ps[:, 4 * s, :], sum_, ALU.mult).then_inc(gated, 1)
                    link = Links(dve, dve_link, n * LINKS)
                    dve.wait_ge(gated, n * NB + NB)
                    for b in range(1, NB):
                        link.do(nc.vector.tensor_tensor(sum_, sum_, part[:, b - 1, :], ALU.add))
                    assert link.n == LINKS
                    dve.sem_inc(freed, 1)


class AddNormed:
    POOL = 5

    def __init__(self, c, sems, out, gain, square, total, root):
        self.c, self.out, self.gain, self.square, self.total, self.root = c, out, gain, square, total, root
        self.summed, self.turned, self.rooted, self.inverted, self.scaled, self.added, self.pool_added = sems

    def scalar(self, act):
        c, nc, out = self.c, self.c.nc, self.out
        with act.Fori(0, KT // 2) as i:
            for s in range(2):
                n = i * 2 + s
                act.wait_ge(out.done, n + (out.first + 3))
                nc.scalar.activation(c.h[:, ds(n, 1), :], c.ps[:, 4 * s, :], ACT.Copy)
                act.wait_ge(self.summed, n + 1)
                nc.scalar.activation(self.square[:, s, :], c.ps[:, 4 * s, :], ACT.Square).then_inc(out.freed, 1)
        act.wait_ge(self.turned, 1)
        nc.scalar.activation(self.root[:, :], c.ps[:, 1, :], ACT.Sqrt, bias=c.eps[:, :], scale=1.0 / D).then_inc(self.rooted, 1)

    def tensor(self, pe):
        pe.wait_ge(self.summed, KT + 2)
        self.c.nc.tensor.matmul(self.c.ps[:, 1, :], self.c.ones[:, :], self.total[:, :], start=True, stop=True).then_inc(self.turned, 1)

    def vector(self, dve):
        c, nc, out = self.c, self.c.nc, self.out
        dve.sem_inc(self.summed, 1)
        nc.vector.memset(self.total[:, :], 0.0).then_inc(self.summed, 1)
        with dve.Fori(0, KT // 2) as i:
            for s in range(2):
                n = i * 2 + s
                dve.wait_ge(out.freed, n + (out.first + 3))
                dve.wait_ge(self.summed, n + 2)
                nc.vector.tensor_tensor(self.total[:, :], self.total[:, :], self.square[:, s, :], ALU.add).then_inc(self.summed, 1)
        dve.wait_ge(self.rooted, 1)
        nc.vector.reciprocal(self.root[:, :], self.root[:, :]).then_inc(self.inverted, 1)
        dve.wait_ge(self.inverted, 1)
        for k in range(KT):
            nc.vector.scalar_tensor_tensor(c.h[:, k, :], c.h[:, k, :], self.gain(k), self.root[:, :], ALU.mult, ALU.mult
                                           ).then_inc(self.scaled, 1)
        for k in range(self.POOL, KT):
            dve.wait_ge(self.scaled, k + 1)
            nc.vector.tensor_tensor(c.x[:, k, :], c.x[:, k, :], c.h[:, k, :], ALU.add).then_inc(self.added, 1)

    def gpsimd(self, pool):
        c, nc = self.c, self.c.nc
        for k in range(self.POOL):
            pool.wait_ge(self.scaled, k + 1)
            nc.gpsimd.tensor_tensor(c.x[:, k, :], c.x[:, k, :], c.h[:, k, :], ALU.add).then_inc(self.pool_added, 1)
        pool.wait_ge(self.pool_added, self.POOL)


def conv_ffn(c, layer):
    nc = c.nc
    w_up, w_down = c.ins["ffn_w_up_2"], c.ins["ffn_w_down_2"]
    with c.nc.sbuf_tensor("conv_ffn_hidden", [P, FT, S], F32) as hidden:
        with c.stage(u=[P, 2, 2, S], root=[P, S], square=[P, 2, S], total=[P, S], out_root=[P, S]) as (
                block, sems, u, root, square, total, out_root):
            loaded, done, freed, filtered, convolved, dve_link, gelued = sems[0:2], *sems[2:8]
            norm = Norm(c, sems[8:14], root, layer_gain(c, "norm_ffn_pre_2", layer))
            out = ProjectOut(c, lambda n: layer_columns(w_down, layer, n * P, P), FT, lambda k: hidden[:, k, :], loaded, done,
                             freed, ready=freed, ready_from=2, first=FT, landed=32 * FT // 2)
            add = AddNormed(c, sems[14:21], out, layer_gain(c, "norm_ffn_post_2", layer), square, total, out_root)

            @block.gpsimd
            def _(pool):
                add.gpsimd(pool)
            TAPS, LINKS = 3, 2
            cw, cb = c.column("ffn_conv_w_2"), c.column("ffn_conv_b_2")

            @block.sync
            def _(sp):
                def loads(n, slot):
                    v = slot[:, 0:2 * KT * P].rearrange("p (g k n) -> p g k n", g=2, k=KT)
                    return [(v[:, g, :, :], layer_columns(w_up, layer, n * P + g * F2, P)) for g in range(2)]
                stream_weights(sp, c, FT, loads, loaded, done)
                out.sync(sp)

            @block.tensor
            def _(pe):
                norm.tensor(pe)
                multiply_steps(pe, c, FT, 2, loaded, done, freed, 2, KT,
                               lambda slot, t, k: slot[:, (t * KT + k) * P:(t * KT + k + 1) * P], lambda k: c.h[:, k, :],
                               norm.ready)
                out.tensor(pe)
                add.tensor(pe)

            @block.scalar
            def _(act):
                norm.scalar(act)
                with act.Fori(0, FT // 2) as i:
                    for s in range(2):
                        n = i * 2 + s
                        act.wait_ge(done, n + 3)
                        act.wait_ge(freed, n + 1)
                        for t in range(2):
                            nc.scalar.activation(
                                u[:, s, t, :], c.ps[:, 4 * s + t, :], ACT.Identity,
                                bias=c.vec[:, ds(layer * (2 * FT) + n + (cb + t * FT), 1)],
                                scale=c.vec[:, ds(layer * (TAPS * 2 * FT) + n + (cw + 2 * 2 * FT + t * FT), 1)]).then_inc(filtered, 1)
                        act.wait_ge(convolved, n * 2 + 1)
                        nc.scalar.activation(u[:, s, 0, :], u[:, s, 0, :], ACT.Gelu_apprx_tanh).then_inc(gelued, 1)
                add.scalar(act)

            @block.vector
            def _(dve):
                dve.sem_inc(freed, 2)
                norm.vector(dve)
                with dve.Fori(0, FT // 2) as i:
                    for s in range(2):
                        n = i * 2 + s
                        link = Links(dve, dve_link, n * LINKS)
                        for t in range(2):
                            dve.wait_ge(filtered, n * 2 + (t + 1))
                            for back in (1, 2):
                                ins = nc.vector.scalar_tensor_tensor(
                                    u[:, s, t, back:], c.ps[:, 4 * s + t, 0:S - back],
                                    c.vec[:, ds(layer * (TAPS * 2 * FT) + n + (cw + (2 - back) * 2 * FT + t * FT), 1)],
                                    u[:, s, t, back:], ALU.mult, ALU.add)
                                if back == 1:
                                    link.do(ins)
                                else:
                                    ins.then_inc(convolved, 1)
                        assert link.n == LINKS
                        dve.wait_ge(gelued, n + 1)
                        dve.wait_ge(convolved, n * 2 + 2)
                        nc.vector.tensor_tensor(hidden[:, ds(n, 1), :], u[:, s, 0, :], u[:, s, 1, :], ALU.mult).then_inc(freed, 1)
                add.vector(dve)


def project_layer_out(c, layer, moving):
    with c.stage(square=[P, 2, S], total=[P, S], root=[P, S]) as (block, sems, square, total, root):
        out = ProjectOut(c, lambda n: layer_columns(c.ins["w_o_2"], layer, n * P, P), KT, moving, sems[0:2], sems[2], sems[3])
        add = AddNormed(c, sems[4:11], out, layer_gain(c, "norm_mix_post_2", layer), square, total, root)

        @block.sync
        def _(sp):
            out.sync(sp)

        @block.tensor
        def _(pe):
            out.tensor(pe)
            add.tensor(pe)

        @block.scalar
        def _(act):
            act.sem_inc(out.freed, 2)
            add.scalar(act)

        @block.vector
        def _(dve):
            add.vector(dve)

        @block.gpsimd
        def _(pool):
            add.gpsimd(pool)


def second_block(c):
    nc = c.nc
    before = c.turn
    with nc.Fori(0, DEPTH) as layer:
        with ExitStack() as ctx:
            sb = lambda name, shape: ctx.enter_context(nc.sbuf_tensor(name, shape, F32))
            o_nsa, o_swa = sb("o_nsa", [P, 4, S]), sb("o_swa", [P, 4, S])
            with nc.sbuf_tensor("nsa_gates", [P, TT, 24], F32) as nsa_gate, \
                    nc.sbuf_tensor("compress_w1", [P, CMP_LEN, CMP_HID], F32) as w1:
                nsa_gates(c, layer, nsa_gate, w1)
                attend(c, layer, nsa_gate, w1, o_nsa, o_swa)
            o_conv, o_pool = sb("o_conv", [P, 4, S]), sb("o_pool", [P, 4, S])
            gates = sb("branch_gates", [P, 32, S])
            with nc.sbuf_tensor("pooled", [P, 4, S], F32) as pooled_in:
                conv_pool_gates(c, layer, o_conv, o_pool, gates, pooled_in)
                conv_norm_pool_mix(c, layer, o_conv, o_pool, pooled_in)
            merge_branches(c, layer, (o_nsa, o_conv, o_pool, o_swa), gates)
            project_layer_out(c, layer, lambda k: gates[:, k, :])
        conv_ffn(c, layer)
        if c.turn != before:
            with c.stage():
                pass


def build(nc, ins, out):
    with ExitStack() as ctx:
        c = Core(nc, ctx, ins, out)
        set_up(c)
        for layer, mixer in enumerate((gated_deltanet, dilated_attention)):
            mixer(c, layer)
            swiglu(c, layer)
        second_block(c)
        write_out(c)


def kernel(**inputs):
    import concourse.bacc as bacc
    from concourse.bass_utils import run_bass_kernel_spmd as run

    nc = bacc.Bacc("TRN2", target_bir_lowering=False, num_devices=1)
    arrays = {f"in_{k}": np.ascontiguousarray(v) for k, v in inputs.items()}
    arrays["in_constants"] = packed_constants()
    ins = {k[3:]: nc.dram_tensor(k, a.shape, F32, kind="ExternalInput").ap() for k, a in arrays.items()}
    out = nc.dram_tensor("out_x", (1, S, D), F32, kind="ExternalOutput").ap()
    build(nc, ins, out)
    return run(nc, [arrays], core_ids=[0]).results[0]["out_x"]
```
